# Optimizing a Trainium2 kernel written in Bass

```python
import math
import jax, jax.numpy as jnp
from jax import lax
import numpy as np

D_MODEL = 1024
BATCH = 1
SEQ = 256
DEPTH = 2

N_MIXERS = 2
D_FF = 2816
HG_HEADS = 8
HG_KEY = D_MODEL // HG_HEADS
HG_VAL = D_MODEL // HG_HEADS
HG_CHUNK = 64
FOX_HEADS = 16
FOX_HEAD_DIM = D_MODEL // FOX_HEADS
Q_BLOCK = 128
N_HG_LAYERS = (DEPTH + 1) // 2
N_FOX_LAYERS = DEPTH // 2
EPS = 1e-6
MASK_VALUE = -1e30
MIN_GATE = 1e-30


def rmsnorm(x, g):
    x32 = x.astype(jnp.float32)
    y = x32 * lax.rsqrt(jnp.mean(x32 * x32, axis=-1, keepdims=True) + EPS)
    return (y * g.astype(jnp.float32)).astype(x.dtype)

def swiglu(h, w_in, w_out):
    gate, up = jnp.split(h @ w_in, 2, axis=-1)
    return (jax.nn.silu(gate) * up) @ w_out

def hgrn2_mixer(h, w_in, lb, out_norm_g, w_out):
    B, T, _ = h.shape
    C = HG_CHUNK
    n = T // C
    q, z_f, i, g = jnp.split(h @ w_in, 4, axis=-1)
    z32 = z_f.astype(jnp.float32)
    lb = lb.astype(jnp.float32)
    f = lb + (1.0 - lb) * jax.nn.sigmoid(z32)
    log_f = jnp.log(jnp.maximum(f, MIN_GATE))
    k = (1.0 - lb) * jax.nn.sigmoid(-z32)
    q = jax.nn.silu(q.astype(jnp.float32))
    v = i.astype(jnp.float32)

    def to_chunks(a, d):
        return a.reshape(B, n, C, HG_HEADS, d).transpose(1, 0, 3, 2, 4)

    qc, kc, lfc = to_chunks(q, HG_KEY), to_chunks(k, HG_KEY), to_chunks(log_f, HG_KEY)
    vc = to_chunks(v, HG_VAL)
    causal = jnp.tril(jnp.ones((C, C), dtype=bool))[:, :, None]

    def step(S, inp):
        qb, kb, vb, lb_c = inp
        b = jnp.cumsum(lb_c, axis=2)
        o_inter = jnp.einsum('bhtk,bhkv->bhtv', qb * jnp.exp(b), S)
        diff = b[:, :, :, None, :] - b[:, :, None, :, :]
        decay = jnp.where(causal, jnp.exp(jnp.where(causal, diff, 0.0)), 0.0)
        scores = jnp.einsum('bhtk,bhtsk,bhsk->bhts', qb, decay, kb)
        o_intra = jnp.einsum('bhts,bhsv->bhtv', scores, vb)
        b_last = b[:, :, -1:, :]
        k_dec = kb * jnp.exp(b_last - b)
        S_new = jnp.exp(b_last[:, :, 0, :])[..., None] * S + jnp.einsum('bhsk,bhsv->bhkv', k_dec, vb)
        return S_new, o_inter + o_intra

    S0 = jnp.zeros((B, HG_HEADS, HG_KEY, HG_VAL), jnp.float32)
    _, o = lax.scan(step, S0, (qc, kc, vc, lfc))
    o = o.transpose(1, 0, 3, 2, 4).reshape(B, T, HG_HEADS, HG_VAL)
    o = rmsnorm(o, out_norm_g).reshape(B, T, D_MODEL)
    o = o * jax.nn.silu(g.astype(jnp.float32))
    return o.astype(h.dtype) @ w_out

def fox_mixer(h, w_in, b_f, q_norm_g, k_norm_g, w_out):
    B, T, _ = h.shape
    H, Dh = FOX_HEADS, FOX_HEAD_DIM
    nb = T // Q_BLOCK
    D = D_MODEL
    proj = h @ w_in
    q, k, v, g, z_f = jnp.split(proj, [D, 2 * D, 3 * D, 4 * D], axis=-1)
    q = rmsnorm(q.reshape(B, T, H, Dh), q_norm_g).transpose(0, 2, 1, 3)
    k = rmsnorm(k.reshape(B, T, H, Dh), k_norm_g).transpose(0, 2, 1, 3)
    v = v.reshape(B, T, H, Dh).transpose(0, 2, 1, 3)
    log_f = jax.nn.log_sigmoid(z_f.astype(jnp.float32) + b_f.astype(jnp.float32))
    c = jnp.cumsum(log_f, axis=1).transpose(0, 2, 1)
    qb = q.reshape(B, H, nb, Q_BLOCK, Dh).transpose(2, 0, 1, 3, 4)
    cq = c.reshape(B, H, nb, Q_BLOCK).transpose(2, 0, 1, 3)
    scale = 1.0 / math.sqrt(Dh)
    key_pos = jnp.arange(T)

    def block(args):
        qi, cqi, start = args
        s = jnp.einsum('bhqd,bhkd->bhqk', qi, k).astype(jnp.float32) * scale
        s = s + cqi[..., None] - c[:, :, None, :]
        qpos = start + jnp.arange(Q_BLOCK)
        s = jnp.where(key_pos[None, :] <= qpos[:, None], s, MASK_VALUE)
        p = jax.nn.softmax(s, axis=-1)
        return jnp.einsum('bhqk,bhkd->bhqd', p.astype(v.dtype), v)

    o = lax.map(block, (qb, cq, jnp.arange(nb) * Q_BLOCK))
    o = o.transpose(1, 0, 3, 2, 4).reshape(B, T, D)
    o = o * jax.nn.sigmoid(g)
    return o @ w_out

def first_inputs(seed: int = 0) -> dict:
    key = jax.random.key(seed)
    ks = jax.random.split(key, 16)
    f32 = jnp.float32
    D = D_MODEL

    def w(k, shape, fan_in):
        return jax.random.normal(k, shape, f32) * (fan_in ** -0.5)

    return {
        "x": jax.random.normal(ks[0], (BATCH, SEQ, D), f32),
        "norm_g": 1.0 + 0.05 * jax.random.normal(ks[1], (DEPTH, 3, D), f32),
        "ffn_w_in": w(ks[2], (DEPTH, 2, D, 2 * D_FF), D),
        "ffn_w_out": w(ks[3], (DEPTH, 2, D_FF, D), D_FF),
        "hg_w_in": w(ks[4], (N_HG_LAYERS, D, 4 * D), D),
        "hg_lb_logits": 0.5 * jax.random.normal(ks[5], (N_HG_LAYERS, HG_HEADS * HG_KEY), f32),
        "hg_out_norm_g": 1.0 + 0.05 * jax.random.normal(ks[6], (N_HG_LAYERS, HG_VAL), f32),
        "hg_w_out": w(ks[7], (N_HG_LAYERS, D, D), D),
        "fox_w_in": w(ks[8], (N_FOX_LAYERS, D, 4 * D + FOX_HEADS), D),
        "fox_b_f": 2.0 + 0.5 * jax.random.normal(ks[9], (N_FOX_LAYERS, FOX_HEADS), f32),
        "fox_q_norm_g": 1.0 + 0.05 * jax.random.normal(ks[10], (N_FOX_LAYERS, FOX_HEAD_DIM), f32),
        "fox_k_norm_g": 1.0 + 0.05 * jax.random.normal(ks[11], (N_FOX_LAYERS, FOX_HEAD_DIM), f32),
        "fox_w_out": w(ks[12], (N_FOX_LAYERS, D, D), D),
    }

def first_block(x, norm_g, ffn_w_in, ffn_w_out, hg_w_in, hg_lb_logits, hg_out_norm_g, hg_w_out,
              fox_w_in, fox_b_f, fox_q_norm_g, fox_k_norm_g, fox_w_out):
    p = jax.nn.softmax(hg_lb_logits.astype(jnp.float32), axis=0)
    lbs = jnp.cumsum(p, axis=0) - p[0]
    for layer in range(DEPTH):
        j = layer // N_MIXERS
        x = x + 0.5 * swiglu(rmsnorm(x, norm_g[layer, 0]), ffn_w_in[layer, 0], ffn_w_out[layer, 0])
        hn = rmsnorm(x, norm_g[layer, 1])
        if layer % N_MIXERS == 0:
            x = x + hgrn2_mixer(hn, hg_w_in[j], lbs[j], hg_out_norm_g[j], hg_w_out[j])
        else:
            x = x + fox_mixer(hn, fox_w_in[j], fox_b_f[j], fox_q_norm_g[j], fox_k_norm_g[j], fox_w_out[j])
        x = x + 0.5 * swiglu(rmsnorm(x, norm_g[layer, 2]), ffn_w_in[layer, 1], ffn_w_out[layer, 1])
    return x


N_A_LAYERS = DEPTH // 2
N_B_LAYERS = DEPTH - N_A_LAYERS
CONV_WIDTH = 3
N_HEADS = 16
N_KV_GROUPS = 4
HEADS_PER_GROUP = N_HEADS // N_KV_GROUPS
HEAD_DIM = D_MODEL // N_HEADS
N_BRANCH = 3
CMP_BLOCK = 32
CMP_STRIDE = 16
CMP_HIDDEN = 2 * HEAD_DIM
SLC_BLOCK = 64
N_SELECT = 16
WINDOW = 512
N_BUCKETS = 32
MAX_EXACT = N_BUCKETS // 2
MAX_DISTANCE = 4096
NEG = -1e30
BIG = 1e30


def rmsnorm_2(x, g):
    xf = x.astype(jnp.float32)
    y = xf * lax.rsqrt(jnp.mean(xf * xf, axis=-1, keepdims=True) + EPS)
    return (y * g.astype(jnp.float32)).astype(x.dtype)

def swiglu_ffn(x, w_in, w_out):
    gate, up = jnp.split(x @ w_in, 2, axis=-1)
    return (jax.nn.silu(gate) * up) @ w_out

def rel_bucket(rel):
    n = jnp.maximum(rel, 0)
    nf = jnp.maximum(n, 1).astype(jnp.float32)
    large = MAX_EXACT + (jnp.log(nf / MAX_EXACT) / math.log(MAX_DISTANCE / MAX_EXACT)
                         * (N_BUCKETS - MAX_EXACT)).astype(jnp.int32)
    large = jnp.minimum(large, N_BUCKETS - 1)
    return jnp.where(n < MAX_EXACT, n, large)

def short_conv_mixer(x, w_in, conv_w, w_out):
    b_gate, c_gate, v = jnp.split(x @ w_in, 3, axis=-1)
    u = c_gate * v
    y = lax.conv_general_dilated(u, conv_w[:, None, :], window_strides=(1,),
                                 padding=[(CONV_WIDTH - 1, 0)],
                                 dimension_numbers=('NWC', 'WIO', 'NWC'),
                                 feature_group_count=D_MODEL)
    return (b_gate * y) @ w_out

def compress(raw, pe, w1, w2):
    bsz, s = raw.shape[0], raw.shape[1]
    nc = (s - CMP_BLOCK) // CMP_STRIDE + 1
    idx = jnp.arange(nc)[:, None] * CMP_STRIDE + jnp.arange(CMP_BLOCK)[None, :]
    blk = raw[:, idx] + pe[None, None, :, None, :]
    blk = blk.transpose(0, 3, 1, 2, 4).reshape(bsz, N_KV_GROUPS, nc, CMP_BLOCK * HEAD_DIM)
    return jax.nn.gelu(blk @ w1) @ w2

def shared_kv(h, kv_norm, w_kv, k_norm, pe_k, pe_v, w1_k, w2_k, w1_v, w2_v):
    bsz, s, _ = h.shape
    kv = (rmsnorm_2(h, kv_norm) @ w_kv).reshape(bsz, s, N_BRANCH, 2, N_KV_GROUPS, HEAD_DIM)
    k_c = rmsnorm_2(compress(kv[:, :, 0, 0], pe_k, w1_k, w2_k), k_norm[0])
    v_c = compress(kv[:, :, 0, 1], pe_v, w1_v, w2_v)
    ns = s // SLC_BLOCK
    k_s = rmsnorm_2(kv[:, :, 1, 0], k_norm[1]).transpose(0, 2, 1, 3).reshape(bsz, N_KV_GROUPS, ns, SLC_BLOCK, HEAD_DIM)
    v_s = kv[:, :, 1, 1].transpose(0, 2, 1, 3).reshape(bsz, N_KV_GROUPS, ns, SLC_BLOCK, HEAD_DIM)
    pad = ((0, 0), (0, 0), (WINDOW, 0), (0, 0))
    k_w = jnp.pad(rmsnorm_2(kv[:, :, 2, 0], k_norm[2]).transpose(0, 2, 1, 3), pad)
    v_w = jnp.pad(kv[:, :, 2, 1].transpose(0, 2, 1, 3), pad)
    return k_c, v_c, k_s, v_s, k_w, v_w

def masked_softmax(s, mask):
    return jax.nn.softmax(jnp.where(mask, s.astype(jnp.float32), NEG), axis=-1)

def nsa_mixer(x, w_q, q_norm, w_o, rel_bias, kv):
    k_c, v_c, k_s, v_s, k_w, v_w = kv
    bsz, s, _ = x.shape
    G, HG, dh = N_KV_GROUPS, HEADS_PER_GROUP, HEAD_DIM
    proj = x @ w_q
    q = rmsnorm_2(proj[..., :N_HEADS * dh].reshape(bsz, s, G, HG, dh), q_norm)
    q = q.transpose(0, 2, 3, 1, 4)
    gates = jax.nn.sigmoid(proj[..., N_HEADS * dh:].astype(jnp.float32))
    gates = gates.reshape(bsz, s, G, HG, N_BRANCH).transpose(0, 2, 3, 1, 4).astype(x.dtype)
    nc, ns = k_c.shape[2], k_s.shape[2]
    n_sel = min(N_SELECT, ns)
    scale = HEAD_DIM ** -0.5
    c_start = jnp.arange(nc) * CMP_STRIDE
    c_end = c_start + CMP_BLOCK - 1
    s_start = jnp.arange(ns) * SLC_BLOCK
    overlap = (jnp.clip(jnp.minimum(c_start[:, None] + CMP_BLOCK, s_start[None, :] + SLC_BLOCK)
                        - jnp.maximum(c_start[:, None], s_start[None, :]), 0) / CMP_STRIDE).astype(jnp.float32)
    bias_grp = rel_bias.reshape(N_BUCKETS, G, HG).transpose(1, 0, 2)
    bi = jnp.arange(bsz)[:, None, None, None]
    gi = jnp.arange(G)[None, :, None, None]
    blk_ids = jnp.arange(ns)

    def head_bias(rel):
        return rel_bias[rel_bucket(rel)].reshape(rel.shape + (G, HG)).transpose(2, 3, 0, 1)

    def block(qb):
        q0 = qb * Q_BLOCK
        qblk = lax.dynamic_slice_in_dim(q, q0, Q_BLOCK, axis=3)
        gblk = lax.dynamic_slice_in_dim(gates, q0, Q_BLOCK, axis=3)
        t = q0 + jnp.arange(Q_BLOCK)
        rel_c = t[:, None] - c_end[None, :]
        s_c = jnp.einsum('bghqd,bgnd->bghqn', qblk, k_c) * scale + head_bias(rel_c)
        p_c = masked_softmax(s_c, rel_c >= 0)
        p_c = jnp.where((t >= CMP_BLOCK - 1)[:, None], p_c, 0.0)
        o_c = jnp.einsum('bghqn,bgnd->bghqd', p_c.astype(v_c.dtype), v_c)
        imp = jnp.einsum('bghqn,nj->bgqj', p_c, overlap)
        blk_t = t // SLC_BLOCK
        valid = blk_ids[None, :] <= blk_t[:, None]
        forced = ((blk_ids[None, :] == 0) | (blk_ids[None, :] == blk_t[:, None])
                  | (blk_ids[None, :] == blk_t[:, None] - 1))
        score = jnp.where(valid, jnp.where(forced, BIG, imp), NEG)
        _, idx = lax.top_k(score, n_sel)
        k_sel = k_s[bi, gi, idx].reshape(bsz, G, Q_BLOCK, n_sel * SLC_BLOCK, dh)
        v_sel = v_s[bi, gi, idx].reshape(bsz, G, Q_BLOCK, n_sel * SLC_BLOCK, dh)
        pos = (idx[..., None] * SLC_BLOCK + jnp.arange(SLC_BLOCK)).reshape(bsz, G, Q_BLOCK, n_sel * SLC_BLOCK)
        rel_s = t[None, None, :, None] - pos
        bias_s = bias_grp[gi, rel_bucket(rel_s)].transpose(0, 1, 4, 2, 3)
        s_s = jnp.einsum('bghqd,bgqkd->bghqk', qblk, k_sel) * scale + bias_s
        p_s = masked_softmax(s_s, (rel_s >= 0)[:, :, None])
        o_s = jnp.einsum('bghqk,bgqkd->bghqd', p_s.astype(v_sel.dtype), v_sel)
        k_wb = lax.dynamic_slice_in_dim(k_w, q0, Q_BLOCK + WINDOW, axis=2)
        v_wb = lax.dynamic_slice_in_dim(v_w, q0, Q_BLOCK + WINDOW, axis=2)
        s_pos = q0 - WINDOW + jnp.arange(Q_BLOCK + WINDOW)
        rel_w = t[:, None] - s_pos[None, :]
        mask_w = (rel_w >= 0) & (rel_w < WINDOW) & (s_pos >= 0)[None, :]
        s_w = jnp.einsum('bghqd,bgkd->bghqk', qblk, k_wb) * scale + head_bias(rel_w)
        p_w = masked_softmax(s_w, mask_w)
        o_w = jnp.einsum('bghqk,bgkd->bghqd', p_w.astype(v_wb.dtype), v_wb)
        return gblk[..., 0:1] * o_c + gblk[..., 1:2] * o_s + gblk[..., 2:3] * o_w

    out = lax.map(block, jnp.arange(s // Q_BLOCK))
    out = out.transpose(1, 0, 4, 2, 3, 5).reshape(bsz, s, N_HEADS * dh)
    return out @ w_o

def second_inputs(seed: int = 0) -> dict:
    key = jax.random.key(seed)
    ks = jax.random.split(key, 32)

    def w(k, shape, fan_in):
        return jax.random.normal(k, shape, jnp.float32) * (fan_in ** -0.5)

    def gain(k, shape):
        return 1.0 + 0.02 * jax.random.normal(k, shape, jnp.float32)

    q_cols = N_HEADS * HEAD_DIM + N_BRANCH * N_HEADS
    kv_cols = N_BRANCH * 2 * N_KV_GROUPS * HEAD_DIM
    return {
        'x': jax.random.normal(ks[0], (BATCH, SEQ, D_MODEL), jnp.float32),
        'ffn1_norm': gain(ks[1], (DEPTH, D_MODEL)),
        'ffn1_w_in': w(ks[2], (DEPTH, D_MODEL, 2 * D_FF), D_MODEL),
        'ffn1_w_out': w(ks[3], (DEPTH, D_FF, D_MODEL), D_FF),
        'mix_norm': gain(ks[4], (DEPTH, D_MODEL)),
        'ffn2_norm': gain(ks[5], (DEPTH, D_MODEL)),
        'ffn2_w_in': w(ks[6], (DEPTH, D_MODEL, 2 * D_FF), D_MODEL),
        'ffn2_w_out': w(ks[7], (DEPTH, D_FF, D_MODEL), D_FF),
        'conv_w_in': w(ks[8], (N_A_LAYERS, D_MODEL, 3 * D_MODEL), D_MODEL),
        'conv_w': w(ks[9], (N_A_LAYERS, CONV_WIDTH, D_MODEL), CONV_WIDTH),
        'conv_w_out': w(ks[10], (N_A_LAYERS, D_MODEL, D_MODEL), D_MODEL),
        'attn_w_q': w(ks[11], (N_B_LAYERS, D_MODEL, q_cols), D_MODEL),
        'attn_q_norm': gain(ks[12], (N_B_LAYERS, HEAD_DIM)),
        'attn_w_o': w(ks[13], (N_B_LAYERS, N_HEADS * HEAD_DIM, D_MODEL), N_HEADS * HEAD_DIM),
        'kv_norm': gain(ks[14], (D_MODEL,)),
        'w_kv': w(ks[15], (D_MODEL, kv_cols), D_MODEL),
        'k_norm': gain(ks[16], (N_BRANCH, HEAD_DIM)),
        'cmp_pe_k': 0.1 * jax.random.normal(ks[17], (CMP_BLOCK, HEAD_DIM), jnp.float32),
        'cmp_pe_v': 0.1 * jax.random.normal(ks[18], (CMP_BLOCK, HEAD_DIM), jnp.float32),
        'cmp_w1_k': w(ks[19], (CMP_BLOCK * HEAD_DIM, CMP_HIDDEN), CMP_BLOCK * HEAD_DIM),
        'cmp_w2_k': w(ks[20], (CMP_HIDDEN, HEAD_DIM), CMP_HIDDEN),
        'cmp_w1_v': w(ks[21], (CMP_BLOCK * HEAD_DIM, CMP_HIDDEN), CMP_BLOCK * HEAD_DIM),
        'cmp_w2_v': w(ks[22], (CMP_HIDDEN, HEAD_DIM), CMP_HIDDEN),
        'rel_bias': 0.5 * jax.random.normal(ks[23], (N_BUCKETS, N_HEADS), jnp.float32),
    }

def second_block(x, ffn1_norm, ffn1_w_in, ffn1_w_out, mix_norm, ffn2_norm, ffn2_w_in, ffn2_w_out,
              conv_w_in, conv_w, conv_w_out, attn_w_q, attn_q_norm, attn_w_o,
              kv_norm, w_kv, k_norm, cmp_pe_k, cmp_pe_v, cmp_w1_k, cmp_w2_k, cmp_w1_v, cmp_w2_v,
              rel_bias):
    h = x
    kv = None
    for i in range(DEPTH):
        if i == N_A_LAYERS:
            kv = shared_kv(h, kv_norm, w_kv, k_norm, cmp_pe_k, cmp_pe_v,
                           cmp_w1_k, cmp_w2_k, cmp_w1_v, cmp_w2_v)
        h = h + 0.5 * swiglu_ffn(rmsnorm_2(h, ffn1_norm[i]), ffn1_w_in[i], ffn1_w_out[i])
        hn = rmsnorm_2(h, mix_norm[i])
        if i < N_A_LAYERS:
            h = h + short_conv_mixer(hn, conv_w_in[i], conv_w[i], conv_w_out[i])
        else:
            j = i - N_A_LAYERS
            h = h + nsa_mixer(hn, attn_w_q[j], attn_q_norm[j], attn_w_o[j], rel_bias, kv)
        h = h + 0.5 * swiglu_ffn(rmsnorm_2(h, ffn2_norm[i]), ffn2_w_in[i], ffn2_w_out[i])
    return h


def setup_inputs(seed=0):
    out = dict(first_inputs(seed))
    for name, value in second_inputs(seed + 1).items():
        if name != "x":
            out[name + "_2"] = value
    return out


def reference(
    x, norm_g, ffn_w_in, ffn_w_out, hg_w_in, hg_lb_logits, hg_out_norm_g, hg_w_out, fox_w_in,
    fox_b_f, fox_q_norm_g, fox_k_norm_g, fox_w_out, ffn1_norm_2, ffn1_w_in_2, ffn1_w_out_2,
    mix_norm_2, ffn2_norm_2, ffn2_w_in_2, ffn2_w_out_2, conv_w_in_2, conv_w_2, conv_w_out_2,
    attn_w_q_2, attn_q_norm_2, attn_w_o_2, kv_norm_2, w_kv_2, k_norm_2, cmp_pe_k_2, cmp_pe_v_2,
    cmp_w1_k_2, cmp_w2_k_2, cmp_w1_v_2, cmp_w2_v_2, rel_bias_2,
):
    x = first_block(
        x, norm_g, ffn_w_in, ffn_w_out, hg_w_in, hg_lb_logits, hg_out_norm_g, hg_w_out,
        fox_w_in, fox_b_f, fox_q_norm_g, fox_k_norm_g, fox_w_out,
    )
    return second_block(
        x, ffn1_norm_2, ffn1_w_in_2, ffn1_w_out_2, mix_norm_2, ffn2_norm_2, ffn2_w_in_2,
        ffn2_w_out_2, conv_w_in_2, conv_w_2, conv_w_out_2, attn_w_q_2, attn_q_norm_2,
        attn_w_o_2, kv_norm_2, w_kv_2, k_norm_2, cmp_pe_k_2, cmp_pe_v_2, cmp_w1_k_2, cmp_w2_k_2,
        cmp_w1_v_2, cmp_w2_v_2, rel_bias_2,
    )


_drawn_inputs = setup_inputs


def setup_inputs(seed=0):
    import zlib

    import numpy as np

    out = dict(_drawn_inputs(seed))
    spreads = {}
    factors = {'fox_q_norm_g': 5.418,
     'fox_k_norm_g': 6.003,
     'ffn1_norm_2': 5.656,
     'ffn2_norm_2': 8.0,
     'attn_q_norm_2': 8.0,
     'kv_norm_2': 8.0,
     'k_norm_2': 8.0,
     'cmp_pe_k_2': 8.0,
     'cmp_pe_v_2': 27.456,
     'rel_bias_2': 4.354}
    for name, (base, spread) in spreads.items():
        noise = np.random.default_rng([zlib.crc32(name.encode()), seed]).standard_normal(out[name].shape)
        drawn = base * np.exp(spread * noise) if base else spread * noise
        out[name] = __import__('jax').numpy.asarray(drawn.astype(out[name].dtype))
    for name, factor in factors.items():
        out[name] = (out[name] * factor).astype(out[name].dtype)
    return out
```

```python
from contextlib import ExitStack

import numpy as np

import concourse.bass as bass
import concourse.mybir as mybir
from concourse.alu_op_type import AluOpType as ALU

ACT = mybir.ActivationFunctionType
AX = mybir.AxisListType
F32 = mybir.dt.float32
F32R = mybir.dt.float32r
I32 = mybir.dt.int32

P = 128
D = 1024
KT = D // P
T = 256
NT = T // P
D_FF = 2816
FC = 256
NCH = D_FF // FC
CW = 512
EPS = 1e-6
NEG = -1e30
MIN_GATE = 1e-30

HG_HEADS, HG_CHUNK = 8, 64
FOX_HEADS = NSA_HEADS = 16
DH = 64
GROUPS = 4
CMP_BLOCK, CMP_STRIDE = 32, 16
NC_CMP = (T - CMP_BLOCK) // CMP_STRIDE + 1
NB_CMP = CMP_STRIDE
N_BUCKETS, MAX_EXACT, MAX_DISTANCE = 32, 16, 4096
REL_ROWS = N_BUCKETS + 1
REL_W = 512
ARENA = 14336

G_NORM = 0
G_FFN1, G_MIX, G_FFN2 = 48, 64, 80
G_KV = 96
G_CONV = 104
G_LB = 128
G_FOXQ, G_FOXK, G_NSAQ, G_KN = 136, 137, 138, 139
G_PE = 142
G_ROWS = 174


class Loop:

    def __init__(self, n, per):
        self.n, self.per, self.var = n, per, None


class Point:

    def __init__(self, counter, k, loop):
        self.counter, self.k, self.loop = counter, k, loop


class Counter:

    def __init__(self, prog, name, step=1):
        self.prog, self.step, self.n = prog, step, 0
        self.sem = prog.stack.enter_context(prog.nc.semaphore(name))
        self.name = name
        prog.counters.append(self)

    def mark(self, ins):
        ins.then_inc(self.sem, self.step)
        self.n += 1
        return Point(self, self.n, self.prog.loop)


class Engine:

    def __init__(self, prog, eng, name):
        self.prog, self.queue, self.done = prog, eng, Counter(prog, "done_" + name)
        self.met, self.pending = {}, {}

    def mark(self, ins):
        return self.done.mark(ins)

    def wait(self, *points, fixed=False):
        cur = self.prog.loop
        for p in points:
            if p is None:
                continue
            c, k = p.counter, p.k
            if p.loop is not None and p.loop is not cur:
                k += (p.loop.n - 1) * p.loop.per.get(c.name, 0)
            moves = cur is not None and not fixed and cur.per.get(c.name, 0) > 0
            if not moves and self.met.get(c.name, 0) >= k:
                continue
            before = self.pending.get(c)
            assert before is None or before[0] == moves, c.name
            self.pending[c] = (moves, max(k, before[1] if before else 0))

    def flush(self):
        return self.eng

    @property
    def eng(self):
        cur = self.prog.loop
        for c, (moves, k) in self.pending.items():
            if moves:
                self.queue.wait_ge(c.sem, (cur.var * cur.per[c.name] + k) * c.step)
            else:
                self.queue.wait_ge(c.sem, k * c.step)
                self.met[c.name] = k
        self.pending = {}
        return self.queue


class Program:
    def __init__(self, nc, stack):
        self.nc, self.stack, self.loop, self.counters = nc, stack, None, []
        self.pe = Engine(self, nc.tensor, "pe")
        self.act = Engine(self, nc.scalar, "act")
        self.dve = Engine(self, nc.vector, "dve")
        self.sp = Engine(self, nc.sync, "sp")
        self.pool = Engine(self, nc.gpsimd, "pool")

    def repeat(self, n, per, body):
        et = mybir.EngineType
        start = {c.name: c.n for c in self.counters}
        self.loop = Loop(n, per)
        with self.nc.Fori(0, n, engines=(et.Activation, et.PE, et.DVE, et.SP)) as i:
            self.loop.var = i
            body(i)
        for c in self.counters:
            grown = c.n - start[c.name]
            assert grown == per.get(c.name, 0), (c.name, grown)
            c.n += (n - 1) * grown
        self.loop = None


class Kernel:
    def __init__(self, nc, stack, t):
        self.nc, self.stack, self.t = nc, stack, t
        g = self.g = Program(nc, stack)
        self.pe, self.act, self.dve, self.sp, self.pool = g.pe, g.act, g.dve, g.sp, g.pool
        sb = self.sb
        self.x = sb("x_tok", [P, NT, D])
        self.xt_hi = sb("xt_hi", [P, KT, T], F32R)
        self.xt_lo = sb("xt_lo", [P, KT, T], F32R)
        self.xg = sb("xt_full", [P, 2, CW])
        self.raw = sb("raw_in", [P, 2, KT // 2, CW])
        self.raw_out = sb("raw_out", [P, FC // P, D])
        self.w_hi = sb("w_hi", [P, 2, KT, CW], F32R)
        self.w_lo = sb("w_lo", [P, 2, KT, CW], F32R)
        self.wo_hi = sb("wo_hi", [P, FC // P, D], F32R)
        self.wo_lo = sb("wo_lo", [P, FC // P, D], F32R)
        self.silu = sb("silu", [P, NT, FC])
        self.h = sb("h_tok", [P, NT, FC])
        self.ht_hi = sb("ht_hi", [P, FC // P * NT, P], F32R)
        self.ht_lo = sb("ht_lo", [P, FC // P * NT, P], F32R)
        self.ident = sb("ident", [P, P])
        self.gains = sb("gains", [P, G_ROWS])
        self.ssq = sb("ssq", [P, NT])
        self.inv = sb("inv", [P, NT])
        self.rstd = sb("rstd", [P, NT])
        self.diag = sb("diag", [P, NT, P])
        self.sq_junk = sb("sq_junk", [P, CW])
        self.hn = sb("hn", [P, 2, 3, KT])
        self.masks = sb("masks", [P, 8, P], I32)
        self.rowmask = sb("rowmask", [P, NT])
        self.og = sb("hg_gain", [P, P])[:]
        self.lbs = sb("lower_bound", [P, 2, KT])
        self.arena = sb("arena", [P, ARENA])
        self.small = sb("small", [P, 2, 5, 16])
        self.bank = [self.ps(f"bank{t}", [P, CW]) for t in range(2)]
        self.acc = [self.ps(f"acc{i}", [P, CW]) for i in range(4)]
        self.tr = [self.ps(f"tr{i}", [P, CW]) for i in range(2)]
        self.landed = [Counter(g, f"landed_{n}", 16) for n in ("a", "b", "out")]
        self.consts_in = Counter(g, "consts_in", 16)
        self.arena_in = Counter(g, "arena_in", 16)
        self.scratch = Counter(g, "scratch", 16)
        self.stored = Counter(g, "stored", 16)
        self.split_hi = [None, None, None]
        self.split_lo = [None, None, None]
        self.used = [None, None]
        self.w_ready = [[None, None], [None, None]]
        self.used_out = None
        self.par = 0
        self.bank_free = [None, None]
        self.acc_free = [None] * 4
        self.tr_free = [None, None]
        self.queue = []
        self.x_ready = [None, None]

    def sb(self, name, shape, dt=F32):
        return self.stack.enter_context(self.nc.sbuf_tensor(name, shape, dt))

    def ps(self, name, shape):
        return self.stack.enter_context(self.nc.psum_tensor(name, shape, F32))

    def area(self, at, *shape, parts=P):
        n = int(np.prod(shape))
        assert at + n <= ARENA
        v = self.arena[0:parts, at:at + n]
        if len(shape) == 2:
            v = v.rearrange("p (a b) -> p a b", a=shape[0])
        elif len(shape) == 3:
            v = v.rearrange("p (a b c) -> p a b c", a=shape[0], b=shape[1])
        elif len(shape) == 4:
            v = v.rearrange("p (a b c d) -> p a b c d", a=shape[0], b=shape[1], c=shape[2])
        return v

    def a(self, out, src, func, *after, **kw):
        self.act.wait(*after)
        return self.act.mark(self.act.eng.activation(out, src, func, **kw))

    def tt(self, out, x, y, op, *after):
        self.dve.wait(*after)
        return self.dve.mark(self.dve.eng.tensor_tensor(out, x, y, op))

    def ts(self, out, x, s1, s2, op0, op1, *after):
        self.dve.wait(*after)
        if op1 is None:
            return self.dve.mark(self.dve.eng.tensor_scalar(out, x, s1, None, op0))
        return self.dve.mark(self.dve.eng.tensor_scalar(out, x, s1, s2, op0, op1))

    def stt(self, out, x, s, y, op0, op1, *after):
        self.dve.wait(*after)
        return self.dve.mark(self.dve.eng.scalar_tensor_tensor(out, x, s, y, op0, op1))

    def red(self, out, x, op, *after, **kw):
        self.dve.wait(*after)
        return self.dve.mark(self.dve.eng.tensor_reduce(out, x, AX.X, op, **kw))

    def mm(self, out, lhs, rhs, *after, start=True, stop=True):
        self.pe.wait(*after)
        return self.pe.mark(self.pe.eng.matmul(out, lhs, rhs, start=start, stop=stop))

    def split_piece(self, s, dst_hi, dst_lo, raw, parts, free):
        act, dve, sp = self.act, self.dve, self.sp
        sp.wait(self.split_lo[s])
        for to, src in parts:
            landed = self.landed[s].mark(sp.eng.dma_start(to(raw), src))
        act.wait(landed, free)
        self.split_hi[s] = act.mark(act.eng.activation(dst_hi, raw, ACT.Copy))
        dve.wait(self.split_hi[s])
        self.split_lo[s] = dve.mark(dve.eng.tensor_tensor(dst_lo, raw, dst_hi.bitcast(F32), ALU.subtract))

    def prefetch(self, piece, par, parts, w=CW):
        sl = (slice(None), par, slice(piece * KT // 2, (piece + 1) * KT // 2), slice(0, w))
        self.split_piece(piece, self.w_hi[sl], self.w_lo[sl], self.raw[:, piece, :, 0:w], parts, self.used[par])

    def prefetch_out(self, src):
        self.split_piece(2, self.wo_hi[:], self.wo_lo[:], self.raw_out[:], [(lambda r: r, src)], self.used_out)

    def ffn_src(self, w_in, c):
        v = w_in.rearrange("(k p) (g n) -> p k g n", p=P, g=2)
        if not isinstance(c, int):
            c = self.sp.queue.snap(c)
        return lambda piece: [
            (lambda r, g=g: r[:, :, g * FC:(g + 1) * FC],
             v[:, piece * KT // 2:(piece + 1) * KT // 2, g, bass.ds(c * FC, FC)]) for g in range(2)]

    def mat_src(self, w, c0, wd=CW):
        v = w.rearrange("(k p) n -> p k n", p=P)
        return lambda piece: [(lambda r: r, v[:, piece * KT // 2:(piece + 1) * KT // 2, c0:c0 + wd])]

    def kv_pair_src(self, w):
        v = w.rearrange("(k p) (b g d) -> p k b g d", p=P, b=6, g=GROUPS)
        return lambda piece: [
            (lambda r, b=b, k=k: r.rearrange("p k (g b d) -> p k b g d", g=GROUPS, b=2)[:, k, b],
             v[:, piece * KT // 2 + k, b]) for b in range(2) for k in range(KT // 2)]

    def product(self, par, t, w=CW, feature_major=False):
        pe = self.pe
        pe.wait(self.bank_free[t])
        pe.wait(*self.w_ready[par])
        pe.wait(*self.xt_ready[t], fixed=True)
        if feature_major:
            pe.wait(*self.xt_ready[1], fixed=True)
        out = self.bank[t]
        w_hi, w_lo = self.w_hi[:, par], self.w_lo[:, par]
        if feature_major:
            for f in range(2):
                c = slice((2 * t + f) * P, (2 * t + f + 1) * P)
                o = out[:, f * T:(f + 1) * T]
                for k in range(KT):
                    mm = pe.eng.matmul
                    mm(o, w_hi[:, k, c], self.xt_hi[:, k, :], start=(k == 0), stop=False)
                    mm(o, w_hi[:, k, c], self.xt_lo[:, k, :], start=False, stop=False)
                    last = mm(o, w_lo[:, k, c], self.xt_hi[:, k, :], start=False,
                              stop=(k == KT - 1))
        else:
            tok = slice(t * P, (t + 1) * P)
            for k in range(KT):
                mm = pe.eng.matmul
                mm(out[:, 0:w], self.xt_hi[:, k, tok], w_hi[:, k, 0:w], start=(k == 0), stop=False)
                mm(out[:, 0:w], self.xt_hi[:, k, tok], w_lo[:, k, 0:w], start=False, stop=False)
                last = mm(out[:, 0:w], self.xt_lo[:, k, tok], w_hi[:, k, 0:w], start=False,
                          stop=(k == KT - 1))
        return pe.mark(last)

    def pop_next(self, piece):
        if self.queue:
            src, w = self.queue[0]
            self.prefetch(piece, 1 - self.par, src(piece), w)
            self.w_ready[1 - self.par][piece] = self.split_lo[piece]
            if piece == 1:
                self.queue.pop(0)

    def chunk(self, read, w=CW, feature_major=False, between=None):
        for t in range(2):
            self.pop_next(t)
            point = self.product(self.par, t, w, feature_major)
            if t == 0 and between:
                between()
            read(t, point)
        self.used[self.par] = point
        self.par = 1 - self.par

    def to_xt(self, src, gain=None, normed=False, deferred=False, ready=(None, None)):
        pe, act, dve = self.pe, self.act, self.dve
        self.xt_ready = [None, None]
        rstd_at = [None, None]
        for t in range(NT):
            if normed:
                act.wait(ready[t])
                part = []
                for half in range(2):
                    p = act.mark(act.eng.activation(
                        self.sq_junk[:], self.x[:, t, half * CW:(half + 1) * CW], ACT.Square,
                        accum_out=self.hn[:, t, 0, half:half + 1]))
                    act.wait(p)
                dve.wait(p)
                ms = self.ssq[:, t:t + 1]
                q = dve.mark(dve.eng.tensor_tensor(ms, self.hn[:, t, 0, 0:1], self.hn[:, t, 0, 1:2], ALU.add))
                dve.wait(q)
                q = dve.mark(dve.eng.tensor_scalar(self.inv[:, t:t + 1], ms, 1.0 / D, EPS, ALU.mult, ALU.add))
                dve.wait(q)
                q = dve.mark(dve.eng.reciprocal(ms, self.inv[:, t:t + 1]))
                act.wait(q)
                rstd_at[t] = act.mark(act.eng.activation(self.rstd[:, t:t + 1], ms, ACT.Sqrt))
                if not deferred:
                    dve.wait(rstd_at[t])
                    rstd_at[t] = dve.mark(dve.eng.tensor_scalar(
                        self.diag[:, t, :], self.ident[:], self.rstd[:, t:t + 1], None, ALU.mult))
        self.rstd_at = rstd_at
        for t in range(NT):
            pts = []
            for half in range(2):
                pe.wait(ready[t], self.tr_free[half])
                if normed and not deferred:
                    pe.wait(rstd_at[t])
                for k in range(4):
                    lhs = src(t, 4 * half + k)
                    o = self.tr[half][:, k * P:(k + 1) * P]
                    if normed and not deferred:
                        ins = pe.eng.matmul(o, lhs, self.diag[:, t, :], start=True, stop=True)
                    else:
                        ins = pe.eng.transpose(o, lhs, self.ident[:])
                turned = pe.mark(ins)
                self.src_read = turned
                hi = self.xt_hi[:, 4 * half:4 * half + 4, t * P:(t + 1) * P]
                lo = self.xt_lo[:, 4 * half:4 * half + 4, t * P:(t + 1) * P]
                full = self.tr[half][:].rearrange("p (k n) -> p k n", k=4)
                if gain is not None:
                    g = self.gains[:, gain + 4 * half:gain + 4 * half + 4].unsqueeze(2).to_broadcast([P, 4, P])
                    dve.wait(turned, self.xg_free[half])
                    scaled = self.xg[:, half, :].rearrange("p (k n) -> p k n", k=4)
                    turned = dve.mark(dve.eng.tensor_tensor(scaled, full, g, ALU.mult))
                    self.tr_free[half] = turned
                    full = scaled
                act.wait(turned, self.used[1 - self.par])
                hi_at = act.mark(act.eng.activation(hi, full, ACT.Copy))
                dve.wait(turned, hi_at, self.used[1 - self.par])
                lo_at = dve.mark(dve.eng.tensor_tensor(lo, full, hi.bitcast(F32), ALU.subtract))
                if gain is not None:
                    self.xg_free[half] = lo_at
                else:
                    self.tr_free[half] = lo_at
                pts += [hi_at, lo_at]
            self.xt_ready[t] = pts

    def x_tile(self, t, k):
        return self.x[:, t, k * P:(k + 1) * P]

    def ffn(self, w_in, w_out, gain, last=False):
        pe, act, dve = self.pe, self.act, self.dve
        self.to_xt(self.x_tile, gain=gain, normed=True, deferred=True, ready=self.x_ready)
        rstd_at = self.rstd_at
        w_out_v = w_out.rearrange("(c k p) n -> c p k n", p=P, k=FC // P)
        h_at = [None, None]
        state = {"turned": None}

        def read(t, point):
            act.wait(point)
            act.wait(rstd_at[t], fixed=True)
            act.wait(self.h_at[t])
            s = act.mark(act.eng.activation(self.silu[:, t, :], self.bank[t][:, 0:FC], ACT.Silu,
                                            scale=self.rstd[:, t:t + 1]))
            dve.wait(s, state["turned"])
            self.h_at[t] = dve.mark(dve.eng.scalar_tensor_tensor(
                self.h[:, t, :], self.bank[t][:, FC:2 * FC], self.rstd[:, t:t + 1], self.silu[:, t, :],
                ALU.mult, ALU.mult))
            self.bank_free[t] = self.h_at[t]

        def turn():
            pe.wait(*self.h_at, self.tr_free[0])
            for f in range(FC // P):
                for t in range(NT):
                    i = f * NT + t
                    ins = pe.eng.transpose(self.tr[0][:, i * P:(i + 1) * P],
                                           self.h[:, t, f * P:(f + 1) * P], self.ident[:])
            state["turned"] = pe.mark(ins)
            full = self.tr[0][:].rearrange("p (i n) -> p i n", n=P)
            act.wait(state["turned"], self.used_out)
            self.ht_hi_at = act.mark(act.eng.activation(self.ht_hi[:], full, ACT.Copy))
            dve.wait(self.ht_hi_at)
            self.ht_at = dve.mark(dve.eng.tensor_tensor(self.ht_lo[:], full, self.ht_hi[:].bitcast(F32),
                                                        ALU.subtract))
            self.tr_free[0] = self.ht_at

        def second(c, start, stop):
            pe.wait(self.ht_at, self.split_lo[2])
            for t in range(NT):
                for half in range(2):
                    a = 2 * t + half
                    if start:
                        pe.wait(self.acc_free[a])
                    cols = slice(half * CW, (half + 1) * CW)
                    for f in range(FC // P):
                        i = f * NT + t
                        mm = pe.eng.matmul
                        mm(self.acc[a][:], self.ht_hi[:, i, :], self.wo_hi[:, f, cols],
                           start=(start and f == 0), stop=False)
                        mm(self.acc[a][:], self.ht_hi[:, i, :], self.wo_lo[:, f, cols], start=False, stop=False)
                        ins = mm(self.acc[a][:], self.ht_lo[:, i, :], self.wo_hi[:, f, cols], start=False,
                                 stop=(stop and f == FC // P - 1))
                    if stop:
                        self.acc_at[a] = pe.mark(ins)
            self.used_out = self.acc_at[3] if stop else pe.mark(ins)

        def body(c, start=False):
            if not isinstance(c, int):
                c = self.sp.queue.snap(c)
            self.prefetch_out(w_out_v[c] if isinstance(c, int) else w_out_v[bass.ds(c, 1)].rearrange(
                "c p k n -> (c p) k n"))
            self.chunk(read, between=turn)
            second(c, start, False)

        self.acc_at = [None] * 4
        self.queue.insert(0, (self.ffn_src(w_in, 1), CW))
        self.h_at = list(self.h_at_prev)
        self.chunk(read)
        self.queue.insert(0, (self.ffn_src(w_in, 2), CW))
        body(0, start=True)

        per = {"done_act": 2 * 6, "done_dve": 2 * 6, "done_pe": 2 * 4,
               "landed_a": 4, "landed_b": 4, "landed_out": 2}

        def two(i):
            for j in range(2):
                c = i * 2 + (1 + j)
                self.queue.insert(0, (self.ffn_src(w_in, c + 2), CW))
                body(c)

        self.g.repeat((NCH - 3) // 2, per, two)
        body(NCH - 2)
        self.prefetch_out(w_out_v[NCH - 1])
        turn()
        second(NCH - 1, False, True)
        self.h_at_prev = list(self.h_at)
        ready = []
        for t in range(NT):
            for half in range(2):
                cols = slice(half * CW, (half + 1) * CW)
                dve.wait(self.acc_at[2 * t + half], self.src_read)
                p = dve.mark(dve.eng.scalar_tensor_tensor(self.x[:, t, cols], self.acc[2 * t + half][:], 0.5,
                                                          self.x[:, t, cols], ALU.mult, ALU.add))
                self.acc_free[2 * t + half] = p
            ready.append(p)
        self.x_ready = ready

    def out_projection(self):
        for c in range(D // CW):
            def read(t, point):
                cols = slice(c * CW, (c + 1) * CW)
                self.dve.wait(point, self.src_read)
                self.bank_free[t] = self.dve.mark(self.dve.eng.tensor_tensor(
                    self.x[:, t, cols], self.bank[t][:], self.x[:, t, cols], ALU.add))
                self.x_ready[t] = self.bank_free[t]
            self.chunk(read)

    def conv_chunks(self):
        return [(self.mat_src(self.t["conv_w_in_2"][0], c * CW), CW) for c in range(3 * D // CW)] + [
            (self.mat_src(self.t["conv_w_out_2"][0], c * CW), CW) for c in range(D // CW)]

    def conv(self):
        self.to_xt(self.x_tile, gain=G_MIX, normed=True, ready=self.x_ready)
        taps = 3
        b = self.area(0, KT, T)
        y = self.area(2048, KT, T)
        u = self.area(4096, KT, T + taps - 1)
        self.pool.wait(*self.x_ready)
        zero = self.pool.mark(self.pool.eng.memset(u[:, :, 0:taps - 1], 0.0))
        c_at, z_at = {}, []
        pair = lambda v, n: v[:, 2 * n:2 * n + 2]
        for i in range(2):
            def read(t, p, i=i):
                self.b_at = self.bank_free[t] = self.a(
                    pair(b, 2 * i + t), self.bank[t][:].rearrange("p (f n) -> p f n", f=2), ACT.Copy, p)
            self.chunk(read, feature_major=True)
        for i in range(2):
            def read(t, p, i=i):
                dst = pair(u, 2 * i + t)[:, :, taps - 1:]
                c_at[2 * i + t] = self.bank_free[t] = self.a(
                    dst, self.bank[t][:].rearrange("p (f n) -> p f n", f=2), ACT.Copy, p)
            self.chunk(read, feature_major=True)
        for i in range(2):
            def read(t, p, i=i):
                n = 2 * i + t
                dst = pair(u, n)[:, :, taps - 1:]
                q = self.bank_free[t] = self.tt(dst, self.bank[t][:].rearrange("p (f n) -> p f n", f=2), dst,
                                                ALU.mult, p, c_at[n], zero)
                for f in range(2):
                    k = 2 * n + f
                    g = lambda j: self.gains[:, G_CONV + j * KT + k:G_CONV + j * KT + k + 1]
                    r = self.ts(y[:, k], u[:, k, 0:T], g(0), None, ALU.mult, None, q)
                    r = self.stt(y[:, k], u[:, k, 1:T + 1], g(1), y[:, k], ALU.mult, ALU.add, r)
                    r = self.stt(y[:, k], u[:, k, 2:T + 2], g(2), y[:, k], ALU.mult, ALU.add, r)
                z_at.append(self.tt(pair(y, n), pair(y, n), pair(b, n), ALU.mult, r, self.b_at))
            self.chunk(read, feature_major=True)
        ready = []
        for n in range(4):
            hi = pair(self.xt_hi, n)
            p = self.a(hi, pair(y, n), ACT.Copy, z_at[n], self.used[1 - self.par])
            ready += [p, self.tt(pair(self.xt_lo, n), pair(y, n), hi.bitcast(F32), ALU.subtract, p)]
        self.xt_ready = [ready, ready]
        self.out_projection()

    def head_rms(self, t, src, heads, width, point, slot=0):
        sq = self.sq_junk[:, 0:heads * width]
        ss, ms, r = (self.small[:, slot, j, 0:heads] for j in range(3))
        s3 = src.rearrange("p (h d) -> p h d", h=heads)
        p = self.a(sq.rearrange("p (h d) -> p h d", h=heads), s3, ACT.Square, point, self.sq_free)
        p = self.red(ss, sq.rearrange("p (h d) -> p h d", h=heads), ALU.add, p, self.rms_free[slot])
        self.sq_free = p
        p = self.ts(ms, ss, 1.0 / width, EPS, ALU.mult, ALU.add, p)
        self.dve.wait(p)
        p = self.dve.mark(self.dve.eng.reciprocal(ss, ms))
        return r, self.a(r, ss, ACT.Sqrt, p)

    def turn_heads(self, t, src, dst, gain, *after):
        self.pe.wait(self.tr_free[t], *after)
        for i in range(4):
            ins = self.pe.eng.transpose(self.tr[t][:, i * P:(i + 1) * P], src(i), self.ident[:])
        p = self.pe.mark(ins)
        self.turned_at = p
        v = self.tr[t][:].rearrange("p (i n) -> p i n", i=4)
        self.tr_free[t] = self.a(dst, v, ACT.Copy, p, scale=self.gains[:, gain:gain + 1])
        return self.tr_free[t]

    def normed_heads(self, t, point, dst, dup=1, width=CW):
        n = width // DH
        r, p = self.head_rms(t, self.bank[t][:, 0:width], n, DH, point, slot=t)
        src = self.bank[t][:, 0:width].rearrange("p (h d) -> p h d", h=n)
        if dup == 1:
            o, s, rr = dst.rearrange("p (h d) -> p h d", h=n), src, r.unsqueeze(2).to_broadcast([P, n, DH])
            p = self.tt(o, s, rr, ALU.mult, p)
        else:
            for j in range(dup):
                p = self.tt(dst[:, :, j, :], src, r.unsqueeze(2).to_broadcast([P, n, DH]), ALU.mult, p)
        self.rms_free[t] = self.bank_free[t] = p
        return p

    def fox_chunks(self):
        w = self.t["fox_w_in"][0]
        cols = [0, CW, D, D + CW, 2 * D, 2 * D + CW]
        return ([(self.mat_src(w, c), CW) for c in cols]
                + [(self.mat_src(w, 4 * D, FOX_HEADS), FOX_HEADS)]
                + [(self.mat_src(w, 3 * D + c * CW), CW) for c in range(2)]
                + [(self.mat_src(self.t["fox_w_out"][0], c * CW), CW) for c in range(D // CW)])

    def fox(self):
        tmp = self.area(0, NT, D)
        qt, kt = self.area(2048, KT, T), self.area(4096, KT, T)
        v, g = self.area(6144, NT, D), self.area(8192, NT, D)
        select = self.area(10240, FOX_HEADS, P)
        s_buf = self.area(12288, 2, T)
        pt = self.area(12800, 2, T)
        nct = self.area(13312, T)
        causal = self.area(13568, T)
        upto = self.area(13824, P)
        ones = self.area(13952, P)
        lf = self.area(14080, NT, FOX_HEADS)
        cc = self.area(14112, NT, FOX_HEADS)
        z = self.area(14144, NT, FOX_HEADS)
        bf = self.area(14176, FOX_HEADS)
        nm, den = self.area(14192, NT, FOX_HEADS), self.area(14224, NT, FOX_HEADS)
        gq = self.area(14256, 1)
        sp, pe, pool = self.sp, self.pe, self.pool
        self.act.wait(*self.x_ready)
        load = lambda d, s_: self.arena_in.mark(self.act.eng.dma_start(d, s_))
        load(select, self.t["c_select"])
        load(upto, self.t["c_upto"])
        load(causal, self.t["c_causal"].rearrange("p a b -> p (a b)"))
        b_f = self.t["fox_b_f"]
        here = load(bf, bass.AP(tensor=b_f.tensor, offset=b_f.offset, ap=[[0, P], [1, FOX_HEADS]]))
        pool.wait(*self.x_ready)
        pool.wait(pool.mark(pool.eng.memset(ones, 1.0)))
        set_at = pool.mark(pool.eng.memset(nct, 0.0))
        self.to_xt(self.x_tile, gain=G_NORM + 32, normed=True, ready=self.x_ready)

        gq_at = self.ts(self.gains[:, G_FOXQ:G_FOXQ + 1], self.gains[:, G_FOXQ:G_FOXQ + 1], DH ** -0.5, None,
                        ALU.mult, None)
        self.act.wait(gq_at)
        last = {}
        turned = {}
        todo = []

        def turn_todo():
            while todo:
                todo.pop(0)()

        for i in range(4):
            dst_t, gain = (qt, G_FOXQ) if i < 2 else (kt, G_FOXK)

            def read(t, p, i=i, dst_t=dst_t, gain=gain):
                c = i % 2
                turn_todo()
                cols = tmp[:, t, c * CW:(c + 1) * CW]
                self.dve.wait(turned.get((i - 2, t)))
                n = self.normed_heads(t, p, cols)

                def later():
                    last[i, t] = self.turn_heads(
                        t, lambda j: tmp[:, t, c * CW + j * P:c * CW + (j + 1) * P],
                        dst_t[:, 4 * c:4 * c + 4, t * P:(t + 1) * P], gain, n)
                    turned[i, t] = self.turned_at
                todo.append(later)
            self.chunk(read)
        for i in range(2):
            def read(t, p, i=i):
                turn_todo()
                self.v_at = self.bank_free[t] = self.a(v[:, t, i * CW:(i + 1) * CW], self.bank[t][:], ACT.Copy, p)
            self.chunk(read)
        qk_at = [last[k] for k in last]

        def read(t, p):
            h = self.small[:, t, 3, :]
            p = self.bank_free[t] = self.tt(z[:, t], self.bank[t][:, 0:FOX_HEADS], bf, ALU.add, p, here)
            q = self.a(h, z[:, t], ACT.Abs, p)
            q = self.a(h, h, ACT.Exp, q, scale=-1.0)
            q = self.a(h, h, ACT.Ln, q, bias=1.0)
            self.lf_at[t] = self.stt(lf[:, t], z[:, t], 0.0, h, ALU.min, ALU.subtract, q)
        self.lf_at = [None, None]
        self.chunk(read, w=FOX_HEADS)

        def cumulate():
            pe.wait(set_at, here, *self.tr_free)
            o = self.tr[0]
            self.mm(o[:, 0:16], upto, lf[:, 0], *self.lf_at)
            self.mm(o[:, 16:32], upto, lf[:, 1], start=True, stop=False)
            p = self.mm(o[:, 16:32], ones, lf[:, 0], start=False, stop=True)
            o2 = self.tr[1]
            self.mm(o2[0:16, 0:P], lf[:, 0], upto)
            self.mm(o2[0:16, P:T], lf[:, 1], upto, start=True, stop=False)
            q = self.mm(o2[0:16, P:T], lf[:, 0], ones, start=False, stop=True)
            self.tr_free[0] = self.cc_at = self.a(cc, o[:, 0:32].rearrange("p (t h) -> p t h", t=2), ACT.Copy, p)
            self.tr_free[1] = self.nct_at = self.ts(nct[0:16], o2[0:16, 0:T], -1.0, None, ALU.mult, None, q, set_at)

        for i in range(2):
            def read(t, p, i=i):
                if i == 0 and t == 0:
                    cumulate()
                self.g_at = self.bank_free[t] = self.a(g[:, t, i * CW:(i + 1) * CW], self.bank[t][:],
                                                       ACT.Sigmoid, p)
            self.chunk(read)

        steps = [(h, t) for h in range(FOX_HEADS) for t in range(NT)]
        st = {}

        def scores(i):
            h, t = steps[i]
            rows, n = slice(DH * (h % 2), DH * (h % 2) + DH), (t + 1) * P
            pe.wait(self.bank_free[i % 2], self.nct_at, *qk_at)
            o = self.bank[i % 2][:, 0:n]
            self.mm(o, qt[rows, h // 2, t * P:(t + 1) * P], kt[rows, h // 2, 0:n], start=True, stop=False)
            p = self.mm(o, select[:, h], nct[:, 0:n], start=False, stop=True)
            s = s_buf[:, i % 2, 0:n]
            p = self.bank_free[i % 2] = self.stt(s, o, cc[:, t, h:h + 1], causal[:, T - n:T], ALU.add, ALU.add,
                                                 p, self.cc_at, st.get(("turned", i - 2)))
            p = self.red(nm[:, t, h:h + 1], s, ALU.max, p, negate=True)
            st["exp", i] = self.a(s, s, ACT.Exp, p, bias=nm[:, t, h:h + 1], accum_out=den[:, t, h:h + 1])

        def turn(i):
            h, t = steps[i]
            pe.wait(st["exp", i], self.tr_free[i % 2])
            for b in range(t + 1):
                ins = pe.eng.transpose(self.tr[i % 2][:, b * P:(b + 1) * P],
                                       s_buf[:, i % 2, b * P:(b + 1) * P], self.ident[:])
            p = st["turned", i] = pe.mark(ins)
            n = (t + 1) * P
            if i % 2:
                st["pt", i] = self.tr_free[i % 2] = self.a(pt[:, i % 2, 0:n], self.tr[i % 2][:, 0:n], ACT.Copy, p,
                                                           st.get(("pv", i - 2)))
            else:
                self.dve.wait(p, st.get(("pv", i - 2)))
                st["pt", i] = self.tr_free[i % 2] = self.dve.mark(self.dve.eng.tensor_copy(
                    pt[:, i % 2, 0:n], self.tr[i % 2][:, 0:n]))

        def values(i):
            h, t = steps[i]
            a = 2 * t + h // 8
            pe.wait(st["pt", i], self.v_at, self.acc_free[a])
            for b in range(t + 1):
                p = self.mm(self.acc[a][:, (h % 8) * DH:(h % 8 + 1) * DH], pt[:, i % 2, b * P:(b + 1) * P],
                            v[:, b, h * DH:(h + 1) * DH], start=(b == 0), stop=(b == t))
            st["pv", i] = p

        for i in range(len(steps) + 2):
            if i < len(steps):
                scores(i)
            if 1 <= i <= len(steps):
                turn(i - 1)
            if i >= 2:
                values(i - 2)
        self.dve.wait(st["exp", len(steps) - 1])
        inv_at = self.dve.mark(self.dve.eng.reciprocal(den, den))
        o_at = []
        for t in range(NT):
            for half in range(2):
                cols = slice(half * CW, (half + 1) * CW)
                r = den[:, t, 8 * half:8 * half + 8].unsqueeze(2).to_broadcast([P, 8, DH])
                o3 = tmp[:, t, cols].rearrange("p (h d) -> p h d", h=8)
                p = self.tt(o3, self.acc[2 * t + half][:].rearrange("p (h d) -> p h d", h=8), r, ALU.mult,
                            st["pv", len(steps) - 1 - (half == 0)], st["pv", len(steps) - 1], inv_at)
                self.acc_free[2 * t + half] = p
                p = self.tt(tmp[:, t, cols], tmp[:, t, cols], g[:, t, cols], ALU.mult, p, self.g_at)
            o_at.append(p)
        self.to_xt(lambda t, k: tmp[:, t, k * P:(k + 1) * P], ready=o_at)
        self.out_projection()

    def hgrn_chunks(self):
        w = self.t["hg_w_in"][0]
        cols = [D, D + CW, 0, CW, 2 * D, 2 * D + CW, 3 * D, 3 * D + CW]
        return [(self.mat_src(w, c), CW) for c in cols] + [
            (self.mat_src(self.t["hg_w_out"][0], c * CW), CW) for c in range(D // CW)]

    def hgrn(self):
        H = HG_HEADS
        bc = self.area(0, H, T)
        kk, qq = self.area(2048, H, T), self.area(4096, H, T)
        v, g = self.area(6144, NT, D), self.area(8192, NT, D)
        xx = self.area(10240, 2, 4, T)
        pt = self.area(12288, 3, 4, P)
        tiny_at, reset_at = 10240, 12288
        tiny = self.area(tiny_at, H * T)
        reset = self.area(reset_at, H * T)
        self.to_xt(self.x_tile, gain=G_NORM + 8, normed=True, ready=self.x_ready)
        pool, pe, dve = self.pool, self.pe, self.dve
        pool.wait(*self.x_ready)
        p = pool.mark(pool.eng.memset(reset, 1.0))
        pool.wait(p)
        reset_set = pool.mark(pool.eng.memset(reset.rearrange("p (c n) -> p c n", n=HG_CHUNK)[:, :, 0:1], 0.0))
        f_at, k_at = [], []

        for i in range(2):
            def read(t, p, i=i):
                n = 2 * i + t
                src = self.bank[t][:].rearrange("p (f n) -> p f n", f=2)
                p1 = self.a(bc[:, 2 * n:2 * n + 2], src, ACT.Sigmoid, p)
                p2 = self.bank_free[t] = self.a(kk[:, 2 * n:2 * n + 2], src, ACT.Sigmoid, p, scale=-1.0)
                for f in range(2):
                    h = 2 * n + f
                    lb, om = self.lbs[:, 0, h:h + 1], self.lbs[:, 1, h:h + 1]
                    f_at.append(self.ts(bc[:, h], bc[:, h], om, lb, ALU.mult, ALU.add, p1, self.lb_at))
                    k_at.append(self.ts(kk[:, h], kk[:, h], om, None, ALU.mult, None, p2))
            self.chunk(read, feature_major=True)
        for i in range(2):
            def read(t, p, i=i):
                n = 2 * i + t
                self.q_at = self.bank_free[t] = self.a(
                    qq[:, 2 * n:2 * n + 2], self.bank[t][:].rearrange("p (f n) -> p f n", f=2), ACT.Silu, p)
            self.chunk(read, feature_major=True)
        flat = self.area(0, H * T)
        big = float(2.0 ** 60)
        p = self.ts(tiny, flat, float(2.0 ** -60), big, ALU.is_lt, ALU.mult, *f_at)
        p = self.ts(flat, flat, MIN_GATE, None, ALU.max, None, p)
        p = self.stt(flat, tiny, 1.0, flat, ALU.max, ALU.mult, p)
        p = self.a(flat, flat, ACT.Ln, p)
        p = self.stt(flat, tiny, -60.0 * float(np.log(2.0)) / big, flat, ALU.mult, ALU.add, p)
        self.dve.wait(p, reset_set)
        p = dve.mark(dve.eng.tensor_tensor_scan(flat, reset, flat, 0.0, ALU.mult, ALU.add))
        b_at = p
        pool.wait(b_at)

        state = {"x_free": [None, None], "pt_free": None, "o": {}}

        def scores_step(level, grp):
            hs = slice(4 * grp, 4 * grp + 4)
            n = state["n"] = state.get("n", -1) + 1
            xb = xx[:, n % 2]
            m = 2 ** (level - 1) if level else 0
            if level == 0:
                p = self.q_at
                dve.wait(*k_at)
                ready = self.diag_ready
            elif level <= 7:
                nb = T // (2 * m)
                half = lambda a, j: a.rearrange("p h (b u m) -> p (h b) u m", u=2, m=m)[:, :, j, :]
                B, X, K, Q = bc[:, hs], xb, kk[:, hs], qq[:, hs]
                ref = half(B, 0)[:, :, m - 1:m].to_broadcast([P, 4 * nb, m])
                p = self.tt(half(X, 0), ref, half(B, 0), ALU.subtract, b_at, state["x_free"][n % 2])
                if level < 7:
                    p = self.tt(half(X, 1), half(B, 1), ref, ALU.subtract)
                    p = self.a(X, X, ACT.Exp, p)
                else:
                    self.a(half(X, 0), half(X, 0), ACT.Exp, p)
                    p = self.a(half(X, 1), half(B, 1), ACT.Exp)
                self.tt(half(X, 0), half(X, 0), half(K, 0), ALU.mult, p, *k_at)
                ready = self.tt(half(X, 1), half(X, 1), half(Q, 1), ALU.mult, self.q_at)
            else:
                B, X, K, Q = bc[:, hs], xb, kk[:, hs], qq[:, hs]
                C = HG_CHUNK
                end = lambda c: B[:, :, (c + 1) * C - 1:(c + 1) * C].to_broadcast([P, 4, C])
                ch = lambda a, c: a[:, :, c * C:(c + 1) * C]
                p0 = self.tt(ch(X, 0), end(0), ch(B, 0), ALU.subtract, state["x_free"][n % 2])
                self.tt(ch(X, 0), ch(X, 0), end(1), ALU.add, p0)
                self.tt(ch(X, 1), end(1), ch(B, 1), ALU.subtract)
                p = self.tt(ch(X, 3), ch(B, 3), end(2), ALU.add)
                self.a(X[:, :, 0:2 * C], X[:, :, 0:2 * C], ACT.Exp, p)
                self.a(ch(X, 2), ch(B, 2), ACT.Exp)
                p = self.a(ch(X, 3), ch(X, 3), ACT.Exp)
                self.tt(X[:, :, 0:P], X[:, :, 0:P], K[:, :, 0:P], ALU.mult, p)
                ready = self.tt(X[:, :, P:T], X[:, :, P:T], Q[:, :, P:T], ALU.mult)
            for tile in range(NT if level <= 7 else 1):
                a = 2 * (n % 2) + tile
                pe.wait(ready, self.acc_free[a], *(k_at + [self.q_at] if level == 0 else []))
                for h in range(4):
                    o = self.acc[a][:, h * P:(h + 1) * P]
                    ts = slice(tile * P, (tile + 1) * P)
                    if level == 0:
                        lhs, rhs = kk[:, 4 * grp + h, ts], qq[:, 4 * grp + h, ts]
                    elif level <= 7:
                        lhs = rhs = xb[:, h, ts]
                    else:
                        lhs, rhs = xb[:, h, 0:P], xb[:, h, P:T]
                    p = self.mm(o, lhs, rhs)
                if level <= 7:
                    mask = self.masks[:, level, :].unsqueeze(1).to_broadcast([P, 4, P])
                    self.dve.wait(p, state["pt_zero"])
                    self.acc_free[a] = dve.mark(dve.eng.copy_predicated(
                        pt[:, tile], mask, self.acc[a][:].rearrange("p (h n) -> p h n", h=4)))
                    state["pt_at"] = self.acc_free[a]
                else:
                    self.acc_free[a] = state["cross_at"] = self.a(
                        pt[:, 2], self.acc[a][:].rearrange("p (h n) -> p h n", h=4), ACT.Copy, p,
                        state["pt_free"])
            state["x_free"][n % 2] = p

        def start_group(grp):
            pool.wait(state["pt_free"], b_at)
            state["pt_zero"] = pool.mark(pool.eng.memset(pt[:, 0:2], 0.0))

        def values(grp):
            for t in range(NT):
                pe.wait(state["pt_at"], state["cross_at"], self.v_at, self.bank_free[t])
                for h in range(4):
                    hc = slice((4 * grp + h) * P, (4 * grp + h + 1) * P)
                    o = self.bank[t][:, h * P:(h + 1) * P]
                    if t == 0:
                        p = self.mm(o, pt[:, 0, h], v[:, 0, hc])
                    else:
                        self.mm(o, pt[:, 1, h], v[:, 1, hc], start=True, stop=False)
                        p = self.mm(o, pt[:, 2, h], v[:, 0, hc], start=False, stop=True)
                state["pt_free"] = p
                r, q = self.head_rms(t, self.bank[t][:], 4, P, p, slot=t)
                o = self.out_hg(grp, t)
                o3 = o.rearrange("p (h d) -> p h d", h=4)
                q = self.tt(o3, self.bank[t][:].rearrange("p (h d) -> p h d", h=4),
                            r.unsqueeze(2).to_broadcast([P, 4, P]), ALU.mult, q, p)
                self.bank_free[t] = self.rms_free[t] = q
                state["o"][grp, t] = self.tt(o3, o3, self.og.unsqueeze(1).to_broadcast([P, 4, P]), ALU.mult, q)

        self.diag_ready = None
        steps = [(lv, grp) for grp in range(2) for lv in (0, 1, 2, 3, 4, 5, 6, 7, 8)]

        def some(k):
            for _ in range(k):
                if steps:
                    lv, grp = steps.pop(0)
                    if lv == 0:
                        if grp == 1:
                            values(0)
                        start_group(grp)
                    scores_step(lv, grp)

        for i in range(2):
            def read(t, p, i=i):
                self.v_at = self.bank_free[t] = self.a(v[:, t, i * CW:(i + 1) * CW], self.bank[t][:], ACT.Copy, p)
                some(2)
            self.chunk(read)
        for i in range(2):
            def read(t, p, i=i):
                self.g_at = self.bank_free[t] = self.a(g[:, t, i * CW:(i + 1) * CW], self.bank[t][:],
                                                       ACT.Silu, p)
                some(3)
            self.chunk(read)
        some(99)
        values(1)
        o_at = []
        for t in range(NT):
            for grp in range(2):
                o = self.out_hg(grp, t)
                p = self.tt(o, o, g[:, t, grp * CW:(grp + 1) * CW], ALU.mult, state["o"][grp, t], self.g_at)
            o_at.append(p)
        self.to_xt(lambda t, k: self.out_hg(k // 4, t)[:, (k % 4) * P:(k % 4 + 1) * P], ready=o_at)
        self.out_projection()

    def out_hg(self, grp, t):
        return self.area(4096, 2, NT, CW)[:, grp, t]

    KV_T, KV_V, KV_CT, KV_CV, KV_CB = 0, 2048, 3072, 3136, 4160

    def kv_chunks(self):
        w = self.t["w_kv_2"]
        return [(self.kv_pair_src(w), CW)] + [(self.mat_src(w, c * CW), CW) for c in (1, 2)]

    def kv(self):
        t_ = self.t
        kt = self.area(self.KV_T, 2, GROUPS, T)
        vv = self.area(self.KV_V, 2, NT, GROUPS * DH)
        kct = self.area(self.KV_CT, GROUPS, NB_CMP)
        vcb = self.area(self.KV_CV, 2, CW)
        cb = self.area(self.KV_CB, NT, NSA_HEADS, NB_CMP)
        w1 = self.area(4672, CMP_BLOCK, P)
        kv0 = self.area(8768, GROUPS, T)
        blk = [self.area(9792, GROUPS, T), self.area(10816, GROUPS, T)]
        dup = self.area(11840, 2, GROUPS, 2, DH)
        w2 = self.area(12864, 2, DH)
        hid = self.area(12992, 2, GROUPS * NC_CMP + 4)
        kc = self.area(13120, GROUPS, 2, DH)
        vc = self.area(13632, GROUPS, DH)
        relb = self.area(13888, NSA_HEADS)
        pe, act, dve, pool = self.pe, self.act, self.dve, self.pool
        act.wait(*self.x_ready)
        load = lambda d, s_: self.arena_in.mark(act.eng.dma_start(d, s_))
        load(w1[0:DH], t_["cmp_w1_k_2"].rearrange("(j d) h -> d j h", d=DH))
        load(w1[DH:P], t_["cmp_w1_v_2"].rearrange("(j d) h -> d j h", d=DH))
        load(w2[:, 0], t_["cmp_w2_k_2"])
        load(w2[:, 1], t_["cmp_w2_v_2"])
        load(relb[0:N_BUCKETS], t_["rel_bias_2"])
        oh = self.area(9792, 2, REL_W)
        here = load(oh[0:REL_ROWS], t_["c_rel"].rearrange("a r w -> r a w"))
        pool.wait(*self.x_ready)
        pool.wait(pool.mark(pool.eng.memset(relb[N_BUCKETS:REL_ROWS], NEG)))
        pool.wait(pool.mark(pool.eng.memset(vcb, 0.0)))
        set_at = pool.mark(pool.eng.memset(kct, 0.0))
        self.to_xt(self.x_tile, gain=G_KV, normed=True, ready=self.x_ready)

        rb = relb[0:REL_ROWS]
        p = self.mm(self.acc[0][0:NSA_HEADS, :], rb, oh[0:REL_ROWS, 1], here, set_at, self.acc_free[0])
        rows = self.area(8768, REL_W)
        p = self.acc_free[0] = self.a(rows[0:NSA_HEADS], self.acc[0][0:NSA_HEADS, :], ACT.Copy, p)
        n = NSA_HEADS * REL_W
        scr = self.nc.dram_tensor("bias_rows", (P, NSA_HEADS, REL_W), F32, kind="Internal").ap()
        act.wait(p)
        r_ap = rows[0:NSA_HEADS].unsqueeze(1).to_broadcast([NSA_HEADS, P, REL_W])
        wrote = self.scratch.mark(act.eng.dma_start(scr.rearrange("c h w -> h c w"), r_ap))
        pe.wait(self.acc_free[1])
        for t in range(NT):
            for b in range(NB_CMP):
                first = T + t * P - CMP_STRIDE * b - (CMP_BLOCK - 1) if b < NC_CMP else 0
                o = self.acc[1][:].rearrange("p (t h n) -> p t n h", t=NT, h=NSA_HEADS)[:, t, b]
                p = self.mm(o, oh[0:REL_ROWS, 0, first:first + P], rb)
        self.acc_free[1] = self.a(cb, self.acc[1][:].rearrange("p (t h n) -> p t h n", t=NT, h=NSA_HEADS),
                                  ACT.Copy, p)
        bias_done = p

        def read0(t, p):
            self.kv0_at = self.bank_free[t] = self.a(
                kv0[:, 2 * t:2 * t + 2], self.bank[t][:].rearrange("p (f n) -> p f n", f=2), ACT.Copy, p, wrote)
        self.chunk(read0, feature_major=True)

        blk_at = []
        for j in range(2):
            pe_col = self.gains[:, G_PE + 16 * j:G_PE + 16 * j + 16].unsqueeze(1).to_broadcast(
                [P, GROUPS * T // 16, 16])
            blk_at.append(self.tt(blk[j].rearrange("p g (n j) -> p (g n) j", j=16),
                                  kv0.rearrange("p g (n j) -> p (g n) j", j=16), pe_col, ALU.add,
                                  self.kv0_at, bias_done))
        todo = []

        def branch(br):
            def read(t, p):
                while todo:
                    todo.pop(0)()
                self.dve.wait(self.dup_free[t], bias_done)
                self.v_pts.append(self.a(vv[:, br, t], self.bank[t][:, GROUPS * DH:CW], ACT.Copy, p))
                n = self.normed_heads(t, p, dup[:, t], dup=2, width=GROUPS * DH)

                def later():
                    self.k_pts.append(self.turn_heads(
                        t, lambda j: dup[:, t, j].rearrange("p a d -> p (a d)"),
                        kt[:, br, :, t * P:(t + 1) * P], G_KN + 1 + br, n))
                    self.dup_free[t] = self.turned_at
                todo.append(later)
            return read
        self.dup_free, self.v_pts, self.k_pts = [None, None], [], []
        for br in range(2):
            self.chunk(branch(br))
        while todo:
            todo.pop(0)()

        hid_at = []
        for kv in range(2):
            rows_ = slice(kv * DH, (kv + 1) * DH)
            o = self.acc[2 + kv][:, 0:GROUPS * NC_CMP]
            pe.wait(*blk_at, here, self.acc_free[2 + kv])
            for j in range(CMP_BLOCK):
                b = blk[j // 16].rearrange("p g (n j) -> p g n j", j=16)
                n0 = j // 16
                p = self.mm(o.rearrange("p (g n) -> p g n", g=GROUPS), w1[rows_, j],
                            b[rows_, :, n0:n0 + NC_CMP, j % 16], start=(j == 0), stop=(j == CMP_BLOCK - 1))
            self.acc_free[2 + kv] = self.a(hid[:, kv, 0:GROUPS * NC_CMP], o, ACT.Gelu_apprx_tanh, p)
            hid_at.append(self.acc_free[2 + kv])
        out = self.acc[0]
        pe.wait(*hid_at, self.acc_free[0])
        for kv in range(2):
            for g in range(GROUPS):
                i = kv * GROUPS + g
                p = self.mm(out[0:NC_CMP, i * DH:(i + 1) * DH], hid[:, kv, g * NC_CMP:(g + 1) * NC_CMP], w2[:, kv])
        n = NC_CMP
        ss, ms, r = (self.small[0:n, 0, j, 0:GROUPS] for j in range(3))
        k3 = out[0:n, 0:GROUPS * DH].rearrange("p (g d) -> p g d", g=GROUPS)
        sq = self.sq_junk[0:n, 0:GROUPS * DH].rearrange("p (g d) -> p g d", g=GROUPS)
        vc_at = self.a(vc[0:n], out[0:n, GROUPS * DH:CW].rearrange("p (g d) -> p g d", g=GROUPS), ACT.Copy, p)
        q = self.a(sq, k3, ACT.Square, p, self.sq_free)
        q = self.red(ss, sq, ALU.add, q, self.rms_free[0])
        self.sq_free = q
        q = self.ts(ms, ss, 1.0 / DH, EPS, ALU.mult, ALU.add, q)
        dve.wait(q)
        q = dve.mark(dve.eng.reciprocal(ss, ms))
        q = self.a(r, ss, ACT.Sqrt, q)
        for j in range(2):
            q = self.tt(kc[0:n, :, j], k3, r.unsqueeze(2).to_broadcast([n, GROUPS, DH]), ALU.mult, q, p)
        self.rms_free[0] = q
        self.acc_free[0] = q
        pe.wait(q, self.tr_free[0])
        for g in range(GROUPS):
            ins = pe.eng.transpose(self.tr[0][:, g * NB_CMP:g * NB_CMP + n],
                                   kc[0:n, g].rearrange("p a d -> p (a d)"), self.ident[0:n, 0:n])
        p = pe.mark(ins)
        self.tr_free[0] = self.kct_at = self.a(
            kct[:, :, 0:n], self.tr[0][:, 0:GROUPS * NB_CMP].rearrange("p (g n) -> p g n", g=GROUPS)[:, :, 0:n],
            ACT.Copy, p, set_at, scale=self.gains[:, G_KN:G_KN + 1])
        act.wait(vc_at, set_at)
        for h in range(NSA_HEADS):
            row, col = (h % 8) * NB_CMP, (h % 8) * DH
            self.vcb_at = self.arena_in.mark(act.eng.dma_start(
                vcb[row:row + n, h // 8, col:col + DH], vc[0:n, h * GROUPS // NSA_HEADS]))
        tb = self.area(4672, NSA_HEADS, T)
        act.wait(*hid_at, wrote)
        src = bass.AP(tensor=scr.tensor, offset=scr.offset + P - 1,
                      ap=[[NSA_HEADS * REL_W - 1, P], [REL_W, NSA_HEADS], [1, T]])
        self.tb_at = self.scratch.mark(act.eng.dma_start(tb, src))

    def nsa_chunks(self):
        w = self.t["attn_w_q_2"][0]
        return ([(self.mat_src(w, 0), CW), (self.mat_src(w, CW), CW), (self.mat_src(w, D, 3 * NSA_HEADS), 3 * NSA_HEADS)]
                + [(self.mat_src(self.t["attn_w_o_2"][0], c * CW), CW) for c in range(D // CW)])

    def nsa(self):
        H = NSA_HEADS
        assert T // 64 <= 16 and T <= 512
        kt = self.area(self.KV_T, 2, GROUPS, T)
        vv = self.area(self.KV_V, 2, NT, GROUPS * DH)
        kct = self.area(self.KV_CT, GROUPS, NB_CMP)
        vcb = self.area(self.KV_CV, 2, CW)
        cb = self.area(self.KV_CB, NT, H, NB_CMP)
        tb = self.area(4672, H, T)
        qt = self.area(8768, KT, T)
        tmp = self.area(10816, NT, D)
        s_buf = self.area(12864, 2, 2, T)
        gates = self.area(13888, NT, H, 3)
        nm, den = self.area(13984, NT, 2, H), self.area(14048, NT, 2, H)
        coef = self.area(14112, NT, 2, H)
        pt = self.xg
        pe, act, dve = self.pe, self.act, self.dve
        self.to_xt(self.x_tile, gain=G_MIX + 8, normed=True, ready=self.x_ready)
        g_at = self.ts(self.gains[:, G_NSAQ:G_NSAQ + 1], self.gains[:, G_NSAQ:G_NSAQ + 1], DH ** -0.5, None,
                       ALU.mult, None)
        act.wait(g_at)
        todo, q_pts = [], []
        for i in range(2):
            def read(t, p, i=i):
                while todo:
                    todo.pop(0)()
                n = self.normed_heads(t, p, tmp[:, t, i * CW:(i + 1) * CW])

                def later():
                    q_pts.append(self.turn_heads(
                        t, lambda j: tmp[:, t, i * CW + j * P:i * CW + (j + 1) * P],
                        qt[:, 4 * i:4 * i + 4, t * P:(t + 1) * P], G_NSAQ, n))
                todo.append(later)
            self.chunk(read)

        def read(t, p):
            while todo:
                todo.pop(0)()
            self.gates_at = self.bank_free[t] = self.a(
                gates[:, t].rearrange("p h b -> p (h b)"), self.bank[t][:, 0:3 * H], ACT.Sigmoid, p)
        self.chunk(read, w=3 * H)
        turned_q = self.turned_at

        o_at = {}
        self.kv_ready = [*self.k_pts, *self.v_pts, self.kct_at, self.vcb_at, self.tb_at]
        for t in range(NT):
            sc = self.area(12864, H, NB_CMP)
            mx, sm = self.area(13120, H), self.area(13136, H)
            for odd in range(2):
                pe.wait(self.bank_free[odd], *q_pts, self.kct_at)
                rows = slice(DH * odd, DH * odd + DH)
                for i in range(H // 2):
                    h = 2 * i + odd
                    p = self.mm(self.bank[odd][:, i * NB_CMP:(i + 1) * NB_CMP], qt[rows, h // 2, t * P:(t + 1) * P],
                                kct[rows, h * GROUPS // H])
                v4 = lambda a: a.rearrange("p (i o) n -> p i o n", o=2)[:, :, odd]
                q = self.tt(v4(sc), self.bank[odd][:, 0:H // 2 * NB_CMP].rearrange("p (i n) -> p i n", i=H // 2),
                            v4(cb[:, t]), ALU.add, p, self.cmp_free)
                self.bank_free[odd] = q
            q = self.red(mx, sc, ALU.max, q)
            q = self.tt(sc, sc, mx.unsqueeze(2).to_broadcast([P, H, NB_CMP]), ALU.subtract, q)
            q = self.a(sc, sc, ACT.Exp, q)
            q = self.red(sm, sc, ALU.add, q)
            dve.wait(q)
            q = dve.mark(dve.eng.reciprocal(sm, sm))
            q = self.stt(sm, sm, self.rowmask[:, t:t + 1], gates[:, t, :, 0], ALU.mult, ALU.mult, q, self.gates_at)
            q = self.tt(sc, sc, sm.unsqueeze(2).to_broadcast([P, H, NB_CMP]), ALU.mult, q)
            for half in range(2):
                pe.wait(q, self.tr_free[half])
                p = pe.mark(pe.eng.transpose(self.tr[half][:, 0:P],
                                             sc[:, 8 * half:8 * half + 8].rearrange("p h n -> p (h n)"), self.ident[:]))
                c = self.tr_free[half] = self.a(pt[:, half, 0:P], self.tr[half][:, 0:P], ACT.Copy, p, *self.xg_free)
                self.cmp_free = p
                pe.wait(self.vcb_at, self.acc_free[half])
                p = self.mm(self.acc[half][:], pt[:, half, 0:P], vcb[:, half], c)
                self.xg_free[half] = p
                self.acc_free[half] = o_at[t, half] = self.a(
                    tmp[:, t, half * CW:(half + 1) * CW], self.acc[half][:], ACT.Copy, p, turned_q)

        steps = [(h, t) for h4 in range(H // 4) for t in range(NT) for h in range(4 * h4, 4 * h4 + 4)]
        st = {}
        ob = self.silu[:].rearrange("p a b -> p (a b)")

        def scores(i):
            h, t = steps[i]
            rows, n, g = slice(DH * (h % 2), DH * (h % 2) + DH), (t + 1) * P, h * GROUPS // H
            pe.wait(self.bank_free[i % 2], *q_pts, *self.k_pts)
            for br in range(2):
                p = self.mm(self.bank[i % 2][:, br * n:(br + 1) * n], qt[rows, h // 2, t * P:(t + 1) * P],
                            kt[rows, br, g, 0:n])
            s = s_buf[:, i % 2, :, 0:n]
            bias = tb[:, h, T - n:T].unsqueeze(1).to_broadcast([P, 2, n])
            p = self.bank_free[i % 2] = self.tt(
                s, self.bank[i % 2][:, 0:2 * n].rearrange("p (b n) -> p b n", b=2), bias, ALU.add,
                p, self.tb_at, st.get(("turned", i - 2)), self.cmp_free)
            p = self.red(nm[:, t, :, h], s, ALU.max, p, negate=True)
            for br in range(2):
                q = self.a(s[:, br], s[:, br], ACT.Exp, p, bias=nm[:, t, br, h:h + 1],
                           accum_out=den[:, t, br, h:h + 1])
            st["exp", i] = q

        def turn(i):
            h, t = steps[i]
            n = (t + 1) * P
            pe.wait(st["exp", i], self.tr_free[i % 2])
            for br in range(2):
                for b in range(t + 1):
                    ins = pe.eng.transpose(self.tr[i % 2][:, br * n + b * P:br * n + (b + 1) * P],
                                           s_buf[:, i % 2, br, b * P:(b + 1) * P], self.ident[:])
            p = st["turned", i] = pe.mark(ins)
            st["pt", i] = self.tr_free[i % 2] = self.a(pt[:, i % 2, 0:2 * n], self.tr[i % 2][:, 0:2 * n], ACT.Copy, p,
                                                       st.get(("pv", i - 2)), *self.xg_free)

        def values(i):
            h, t = steps[i]
            n, g, q4 = (t + 1) * P, h * GROUPS // H, i // 4
            a = q4 % 2 + 2
            pe.wait(st["pt", i], self.acc_free[a], *self.v_pts)
            for br in range(2):
                for b in range(t + 1):
                    c = (br * 4 + h % 4) * DH
                    p = self.mm(self.acc[a][:, c:c + DH], pt[:, i % 2, br * n + b * P:br * n + (b + 1) * P],
                                vv[:, br, b, g * DH:(g + 1) * DH], start=(b == 0), stop=(b == t))
            st["pv", i] = p
            if i % 4 == 3:
                hs = slice(h - 3, h + 1)
                dve.wait(st["exp", i])
                q = dve.mark(dve.eng.reciprocal(den[:, t, :, hs], den[:, t, :, hs]))
                gg = gates[:, t, hs, 1:3].rearrange("p h b -> p b h")
                q = self.tt(coef[:, t, :, hs], den[:, t, :, hs], gg, ALU.mult, q)
                o4 = ob.rearrange("p (b h d) -> p b h d", b=2, h=4)
                q = self.tt(o4, self.acc[a][:].rearrange("p (b h d) -> p b h d", b=2, h=4),
                            coef[:, t, :, hs].unsqueeze(3).to_broadcast([P, 2, 4, DH]), ALU.mult, q, p)
                self.acc_free[a] = q
                cols = tmp[:, t, (h - 3) * DH:(h + 1) * DH]
                q = self.tt(cols, cols, ob[:, 0:FC], ALU.add, q, o_at[t, (h - 3) // 8])
                st["o", t] = self.tt(cols, cols, ob[:, FC:], ALU.add, q)

        for i in range(len(steps) + 2):
            if i < len(steps):
                scores(i)
            if 1 <= i <= len(steps):
                turn(i - 1)
            if i >= 2:
                values(i - 2)
        self.xg_free = [p_ for p_ in (st["pv", len(steps) - 2], st["pv", len(steps) - 1])]
        self.to_xt(lambda t, k: tmp[:, t, k * P:(k + 1) * P], ready=[st["o", 0], st["o", 1]])
        self.out_projection()

    def begin(self, stages):
        nc, t, sp, act, pe, dve = self.nc, self.t, self.sp, self.act, self.pe, self.dve
        self.xg_free = [None, None]
        self.h_at_prev = [None, None]
        self.src_read = self.sq_free = self.cmp_free = None
        self.rms_free = [None, None]
        x = t["x"].rearrange("o (t p) d -> p (o t) d", p=P)
        rows = self.arena[:, 0:2 * P].rearrange("p (a n) -> p a n", a=2)
        put = self.consts_in

        def load(dst, src):
            return put.mark(act.eng.dma_start(dst, src))

        load(self.ident[:], t["c_ident"])
        flat = lambda a: a.rearrange("a (k n) -> (a k) n", n=P)
        load(rows[0:48, 0, :], t["norm_g"].rearrange("a b (k n) -> (a b k) n", n=P))
        load(rows[48:64, 0, :], flat(t["ffn1_norm_2"]))
        load(rows[64:80, 0, :], flat(t["mix_norm_2"]))
        load(rows[80:96, 0, :], flat(t["ffn2_norm_2"]))
        load(rows[96:104, 0, :], t["kv_norm_2"].rearrange("(k n) -> k n", n=P))
        load(rows[104:128, 0, :], t["conv_w_2"].rearrange("a b (k n) -> (a b k) n", n=P))
        load(rows[0:8, 1, :], flat(t["hg_lb_logits"]))
        for half in range(2):
            c = slice(half * DH, (half + 1) * DH)
            load(rows[8:9, 1, c], t["fox_q_norm_g"])
            load(rows[9:10, 1, c], t["fox_k_norm_g"])
            load(rows[10:11, 1, c], t["attn_q_norm_2"])
            load(rows[11:14, 1, c], t["k_norm_2"])
        load(rows[14:46, 1, 0:DH], t["cmp_pe_k_2"])
        load(rows[14:46, 1, DH:P], t["cmp_pe_v_2"])
        load(self.masks[:], t["c_masks"])
        load(self.rowmask[:], t["c_rowmask"])
        og = t["hg_out_norm_g"]
        load(self.og, bass.AP(tensor=og.tensor, offset=og.offset, ap=[[0, P], [1, P]]))
        last = load(self.x[:], x)
        self.x_ready = [last, last]
        self.par = 1
        for piece in range(2):
            self.pop_next(piece)
        self.par = 0
        pe.wait(last)
        pe.eng.transpose(self.tr[0][:, 0:P], rows[:, 0, :], self.ident[:])
        p = pe.mark(pe.eng.transpose(self.tr[0][:, P:G_ROWS], rows[0:G_ROWS - P, 1, :],
                                     self.ident[0:G_ROWS - P, 0:G_ROWS - P]))
        act.wait(p)
        self.gains_at = act.mark(act.eng.activation(self.gains[:], self.tr[0][:, 0:G_ROWS], ACT.Copy))
        dve.wait(self.gains_at)
        pe.wait(self.gains_at)
        logit = self.gains[:, G_LB:G_LB + KT]
        e, r, lb, om = self.small[:, 0, 0, 0:KT], self.small[:, 0, 1, 0:KT], self.lbs[:, 0], self.lbs[:, 1]
        p = self.tt(e, logit, logit, ALU.subtract, self.gains_at)
        p = self.a(e, e, ACT.Exp, p)
        dve.wait(p)
        p = dve.mark(dve.eng.reciprocal(r, e))
        p = self.tt(e, e, r, ALU.mult, p)
        p = self.tt(lb, e, e, ALU.subtract, p)
        self.lb_at = self.ts(om, lb, -1.0, 1.0, ALU.mult, ALU.add, p)

    def end(self):
        sp = self.sp
        sp.wait(*self.x_ready)
        out = self.t["out"].rearrange("o (t p) d -> p (o t) d", p=P)
        done = self.stored.mark(sp.eng.dma_start(out, self.x[:]))
        sp.wait(done)
        sp.flush()

    def chunks_of(self, stage):
        t = self.t
        kind = stage[0]
        if kind == "ffn":
            return [(self.ffn_src(stage[1], 0), CW)]
        return self.MIXER_CHUNKS[kind](self)

    MIXER_CHUNKS = {"conv": conv_chunks, "hgrn": hgrn_chunks, "fox": fox_chunks, "kv": kv_chunks,
                    "nsa": nsa_chunks}
    MIXERS = {"conv": conv, "hgrn": hgrn, "fox": fox, "kv": kv, "nsa": nsa}

    def run(self, stages):
        self.queue = [c for s in stages for c in self.chunks_of(s)]
        self.begin(stages)
        for s in stages:
            if s[0] == "ffn":
                self.ffn(*s[1:])
            else:
                self.MIXERS[s[0]](self)
        assert not self.queue, len(self.queue)
        self.end()


def rel_tables():
    n = np.arange(T)
    nf = np.maximum(n, 1).astype(np.float32)
    large = MAX_EXACT + (np.log(nf / np.float32(MAX_EXACT)) / np.float32(np.log(MAX_DISTANCE / MAX_EXACT))
                         * np.float32(N_BUCKETS - MAX_EXACT)).astype(np.int32)
    bucket = np.where(n < MAX_EXACT, n, np.minimum(large, N_BUCKETS - 1))
    tables = np.zeros((2, REL_ROWS, REL_W), np.float32)
    for which, rel in enumerate((np.arange(REL_W) - T, T - 1 - np.arange(REL_W))):
        row = np.where(rel < 0, N_BUCKETS, bucket[np.clip(rel, 0, T - 1)])
        tables[which, row, np.arange(REL_W)] = 1.0
    return tables


def constants():
    i = np.arange(P)
    s, t = i[:, None], i[None, :]
    masks = [s == t]
    m = 1
    while m < P:
        masks.append((s // (2 * m) == t // (2 * m)) & (s % (2 * m) < m) & (t % (2 * m) >= m))
        m *= 2
    causal = np.zeros((P, 2, P), np.float32)
    causal[:, 1] = np.where(t > s, NEG, 0.0)
    select = np.zeros((P, FOX_HEADS, P), np.float32)
    select[np.arange(FOX_HEADS), np.arange(FOX_HEADS)] = 1.0
    rowmask = np.ones((P, NT), np.float32)
    rowmask[:CMP_BLOCK - 1, 0] = 0.0
    return {
        "c_ident": np.eye(P, dtype=np.float32),
        "c_masks": np.stack(masks, 1).astype(np.int32),
        "c_upto": (s <= t).astype(np.float32),
        "c_causal": causal,
        "c_select": select,
        "c_rel": rel_tables(),
        "c_rowmask": rowmask,
    }


def build(nc, t, stages=None):
    with ExitStack() as stack:
        k = Kernel(nc, stack, t)
        if stages is None:
            stages = all_stages(t)
        k.run(stages)


def all_stages(t):
    f_in, f_out = t["ffn_w_in"], t["ffn_w_out"]
    i1, o1, i2, o2 = t["ffn1_w_in_2"], t["ffn1_w_out_2"], t["ffn2_w_in_2"], t["ffn2_w_out_2"]
    return [
        ("ffn", f_in[0, 0], f_out[0, 0], G_NORM),
        ("hgrn",),
        ("ffn", f_in[0, 1], f_out[0, 1], G_NORM + 16),
        ("ffn", f_in[1, 0], f_out[1, 0], G_NORM + 24),
        ("fox",),
        ("ffn", f_in[1, 1], f_out[1, 1], G_NORM + 40),
        ("ffn", i1[0], o1[0], G_FFN1),
        ("conv",),
        ("ffn", i2[0], o2[0], G_FFN2),
        ("kv",),
        ("ffn", i1[1], o1[1], G_FFN1 + 8),
        ("nsa",),
        ("ffn", i2[1], o2[1], G_FFN2 + 8),
    ]


NAMES = [
    "x", "norm_g", "ffn_w_in", "ffn_w_out", "hg_w_in", "hg_lb_logits", "hg_out_norm_g", "hg_w_out",
    "fox_w_in", "fox_b_f", "fox_q_norm_g", "fox_k_norm_g", "fox_w_out", "ffn1_norm_2", "ffn1_w_in_2",
    "ffn1_w_out_2", "mix_norm_2", "ffn2_norm_2", "ffn2_w_in_2", "ffn2_w_out_2", "conv_w_in_2",
    "conv_w_2", "conv_w_out_2", "attn_w_q_2", "attn_q_norm_2", "attn_w_o_2", "kv_norm_2", "w_kv_2",
    "k_norm_2", "cmp_pe_k_2", "cmp_pe_v_2", "cmp_w1_k_2", "cmp_w2_k_2", "cmp_w1_v_2", "cmp_w2_v_2",
    "rel_bias_2",
]


def kernel(**inputs):
    import concourse.bacc as bacc
    from concourse.bass_utils import run_bass_kernel_spmd

    nc = bacc.Bacc("TRN2", target_bir_lowering=False, num_devices=1)
    arrays = {name: np.ascontiguousarray(inputs[name]) for name in NAMES}
    arrays.update(constants())
    t = {name: nc.dram_tensor(name, a.shape, mybir.dt.from_np(a.dtype), kind="ExternalInput").ap()
         for name, a in arrays.items()}
    t["out"] = nc.dram_tensor("out", (1, T, D), F32, kind="ExternalOutput").ap()
    build(nc, t)
    r = run_bass_kernel_spmd(nc, [arrays], core_ids=[0])
    return r.results[0]["out"]
```

```python
from contextlib import ExitStack

import numpy as np

import concourse.bass as bass
import concourse.mybir as mybir
from concourse.alu_op_type import AluOpType as ALU

ACT = mybir.ActivationFunctionType
AX = mybir.AxisListType
F32 = mybir.dt.float32
F32R = mybir.dt.float32r
I32 = mybir.dt.int32

P = 128
D = 1024
KT = D // P
T = 256
NT = T // P
D_FF = 2816
FC = 256
NCH = D_FF // FC
CW = 512
EPS = 1e-6
NEG = -1e30
MIN_GATE = 1e-30

HG_HEADS = 8
FOX_HEADS = NSA_HEADS = 16
DH = 64
GROUPS = 4
CMP_BLOCK, CMP_STRIDE = 32, 16
NC_CMP = (T - CMP_BLOCK) // CMP_STRIDE + 1
NB_CMP = CMP_STRIDE
N_BUCKETS, MAX_EXACT, MAX_DISTANCE = 32, 16, 4096
REL_ROWS = N_BUCKETS + 1
REL_W = 512
ARENA = 14336

G_NORM = 0
G_FFN1, G_MIX, G_FFN2 = 48, 64, 80
G_KV = 96
G_CONV = 104
G_LB = 128
G_FOXQ, G_FOXK, G_NSAQ, G_KN = 136, 137, 138, 139
G_PE = 142
G_ROWS = 174


class Loop:

    def __init__(self, n, per):
        self.n, self.per, self.var = n, per, None


class Point:

    def __init__(self, counter, k, loop):
        self.counter, self.k, self.loop = counter, k, loop


class Counter:

    def __init__(self, prog, name, step=1):
        self.prog, self.step, self.n = prog, step, 0
        self.sem = prog.stack.enter_context(prog.nc.semaphore(name))
        self.name = name
        prog.counters.append(self)

    def mark(self, ins):
        ins.then_inc(self.sem, self.step)
        self.n += 1
        return Point(self, self.n, self.prog.loop)


class Engine:

    def __init__(self, prog, eng, name):
        self.prog, self.queue, self.done = prog, eng, Counter(prog, "done_" + name)
        self.met, self.pending = {}, {}

    def mark(self, ins):
        return self.done.mark(ins)

    def wait(self, *points, fixed=False):
        cur = self.prog.loop
        for p in points:
            if p is None:
                continue
            c, k = p.counter, p.k
            if p.loop is not None and p.loop is not cur:
                k += (p.loop.n - 1) * p.loop.per.get(c.name, 0)
            moves = cur is not None and not fixed and cur.per.get(c.name, 0) > 0
            if not moves and self.met.get(c.name, 0) >= k:
                continue
            before = self.pending.get(c)
            assert before is None or before[0] == moves, c.name
            self.pending[c] = (moves, max(k, before[1] if before else 0))

    def flush(self):
        return self.eng

    @property
    def eng(self):
        cur = self.prog.loop
        for c, (moves, k) in self.pending.items():
            if moves:
                self.queue.wait_ge(c.sem, (cur.var * cur.per[c.name] + k) * c.step)
            else:
                self.queue.wait_ge(c.sem, k * c.step)
                self.met[c.name] = k
        self.pending = {}
        return self.queue


class Program:
    def __init__(self, nc, stack):
        self.nc, self.stack, self.loop, self.counters = nc, stack, None, []
        self.pe = Engine(self, nc.tensor, "pe")
        self.act = Engine(self, nc.scalar, "act")
        self.dve = Engine(self, nc.vector, "dve")
        self.sp = Engine(self, nc.sync, "sp")
        self.pool = Engine(self, nc.gpsimd, "pool")

    def repeat(self, n, per, body):
        et = mybir.EngineType
        start = {c.name: c.n for c in self.counters}
        self.loop = Loop(n, per)
        with self.nc.Fori(0, n, engines=(et.Activation, et.PE, et.DVE, et.SP)) as i:
            self.loop.var = i
            body(i)
        for c in self.counters:
            grown = c.n - start[c.name]
            assert grown == per.get(c.name, 0), (c.name, grown)
            c.n += (n - 1) * grown
        self.loop = None


class Kernel:
    def __init__(self, nc, stack, t):
        self.nc, self.stack, self.t = nc, stack, t
        g = self.g = Program(nc, stack)
        self.pe, self.act, self.dve, self.sp, self.pool = g.pe, g.act, g.dve, g.sp, g.pool
        sb = self.sb
        self.x = sb("x_tok", [P, NT, D])
        self.xt_hi = sb("xt_hi", [P, KT, T], F32R)
        self.xt_lo = sb("xt_lo", [P, KT, T], F32R)
        self.xg = sb("xt_full", [P, 2, CW])
        self.raw = sb("raw_in", [P, 2, KT // 2, CW])
        self.raw_out = sb("raw_out", [P, FC // P, D])
        self.w_hi = sb("w_hi", [P, 2, KT, CW], F32R)
        self.w_lo = sb("w_lo", [P, 2, KT, CW], F32R)
        self.wo_hi = sb("wo_hi", [P, FC // P, D], F32R)
        self.wo_lo = sb("wo_lo", [P, FC // P, D], F32R)
        self.silu = sb("silu", [P, NT, FC])
        self.h = sb("h_tok", [P, NT, FC])
        self.ht_hi = sb("ht_hi", [P, FC // P * NT, P], F32R)
        self.ht_lo = sb("ht_lo", [P, FC // P * NT, P], F32R)
        self.ident = sb("ident", [P, P])
        self.gains = sb("gains", [P, G_ROWS])
        self.rstd = sb("rstd", [P, NT])
        self.diag = sb("diag", [P, NT, P])
        self.sq_junk = sb("sq_junk", [P, CW])
        self.hn = sb("row_sums", [P, NT, 8])
        self.masks = sb("masks", [P, 8, P], I32)
        self.rowmask = sb("rowmask", [P, NT + 8])
        self.og = sb("hg_gain", [P, P])[:]
        self.lbs = sb("lower_bound", [P, 2, KT])
        self.arena = sb("arena", [P, ARENA])
        self.small = sb("small", [P, 2, 5, 16])
        self.bank = [self.ps(f"bank{t}", [P, CW]) for t in range(2)]
        self.acc = [self.ps(f"acc{i}", [P, CW]) for i in range(4)]
        self.tr = [self.ps(f"tr{i}", [P, CW]) for i in range(2)]
        self.landed = [Counter(g, f"landed_{n}", 16) for n in ("a", "b", "out")]
        self.consts_in = Counter(g, "consts_in", 16)
        self.arena_in = Counter(g, "arena_in", 16)
        self.rel_in = Counter(g, "rel_in", 16)
        self.scratch = Counter(g, "scratch", 16)
        self.stored = Counter(g, "stored", 16)
        self.split_hi = [None, None, None]
        self.split_lo = [None, None, None]
        self.used = [None, None]
        self.w_ready = [[None, None], [None, None]]
        self.used_out = None
        self.par = 0
        self.bank_free = [None, None]
        self.acc_free = [None] * 4
        self.tr_free = [None, None]
        self.queue = []
        self.tasks = []
        self.splits = []
        self.fill = None
        self.x_ready, self.x_half = [None, None], [[None, None], [None, None]]

    def sb(self, name, shape, dt=F32):
        return self.stack.enter_context(self.nc.sbuf_tensor(name, shape, dt))

    def ps(self, name, shape):
        return self.stack.enter_context(self.nc.psum_tensor(name, shape, F32))

    def area(self, at, *shape, parts=P):
        n = int(np.prod(shape))
        assert at + n <= ARENA
        v = self.arena[0:parts, at:at + n]
        if len(shape) == 2:
            v = v.rearrange("p (a b) -> p a b", a=shape[0])
        elif len(shape) == 3:
            v = v.rearrange("p (a b c) -> p a b c", a=shape[0], b=shape[1])
        elif len(shape) == 4:
            v = v.rearrange("p (a b c d) -> p a b c d", a=shape[0], b=shape[1], c=shape[2])
        return v

    def a(self, out, src, func, *after, **kw):
        self.act.wait(*after)
        return self.act.mark(self.act.eng.activation(out, src, func, **kw))

    def tt(self, out, x, y, op, *after):
        self.dve.wait(*after)
        return self.dve.mark(self.dve.eng.tensor_tensor(out, x, y, op))

    def ts(self, out, x, s1, s2, op0, op1, *after):
        self.dve.wait(*after)
        if op1 is None:
            return self.dve.mark(self.dve.eng.tensor_scalar(out, x, s1, None, op0))
        return self.dve.mark(self.dve.eng.tensor_scalar(out, x, s1, s2, op0, op1))

    def stt(self, out, x, s, y, op0, op1, *after):
        self.dve.wait(*after)
        return self.dve.mark(self.dve.eng.scalar_tensor_tensor(out, x, s, y, op0, op1))

    def red(self, out, x, op, *after, **kw):
        self.dve.wait(*after)
        return self.dve.mark(self.dve.eng.tensor_reduce(out, x, AX.X, op, **kw))

    def mm(self, out, lhs, rhs, *after, start=True, stop=True):
        self.pe.wait(*after)
        return self.pe.mark(self.pe.eng.matmul(out, lhs, rhs, start=start, stop=stop))

    def split_piece(self, s, dst_hi, dst_lo, raw, parts, free, by_tile=False):
        act, dve, sp = self.act, self.dve, self.sp
        sp.wait(self.split_lo[s])
        for to, src in parts:
            landed = self.landed[s].mark(sp.eng.dma_start(to(raw), src))

        def split(hi, lo, r):
            act.wait(landed, free)
            self.split_hi[s] = act.mark(act.eng.activation(hi, r, ACT.Copy))
            dve.wait(self.split_hi[s])
            self.split_lo[s] = dve.mark(dve.eng.tensor_tensor(lo, r, hi.bitcast(F32), ALU.subtract))

        n = raw.shape[1]
        if by_tile:
            return [lambda k=k: split(dst_hi[:, k], dst_lo[:, k], raw[:, k]) for k in range(n)]
        split(dst_hi, dst_lo, raw)

    def prefetch(self, piece, par, parts, w=CW):
        sl = (slice(None), par, slice(piece * KT // 2, (piece + 1) * KT // 2), slice(0, w))
        self.splits = self.split_piece(piece, self.w_hi[sl], self.w_lo[sl], self.raw[:, piece, :, 0:w], parts,
                                       self.used[par], by_tile=bool(self.fill)) or []

    def prefetch_out(self, src, by_tile=False):
        return self.split_piece(2, self.wo_hi[:], self.wo_lo[:], self.raw_out[:], [(lambda r: r, src)],
                                None if by_tile else self.used_out, by_tile)

    def ffn_src(self, w_in, c):
        v = w_in.rearrange("(k p) (g n) -> p k g n", p=P, g=2)
        if not isinstance(c, int):
            c = self.sp.queue.snap(c)
        return lambda piece: [
            (lambda r, g=g: r[:, :, g * FC:(g + 1) * FC],
             v[:, piece * KT // 2:(piece + 1) * KT // 2, g, bass.ds(c * FC, FC)]) for g in range(2)]

    def mat_src(self, w, c0, wd=CW):
        v = w.rearrange("(k p) n -> p k n", p=P)
        return lambda piece: [(lambda r: r, v[:, piece * KT // 2:(piece + 1) * KT // 2, c0:c0 + wd])]

    def kv_pair_src(self, w):
        v = w.rearrange("(k p) (b g d) -> p k b g d", p=P, b=6, g=GROUPS)
        return lambda piece: [
            (lambda r, b=b, k=k: r.rearrange("p k (g b d) -> p k b g d", g=GROUPS, b=2)[:, k, b],
             v[:, piece * KT // 2 + k, b]) for b in range(2) for k in range(KT // 2)]

    def product(self, par, t, w=CW, feature_major=False, b=None):
        pe = self.pe
        b = t if b is None else b
        if self.fill:
            self.fill()
        pe.wait(self.bank_free[b])
        out = self.bank[b]
        w_hi, w_lo = self.w_hi[:, par], self.w_lo[:, par]

        def operands(half):
            pe.wait(self.w_ready[par][half])
            for tile in ((0, 1) if feature_major else (t,)):
                pe.wait(*self.xt_ready[tile][2 * half:2 * half + 2], fixed=True)

        tok = slice(t * P, (t + 1) * P)
        for f in range(2 if feature_major else 1):
            c = slice((2 * t + f) * P, (2 * t + f + 1) * P)
            for k in range(KT):
                if self.fill and k:
                    self.fill()
                    if k % 2 and self.splits:
                        self.splits.pop(0)()
                if f == 0 and k % 4 == 0:
                    operands(k // 4)
                mm = pe.eng.matmul
                first, end = k == 0, k == KT - 1
                if feature_major:
                    o = out[:, f * T:(f + 1) * T]
                    mm(o, w_hi[:, k, c], self.xt_hi[:, k, :], start=first, stop=False)
                    mm(o, w_hi[:, k, c], self.xt_lo[:, k, :], start=False, stop=False)
                    last = mm(o, w_lo[:, k, c], self.xt_hi[:, k, :], start=False, stop=end)
                else:
                    o = out[:, 0:w]
                    mm(o, self.xt_hi[:, k, tok], w_hi[:, k, 0:w], start=first, stop=False)
                    mm(o, self.xt_hi[:, k, tok], w_lo[:, k, 0:w], start=False, stop=False)
                    last = mm(o, self.xt_lo[:, k, tok], w_hi[:, k, 0:w], start=False, stop=end)
        return pe.mark(last)

    def pop_next(self, piece):
        popped = bool(self.queue)
        if popped:
            src, w = self.queue[0]
            self.prefetch(piece, 1 - self.par, src(piece), w)
            if piece == 1:
                self.queue.pop(0)
        return popped

    def chunk(self, read, w=CW, feature_major=False, between=None, b=None):
        for t in range(2):
            popped = self.pop_next(t)
            point = self.product(self.par, t, w, feature_major, b)
            while self.splits:
                self.splits.pop(0)()
            if popped:
                self.w_ready[1 - self.par][t] = self.split_lo[t]
            if t == 0 and between:
                between()
            read(t, point)
        self.used[self.par] = point
        self.par = 1 - self.par

    def squares(self, t):
        for half in range(2):
            self.sq_at[t] = self.a(self.sq_junk[:], self.x[:, t, half * CW:(half + 1) * CW], ACT.Square,
                                   self.x_half[t][half], self.sq_junk_at, self.sq_free,
                                   accum_out=self.hn[:, t, half:half + 1])
            self.sq_junk_at = self.sq_at[t]

    def rms(self, t):
        sums = self.hn[:, t]
        q = self.ts(sums[:, 2:3], sums[:, 0:1], 1.0 / D, EPS, ALU.mult, ALU.add, self.sq_at[t])
        p = self.a(sums[:, 3:4], sums[:, 1:2], ACT.Sqrt, q, scale=1.0 / D, bias=sums[:, 2:3])
        self.dve.wait(p)
        return self.dve.mark(self.dve.eng.reciprocal(self.rstd[:, t:t + 1], sums[:, 3:4]))

    def norm(self, t):
        self.squares(t)
        return self.ts(self.diag[:, t, :], self.ident[:], self.rstd[:, t:t + 1], None, ALU.mult, None,
                       self.rms(t), self.diag_free[t])

    def to_xt(self, src, gain=None, normed=False, deferred=False, ready=None):
        pe, act, dve = self.pe, self.act, self.dve
        self.xt_ready = [[], []]
        free = self.used[1 - self.par]
        turned, scaled, hi_at = {}, {}, {}
        diag_at = [None, None]
        halves = range(2)
        place = lambda xt, t, half: xt[:, 4 * half:4 * half + 4, t * P:(t + 1) * P]
        if normed:
            self.a(self.hn[:, 0, 4:5], self.ident[:, 0:1], ACT.Sqrt, self.warm_at)
            ready = self.x_half

        def turn(t, half):
            pe.wait(ready[t][half], self.tr_free[half], diag_at[t])
            for k in range(4):
                lhs, o = src(t, 4 * half + k), self.tr[half][:, k * P:(k + 1) * P]
                if diag_at[t]:
                    ins = pe.eng.matmul(o, lhs, self.diag[:, t, :], start=True, stop=True)
                else:
                    ins = pe.eng.transpose(o, lhs, self.ident[:])
            self.src_read = turned[t, half] = pe.mark(ins)
            if diag_at[t]:
                self.diag_free[t] = self.src_read

        def scale(t, half):
            if gain is None:
                scaled[t, half] = self.tr[half][:].rearrange("p (k n) -> p k n", k=4), turned[t, half]
                return
            g = self.gains[:, gain + 4 * half:gain + 4 * half + 4].unsqueeze(2).to_broadcast([P, 4, P])
            o = self.xg[:, half, :].rearrange("p (k n) -> p k n", k=4)
            self.tr_free[half] = self.tt(o, self.tr[half][:].rearrange("p (k n) -> p k n", k=4), g, ALU.mult,
                                         turned[t, half], self.xg_free[half])
            scaled[t, half] = o, self.tr_free[half]

        def hi(t, half):
            v, at = scaled[t, half]
            hi_at[t, half] = self.a(place(self.xt_hi, t, half), v, ACT.Copy, at, free)

        def lo(t, half):
            v, at = scaled[t, half]
            h = place(self.xt_hi, t, half)
            p = self.tt(place(self.xt_lo, t, half), v, h.bitcast(F32), ALU.subtract, at, hi_at[t, half], free)
            if gain is not None:
                self.xg_free[half] = p
            else:
                self.tr_free[half] = p
            self.xt_ready[t] += [hi_at[t, half], p]

        for t in range(NT):
            if normed and not deferred and t == 0:
                diag_at[0] = self.norm(0)
            if normed and deferred:
                self.squares(t)
            for half in halves:
                turn(t, half)
            for half in halves:
                scale(t, half)
            if normed and not deferred and t == 0:
                diag_at[1] = self.norm(1)
            for half in halves:
                hi(t, half)
            for half in halves:
                lo(t, half)
        if normed and deferred:
            self.rstd_at = [self.rms(t) for t in range(NT)]
            self.warm_at = None

    def take_task(self):
        if self.tasks:
            self.tasks.pop(0)()

    def finish_tasks(self):
        self.fill = None
        while self.tasks:
            self.tasks.pop(0)()

    def x_tile(self, t, k):
        return self.x[:, t, k * P:(k + 1) * P]

    def ffn(self, w_in, w_out, gain, last=False):
        pe, act, dve = self.pe, self.act, self.dve
        self.to_xt(self.x_tile, gain=gain, normed=True, deferred=True)
        rstd_at = self.rstd_at
        w_out_v = w_out.rearrange("(c k p) n -> c p k n", p=P, k=FC // P)
        h_at = [None, None]
        state = {"turned": None}

        def read(t, point):
            act.wait(point)
            act.wait(rstd_at[t], fixed=True)
            act.wait(self.h_at[t])
            s = act.mark(act.eng.activation(self.silu[:, t, :], self.bank[t][:, 0:FC], ACT.Silu,
                                            scale=self.rstd[:, t:t + 1]))
            dve.wait(s, state["turned"])
            self.h_at[t] = dve.mark(dve.eng.scalar_tensor_tensor(
                self.h[:, t, :], self.bank[t][:, FC:2 * FC], self.rstd[:, t:t + 1], self.silu[:, t, :],
                ALU.mult, ALU.mult))
            self.bank_free[t] = self.h_at[t]

        def turn():
            pe.wait(*self.h_at, self.tr_free[0])
            for f in range(FC // P):
                for t in range(NT):
                    i = f * NT + t
                    ins = pe.eng.transpose(self.tr[0][:, i * P:(i + 1) * P],
                                           self.h[:, t, f * P:(f + 1) * P], self.ident[:])
            state["turned"] = pe.mark(ins)
            full = self.tr[0][:].rearrange("p (i n) -> p i n", n=P)
            act.wait(state["turned"], self.used_out)
            self.ht_hi_at = act.mark(act.eng.activation(self.ht_hi[:], full, ACT.Copy))
            dve.wait(self.ht_hi_at)
            self.ht_at = dve.mark(dve.eng.tensor_tensor(self.ht_lo[:], full, self.ht_hi[:].bitcast(F32),
                                                        ALU.subtract))
            self.tr_free[0] = self.ht_at

        def second(c, start, stop):
            pe.wait(self.ht_at, self.split_lo[2])
            for t in range(NT):
                for half in range(2):
                    a = 2 * t + half
                    if start:
                        pe.wait(self.acc_free[a])
                    cols = slice(half * CW, (half + 1) * CW)
                    for f in range(FC // P):
                        i = f * NT + t
                        mm = pe.eng.matmul
                        mm(self.acc[a][:], self.ht_hi[:, i, :], self.wo_hi[:, f, cols],
                           start=(start and f == 0), stop=False)
                        mm(self.acc[a][:], self.ht_hi[:, i, :], self.wo_lo[:, f, cols], start=False, stop=False)
                        ins = mm(self.acc[a][:], self.ht_lo[:, i, :], self.wo_hi[:, f, cols], start=False,
                                 stop=(stop and f == FC // P - 1))
                    if stop:
                        self.acc_at[a] = pe.mark(ins)
            self.used_out = self.acc_at[3] if stop else pe.mark(ins)

        def body(c, start=False):
            if not isinstance(c, int):
                c = self.sp.queue.snap(c)
            self.prefetch_out(w_out_v[c] if isinstance(c, int) else w_out_v[bass.ds(c, 1)].rearrange(
                "c p k n -> (c p) k n"))
            self.chunk(read, between=turn)
            second(c, start, False)

        self.acc_at = [None] * 4
        self.queue.insert(0, (self.ffn_src(w_in, 1), CW))
        self.h_at = list(self.h_at_prev)
        self.fill = self.take_task if self.tasks else None
        self.chunk(read)
        self.finish_tasks()
        self.queue.insert(0, (self.ffn_src(w_in, 2), CW))
        body(0, start=True)

        per = {"done_act": 2 * 6, "done_dve": 2 * 6, "done_pe": 2 * 4,
               "landed_a": 4, "landed_b": 4, "landed_out": 2}

        def two(i):
            for j in range(2):
                c = i * 2 + (1 + j)
                self.queue.insert(0, (self.ffn_src(w_in, c + 2), CW))
                body(c)

        self.g.repeat((NCH - 3) // 2, per, two)
        self.prefetch_out(w_out_v[NCH - 2])
        self.chunk(read, between=turn)
        split_last = self.prefetch_out(w_out_v[NCH - 1], by_tile=True)
        whole, ready = [self.ht_at, self.split_lo[2]], [None, None]
        for c in (NCH - 2, NCH - 1):
            for f in range(FC // P):
                pe.wait(*(whole if c == NCH - 2 else ready[f:f + 1]))
                for a in range(4):
                    t, cols = a // 2, slice(a % 2 * CW, (a % 2 + 1) * CW)
                    i, end = f * NT + t, c == NCH - 1 and f == 1
                    mm = pe.eng.matmul
                    mm(self.acc[a][:], self.ht_hi[:, i, :], self.wo_hi[:, f, cols], start=False, stop=False)
                    mm(self.acc[a][:], self.ht_hi[:, i, :], self.wo_lo[:, f, cols], start=False, stop=False)
                    ins = mm(self.acc[a][:], self.ht_lo[:, i, :], self.wo_hi[:, f, cols], start=False, stop=end)
                    if end:
                        self.acc_at[a] = pe.mark(ins)
                if c == NCH - 1:
                    continue
                read_at = pe.mark(ins)
                pe.wait(*self.h_at, self.tr_free[f])
                for t in range(NT):
                    ins = pe.eng.transpose(self.tr[f][:, t * P:(t + 1) * P], self.h[:, t, f * P:(f + 1) * P],
                                           self.ident[:])
                turned = state["turned"] = pe.mark(ins)
                act.wait(read_at)
                split_last[f]()
                full = self.tr[f][:, 0:T].rearrange("p (i n) -> p i n", n=P)
                pair = slice(f * NT, (f + 1) * NT)
                hi_at = self.a(self.ht_hi[:, pair], full, ACT.Copy, turned)
                ready[f] = self.tr_free[f] = self.tt(self.ht_lo[:, pair], full, self.ht_hi[:, pair].bitcast(F32),
                                                     ALU.subtract, hi_at)
        self.used_out = self.acc_at[3]
        self.h_at_prev = list(self.h_at)
        for t in range(NT):
            for half in range(2):
                cols, a = slice(half * CW, (half + 1) * CW), 2 * t + half
                self.x_done(t, half, self.stt(self.x[:, t, cols], self.acc[a][:], 0.5, self.x[:, t, cols],
                                              ALU.mult, ALU.add, self.acc_at[a], self.src_read, self.sq_at[t]))
                self.acc_free[a] = self.x_ready[t]

    def x_done(self, t, half, point):
        self.x_half[t][half] = self.x_ready[t] = point

    def out_projection(self):
        for c in range(D // CW):
            def read(t, point):
                cols = slice(c * CW, (c + 1) * CW)
                self.dve.wait(point, self.src_read, self.sq_at[t])
                self.bank_free[t] = self.dve.mark(self.dve.eng.tensor_tensor(
                    self.x[:, t, cols], self.bank[t][:], self.x[:, t, cols], ALU.add))
                self.x_done(t, c, self.bank_free[t])
            self.chunk(read)

    def conv_chunks(self):
        return [(self.mat_src(self.t["conv_w_in_2"][0], c * CW), CW) for c in range(3 * D // CW)] + [
            (self.mat_src(self.t["conv_w_out_2"][0], c * CW), CW) for c in range(D // CW)]

    def conv(self):
        self.to_xt(self.x_tile, gain=G_MIX, normed=True)
        taps = 3
        b = self.area(0, KT, T)
        y = self.area(2048, KT, T)
        u = self.area(4096, KT, T + taps - 1)
        self.pool.wait(*self.x_ready)
        zero = self.pool.mark(self.pool.eng.memset(u[:, :, 0:taps - 1], 0.0))
        c_at, z_at = {}, []
        pair = lambda v, n: v[:, 2 * n:2 * n + 2]
        for i in range(2):
            def read(t, p, i=i):
                self.b_at = self.bank_free[t] = self.a(
                    pair(b, 2 * i + t), self.bank[t][:].rearrange("p (f n) -> p f n", f=2), ACT.Copy, p)
            self.chunk(read, feature_major=True)
        for i in range(2):
            def read(t, p, i=i):
                dst = pair(u, 2 * i + t)[:, :, taps - 1:]
                c_at[2 * i + t] = self.bank_free[t] = self.a(
                    dst, self.bank[t][:].rearrange("p (f n) -> p f n", f=2), ACT.Copy, p)
            self.chunk(read, feature_major=True)
        for i in range(2):
            def read(t, p, i=i):
                n = 2 * i + t
                dst = pair(u, n)[:, :, taps - 1:]
                q = self.bank_free[t] = self.tt(dst, self.bank[t][:].rearrange("p (f n) -> p f n", f=2), dst,
                                                ALU.mult, p, c_at[n], zero)
                for f in range(2):
                    k = 2 * n + f
                    g = lambda j: self.gains[:, G_CONV + j * KT + k:G_CONV + j * KT + k + 1]
                    r = self.ts(y[:, k], u[:, k, 0:T], g(0), None, ALU.mult, None, q)
                    r = self.stt(y[:, k], u[:, k, 1:T + 1], g(1), y[:, k], ALU.mult, ALU.add, r)
                    r = self.stt(y[:, k], u[:, k, 2:T + 2], g(2), y[:, k], ALU.mult, ALU.add, r)
                z_at.append(self.tt(pair(y, n), pair(y, n), pair(b, n), ALU.mult, r, self.b_at))
            self.chunk(read, feature_major=True)
        ready = []
        for n in range(4):
            hi = pair(self.xt_hi, n)
            p = self.a(hi, pair(y, n), ACT.Copy, z_at[n], self.used[1 - self.par])
            ready += [p, self.tt(pair(self.xt_lo, n), pair(y, n), hi.bitcast(F32), ALU.subtract, p)]
        half_at = [ready[2], ready[3], ready[6], ready[7]]
        self.xt_ready = [half_at, half_at]
        self.out_projection()

    def head_rms(self, t, src, heads, width, point, slot=0):
        sq = self.sq_junk[:, 0:heads * width]
        ss, ms, r = (self.small[:, slot, j, 0:heads] for j in range(3))
        s3 = src.rearrange("p (h d) -> p h d", h=heads)
        p = self.a(sq.rearrange("p (h d) -> p h d", h=heads), s3, ACT.Square, point, self.sq_free, self.sq_junk_at)
        p = self.red(ss, sq.rearrange("p (h d) -> p h d", h=heads), ALU.add, p, self.rms_free[slot])
        self.sq_free = p
        p = self.ts(ms, ss, 1.0 / width, EPS, ALU.mult, ALU.add, p)
        self.dve.wait(p)
        p = self.dve.mark(self.dve.eng.reciprocal(ss, ms))
        return r, self.a(r, ss, ACT.Sqrt, p)

    def turn_heads(self, t, src, dst, gain, *after):
        self.pe.wait(self.tr_free[t], *after)
        for i in range(4):
            ins = self.pe.eng.transpose(self.tr[t][:, i * P:(i + 1) * P], src(i), self.ident[:])
        p = self.pe.mark(ins)
        self.turned_at = p
        v = self.tr[t][:].rearrange("p (i n) -> p i n", i=4)
        self.tr_free[t] = self.a(dst, v, ACT.Copy, p, scale=self.gains[:, gain:gain + 1])
        return self.tr_free[t]

    def normed_heads(self, t, point, dst, dup=1, width=CW, b=None):
        n = width // DH
        b = t if b is None else b
        r, p = self.head_rms(t, self.bank[b][:, 0:width], n, DH, point, slot=t)
        src = self.bank[b][:, 0:width].rearrange("p (h d) -> p h d", h=n)
        if dup == 1:
            o, s, rr = dst.rearrange("p (h d) -> p h d", h=n), src, r.unsqueeze(2).to_broadcast([P, n, DH])
            p = self.tt(o, s, rr, ALU.mult, p)
        else:
            for j in range(dup):
                p = self.tt(dst[:, :, j, :], src, r.unsqueeze(2).to_broadcast([P, n, DH]), ALU.mult, p)
        self.rms_free[t] = self.bank_free[b] = p
        return p

    def fox_chunks(self):
        w = self.t["fox_w_in"][0]
        return ([(self.mat_src(w, c), CW) for c in (0, CW, D, D + CW)]
                + [(self.mat_src(w, 4 * D, FOX_HEADS), FOX_HEADS)]
                + [(self.mat_src(w, c), CW) for c in (2 * D, 2 * D + CW, 3 * D, 3 * D + CW)]
                + [(self.mat_src(self.t["fox_w_out"][0], c * CW), CW) for c in range(D // CW)])

    def fox(self):
        tmp = self.area(0, NT, D)
        qt, kt = self.area(2048, KT, T), self.area(4096, KT, T)
        v, g = self.area(6144, NT, D), self.area(8192, NT, D)
        select = self.area(10240, FOX_HEADS, P)
        s_buf = self.area(12288, 2, T)
        pt = self.area(12800, 2, T)
        nct = self.area(13312, T)
        causal = self.area(13568, T)
        upto = self.area(13824, P)
        ones = self.area(13952, P)
        lf = self.area(14080, NT, FOX_HEADS)
        cc = self.area(14112, NT, FOX_HEADS)
        z = self.area(14144, NT, FOX_HEADS)
        bf = self.area(14176, FOX_HEADS)
        nm, den = self.area(14192, NT, FOX_HEADS), self.area(14224, NT, FOX_HEADS)
        gq = self.area(14256, 1)
        sp, pe, pool = self.sp, self.pe, self.pool
        self.act.wait(*self.x_ready)
        load = lambda d, s_: self.arena_in.mark(self.act.eng.dma_start(d, s_))
        load(select, self.t["c_select"])
        load(upto, self.t["c_upto"])
        load(causal, self.t["c_causal"].rearrange("p a b -> p (a b)"))
        b_f = self.t["fox_b_f"]
        here = load(bf, bass.AP(tensor=b_f.tensor, offset=b_f.offset, ap=[[0, P], [1, FOX_HEADS]]))
        pool.wait(*self.x_ready)
        pool.wait(pool.mark(pool.eng.memset(ones, 1.0)))
        set_at = pool.mark(pool.eng.memset(nct, 0.0))
        self.to_xt(self.x_tile, gain=G_NORM + 32, normed=True)

        gq_at = self.ts(self.gains[:, G_FOXQ:G_FOXQ + 1], self.gains[:, G_FOXQ:G_FOXQ + 1], DH ** -0.5, None,
                        ALU.mult, None)
        self.act.wait(gq_at)
        last = {}
        turned = {}
        todo = []

        def turn_todo():
            while todo:
                todo.pop(0)()

        for i in range(4):
            dst_t, gain = (qt, G_FOXQ) if i < 2 else (kt, G_FOXK)

            def read(t, p, i=i, dst_t=dst_t, gain=gain):
                c = i % 2
                turn_todo()
                cols = tmp[:, t, c * CW:(c + 1) * CW]
                self.dve.wait(turned.get((i - 2, t)))
                n = self.normed_heads(t, p, cols)

                def later():
                    last[i, t] = self.turn_heads(
                        t, lambda j: tmp[:, t, c * CW + j * P:c * CW + (j + 1) * P],
                        dst_t[:, 4 * c:4 * c + 4, t * P:(t + 1) * P], gain, n)
                    turned[i, t] = self.turned_at
                todo.append(later)
            self.chunk(read)
        def read(t, p):
            turn_todo()
            h = self.small[:, t, 3, :]
            p = self.bank_free[t] = self.tt(z[:, t], self.bank[t][:, 0:FOX_HEADS], bf, ALU.add, p, here)
            q = self.a(h, z[:, t], ACT.Abs, p)
            q = self.a(h, h, ACT.Exp, q, scale=-1.0)
            q = self.a(h, h, ACT.Ln, q, bias=1.0)
            self.lf_at[t] = self.stt(lf[:, t], z[:, t], 0.0, h, ALU.min, ALU.subtract, q)
        self.lf_at = [None, None]
        self.chunk(read, w=FOX_HEADS)
        qk_at = [last[k] for k in last]

        def cumulate():
            pe.wait(set_at, here, *self.tr_free)
            o = self.tr[0]
            self.mm(o[:, 0:16], upto, lf[:, 0], *self.lf_at)
            self.mm(o[:, 16:32], upto, lf[:, 1], start=True, stop=False)
            p = self.mm(o[:, 16:32], ones, lf[:, 0], start=False, stop=True)
            o2 = self.tr[1]
            self.mm(o2[0:16, 0:P], lf[:, 0], upto)
            self.mm(o2[0:16, P:T], lf[:, 1], upto, start=True, stop=False)
            q = self.mm(o2[0:16, P:T], lf[:, 0], ones, start=False, stop=True)
            self.tr_free[0] = self.cc_at = self.a(cc, o[:, 0:32].rearrange("p (t h) -> p t h", t=2), ACT.Copy, p)
            self.tr_free[1] = self.nct_at = self.ts(nct[0:16], o2[0:16, 0:T], -1.0, None, ALU.mult, None, q, set_at)

        steps = [(h, t) for h in range(FOX_HEADS) for t in range(NT)]
        st = {}
        v_at = {}

        def scores(i):
            h, t = steps[i]
            rows, n = slice(DH * (h % 2), DH * (h % 2) + DH), (t + 1) * P
            bank, free = ((self.bank[1], self.bank_free), (self.tr[1], self.tr_free))[i % 2]
            pe.wait(free[1], self.nct_at, *qk_at)
            o = bank[:, 0:n]
            self.mm(o, qt[rows, h // 2, t * P:(t + 1) * P], kt[rows, h // 2, 0:n], start=True, stop=False)
            p = self.mm(o, select[:, h], nct[:, 0:n], start=False, stop=True)
            s = s_buf[:, i % 2, 0:n]
            p = free[1] = self.stt(s, o, cc[:, t, h:h + 1], causal[:, T - n:T], ALU.add, ALU.add,
                                                 p, self.cc_at, st.get(("turned", i - 2)))
            p = self.red(nm[:, t, h:h + 1], s, ALU.max, p, negate=True)
            st["exp", i] = self.a(s, s, ACT.Exp, p, bias=nm[:, t, h:h + 1], accum_out=den[:, t, h:h + 1])

        def turn(i):
            h, t = steps[i]
            pe.wait(st["exp", i], self.tr_free[0])
            for b in range(t + 1):
                ins = pe.eng.transpose(self.tr[0][:, b * P:(b + 1) * P],
                                       s_buf[:, i % 2, b * P:(b + 1) * P], self.ident[:])
            p = st["turned", i] = pe.mark(ins)
            n = (t + 1) * P
            st["pt", i] = self.tr_free[0] = self.a(pt[:, i % 2, 0:n], self.tr[0][:, 0:n], ACT.Copy, p,
                                                   st.get(("pv", i - 2)))

        def values(i):
            h, t = steps[i]
            a = 2 * t + h // 8
            pe.wait(st["pt", i], v_at[h // 8], self.acc_free[a])
            for b in range(t + 1):
                p = self.mm(self.acc[a][:, (h % 8) * DH:(h % 8 + 1) * DH], pt[:, i % 2, b * P:(b + 1) * P],
                            v[:, b, h * DH:(h + 1) * DH], start=(b == 0), stop=(b == t))
            st["pv", i] = p

        scaled = {}

        def step(i):
            if i < len(steps):
                scores(i)
            if 1 <= i <= len(steps):
                turn(i - 1)
            if i >= 2:
                values(i - 2)

        def normalise():
            self.dve.wait(st["exp", len(steps) - 1])
            inv_at = self.dve.mark(self.dve.eng.reciprocal(den, den))
            for t in range(NT):
                for half in range(2):
                    r = den[:, t, 8 * half:8 * half + 8].unsqueeze(2).to_broadcast([P, 8, DH])
                    o3 = tmp[:, t, half * CW:(half + 1) * CW].rearrange("p (h d) -> p h d", h=8)
                    scaled[t, half] = self.acc_free[2 * t + half] = self.tt(
                        o3, self.acc[2 * t + half][:].rearrange("p (h d) -> p h d", h=8), r, ALU.mult,
                        st["pv", len(steps) - 1], inv_at)

        o_at = {}

        def gate(t, half):
            cols = slice(half * CW, (half + 1) * CW)
            o_at[t, half] = self.tt(tmp[:, t, cols], tmp[:, t, cols], g[:, t, cols], ALU.mult,
                                    scaled[t, half], g_at[t, half])

        todo_steps = [lambda i=i: step(i) for i in range(len(steps) + 2)] + [normalise]

        def fill():
            if todo_steps:
                todo_steps.pop(0)()

        for i in range(2):
            def read(t, p, i=i):
                v_at[i] = self.bank_free[0] = self.a(v[:, t, i * CW:(i + 1) * CW], self.bank[0][:], ACT.Copy, p)
            if i == 1:
                cumulate()
                self.fill = fill
            self.chunk(read, b=0)
        g_at = {}
        for i in range(2):
            def read(t, p, i=i):
                c = g[:, t, i * CW:(i + 1) * CW]
                if i == 0:
                    g_at[t, 0] = self.bank_free[0] = self.a(c, self.bank[0][:], ACT.Copy, p)
                    return
                while todo_steps:
                    todo_steps.pop(0)()
                if t == 0:
                    for tile in range(NT):
                        c0 = g[:, tile, 0:CW]
                        g_at[tile, 0] = self.a(c0, c0, ACT.Sigmoid, g_at[tile, 0])
                g_at[t, 1] = self.bank_free[0] = self.a(c, self.bank[0][:], ACT.Sigmoid, p)
                gate(t, 0)
                gate(t, 1)
            self.chunk(read, b=0)
        self.fill = None
        self.to_xt(lambda t, k: tmp[:, t, k * P:(k + 1) * P],
                   ready=[(o_at[t, 0], o_at[t, 1]) for t in range(NT)])
        self.out_projection()

    def hgrn_chunks(self):
        w = self.t["hg_w_in"][0]
        cols = [D, D + CW, 0, CW, 2 * D, 2 * D + CW, 3 * D, 3 * D + CW]
        return [(self.mat_src(w, c), CW) for c in cols] + [
            (self.mat_src(self.t["hg_w_out"][0], c * CW), CW) for c in range(D // CW)]

    def hgrn(self):
        H = HG_HEADS
        kk, qq = self.area(2048, H, T), self.area(4096, H, T)
        v, g = self.area(6144, NT, D), self.area(8192, NT, D)
        pt = self.area(10240, 2, 3, 4 * P)
        prods = {1: self.area(0, H, T), 2: self.xg[:].rearrange("p a (h n) -> p (a h) n", h=H // 2)}
        at = 13312
        for m in (4, 8, 16, 32, 64):
            prods[m] = self.area(at, H, T // m)
            at += H * T // m
        prods_at = {}
        pool, pe, dve = self.pool, self.pe, self.dve
        pool.wait(*self.x_ready)
        pt_zero = pool.mark(pool.eng.memset(pt[:], 0.0))
        self.to_xt(self.x_tile, gain=G_NORM + 8, normed=True)
        k_at, q_at = [], []

        for i in range(2):
            def read(t, p, i=i):
                n = 2 * i + t
                src = self.bank[t][:].rearrange("p (f n) -> p f n", f=2)
                f_ = prods[1][:, 2 * n:2 * n + 2]
                p1 = self.a(f_, src, ACT.Sigmoid, p)
                p2 = self.bank_free[t] = self.a(kk[:, 2 * n:2 * n + 2], src, ACT.Sigmoid, p, scale=-1.0)
                for f in range(2):
                    h = 2 * n + f
                    lb, om = self.lbs[:, 0, h:h + 1], self.lbs[:, 1, h:h + 1]
                    p1 = self.ts(prods[1][:, h], prods[1][:, h], om, lb, ALU.mult, ALU.add, p1, self.lb_at)
                    k_at.append(self.ts(kk[:, h], kk[:, h], om, None, ALU.mult, None, p2))
                prods_at[1] = self.ts(f_, f_, MIN_GATE, None, ALU.max, None, p1)
            self.chunk(read, feature_major=True)
        for i in range(2):
            def read(t, p, i=i):
                n = 2 * i + t
                self.bank_free[t] = self.a(
                    qq[:, 2 * n:2 * n + 2], self.bank[t][:].rearrange("p (f n) -> p f n", f=2), ACT.Silu, p)
                q_at.append(self.bank_free[t])
            self.chunk(read, feature_major=True)
        dve.wait(*self.xg_free)
        ready = {(0, grp): [k_at[4 * grp + 3], q_at[2 * grp + 1]] for grp in range(2)}
        state = {"n": 0, "pt": [None, None], "cross": [None, None]}

        def scores_step(level, grp):
            hs = slice(4 * grp, 4 * grp + 4)
            m = 2 ** (level - 1) if level else 0
            n = state["n"] = state["n"] + 1
            made = []
            for tile in range(NT if level <= 7 else 1):
                a = 2 * (n % 2) + tile
                acc = self.acc[a]
                pe.wait(*ready[level, grp], self.acc_free[a])
                s0, t0, w = tile * P, tile * P, P
                if level == 7:
                    t0, w = tile * P + m, m
                elif level == 8:
                    t0 = P
                for h in range(4):
                    p = self.mm(acc[0:w, h * w:(h + 1) * w], kk[:, 4 * grp + h, s0:s0 + w],
                                qq[:, 4 * grp + h, t0:t0 + w])
                made.append((a, tile, p))
            if level < 8:
                if level == 0:
                    q = self.tt(qq[:, hs], qq[:, hs], prods[1][:, hs], ALU.mult, p, prods_at[1])
                    ready[1, grp] = [q]
                else:
                    if m > 1 and m not in prods_at:
                        pair = prods[m // 2].rearrange("p h (n u) -> p (h n) u", u=2)
                        prods_at[m] = self.tt(prods[m].rearrange("p h n -> p (h n)"), pair[:, :, 0],
                                              pair[:, :, 1], ALU.mult, prods_at[m // 2])
                    half = lambda v_, j_: v_.rearrange("p h (n u m) -> p (h n) u m", u=2, m=m)[:, :, j_]
                    nb = T // (2 * m)
                    other = lambda j_: prods[m][:, hs].rearrange("p h (n u) -> p (h n) u", u=2)[
                        :, :, j_:j_ + 1].to_broadcast([P, 4 * nb, m])
                    q0 = self.tt(half(kk[:, hs], 0), half(kk[:, hs], 0), other(1), ALU.mult, p, prods_at[m],
                                 *ready[level, grp])
                    q1 = self.tt(half(qq[:, hs], 1), half(qq[:, hs], 1), other(0), ALU.mult)
                    ready[level + 1, grp] = [q0, q1]
            for a, tile, p in made:
                if level <= 6:
                    mask = self.masks[:, level, :].unsqueeze(1).to_broadcast([P, 4, P])
                    dve.wait(p, pt_zero, state["pt"][grp])
                    q = dve.mark(dve.eng.copy_predicated(
                        pt[:, grp, tile].rearrange("p (h n) -> p h n", h=4), mask,
                        self.acc[a][:].rearrange("p (h n) -> p h n", h=4)))
                    if tile == 1:
                        state["pt"][grp] = q
                elif level == 7:
                    q = self.a(pt[0:m, grp, tile].rearrange("p (h n) -> p h n", h=4)[:, :, m:],
                               self.acc[a][0:m, 0:4 * m].rearrange("p (h n) -> p h n", h=4), ACT.Copy,
                               p, pt_zero, state["pt"][grp])
                    state["half"] = q
                else:
                    q = state["cross"][grp] = self.a(pt[:, grp, 2], self.acc[a][:], ACT.Copy, p, pt_zero)
                self.acc_free[a] = q

        sums = self.small[:, 0, 0:2].rearrange("p a n -> p (a n)")[:, 0:16]
        ms, r = self.small[:, 0, 2], self.small[:, 0, 3]
        square_at, o_at = [], {}

        def values(grp, t):
            a = 2 * grp + t
            pe.wait(state["pt"][grp], state["half"], state["cross"][grp], self.v_at, self.acc_free[a])
            for h in range(4):
                hc = slice((4 * grp + h) * P, (4 * grp + h + 1) * P)
                o = self.acc[a][:, h * P:(h + 1) * P]
                score = lambda j: pt[:, grp, j, h * P:(h + 1) * P]
                p = self.mm(o, score(t), v[:, t, hc], start=True, stop=(t == 0))
                if t == 1:
                    p = self.mm(o, score(2), v[:, 0, hc], start=False, stop=True)
            o_at[grp, t] = p
            p = self.a(self.sq_junk[:], self.acc[a][:], ACT.Square, p, self.sq_free, self.sq_junk_at)
            self.sq_free = self.red(sums[:, 4 * a:4 * a + 4], self.sq_junk[:].rearrange("p (h d) -> p h d", h=4),
                                    ALU.add, p, self.rms_free[0])
            square_at.append(self.sq_free)

        def roots():
            p = self.ts(ms, sums, 1.0 / P, EPS, ALU.mult, ALU.add, *square_at)
            dve.wait(p)
            p = dve.mark(dve.eng.reciprocal(sums, ms))
            self.root_at = self.a(r, sums, ACT.Sqrt, p)

        gated = {}

        def gate(grp, t):
            a = 2 * grp + t
            for h in range(4):
                hc, gc = slice(h * P, (h + 1) * P), slice((4 * grp + h) * P, (4 * grp + h + 1) * P)
                gated[t, grp] = self.stt(self.out_hg(grp, t)[:, hc], self.acc[a][:, hc], r[:, 4 * a + h:4 * a + h + 1],
                                         g[:, t, gc], ALU.mult, ALU.mult, o_at[grp, t], self.root_at, g_at[grp, t])
            self.acc_free[a] = self.rms_free[0] = gated[t, grp]

        todo = [lambda lv=lv, grp=grp: scores_step(lv, grp) for lv in range(9) for grp in range(2)]
        todo += [lambda grp=grp, t=t: values(grp, t) for grp in range(2) for t in range(NT)]
        todo.append(roots)
        slot = {"n": 0}

        def fill():
            slot["n"] += 1
            if slot["n"] % 2 and todo:
                todo.pop(0)()

        self.fill = fill
        for i in range(2):
            def read(t, p, i=i):
                self.v_at = self.bank_free[t] = self.a(v[:, t, i * CW:(i + 1) * CW], self.bank[t][:], ACT.Copy, p)
            self.chunk(read)
        g_at = {}
        for i in range(2):
            def read(t, p, i=i):
                c = g[:, t, i * CW:(i + 1) * CW].rearrange("p (h d) -> p h d", h=4)
                self.bank_free[t] = self.a(c, self.bank[t][:].rearrange("p (h d) -> p h d", h=4), ACT.Silu, p)
                g_at[i, t] = self.tt(c, c, self.og.unsqueeze(1).to_broadcast([P, 4, P]), ALU.mult,
                                     self.bank_free[t])
                if i == 1:
                    while todo:
                        todo.pop(0)()
                    if t == 0:
                        gate(0, 0)
                        gate(0, 1)
                    gate(1, t)
            self.chunk(read)
        self.fill = None
        self.xg_free = [g_at[1, 1], g_at[1, 1]]
        self.to_xt(lambda t, k: self.out_hg(k // 4, t)[:, (k % 4) * P:(k % 4 + 1) * P],
                   ready=[(gated[t, 0], gated[t, 1]) for t in range(NT)])
        self.out_projection()

    def out_hg(self, grp, t):
        return self.area(4096, 2, NT, CW)[:, grp, t]

    KV_T, KV_V, KV_CT, KV_CV, KV_CB = 0, 2048, 3072, 3136, 4160

    def kv_chunks(self):
        w = self.t["w_kv_2"]
        return [(self.kv_pair_src(w), CW)] + [(self.mat_src(w, c * CW), CW) for c in (1, 2)]

    def kv_areas(self):
        class Areas:
            pass
        a = Areas()
        a.kt = self.area(self.KV_T, 2, GROUPS, T)
        a.vv = self.area(self.KV_V, 2, NT, GROUPS * DH)
        a.kct = self.area(self.KV_CT, GROUPS, NB_CMP)
        a.vcb = self.area(self.KV_CV, 2, CW)
        a.cb = self.area(self.KV_CB, NT, NSA_HEADS, NB_CMP)
        a.w1 = self.area(4672, CMP_BLOCK, P)
        a.kv0 = self.area(8768, GROUPS, T)
        a.blk = [self.area(9792, GROUPS, T), self.area(10816, GROUPS, T)]
        a.dup = self.area(11840, 2, GROUPS, 2, DH)
        a.w2 = self.area(12864, 2, DH)
        a.hid = self.area(12992, 2, GROUPS * NC_CMP + 4)
        a.kc = self.area(13120, GROUPS, 2, DH)
        a.vc = self.area(13632, GROUPS, DH)
        a.relb = self.area(13888, NSA_HEADS)
        return a

    def kv_prepare(self):
        t_, a = self.t, self.kv_areas()
        pe, act, pool = self.pe, self.act, self.pool
        kct, vcb, cb, w1, w2, relb = a.kct, a.vcb, a.cb, a.w1, a.w2, a.relb
        act.wait(*self.x_ready)
        load = lambda d, s_: self.arena_in.mark(act.eng.dma_start(d, s_))
        load_rel = lambda d, s_: self.rel_in.mark(act.eng.dma_start(d, s_))
        load_rel(relb[0:N_BUCKETS], t_["rel_bias_2"])
        oh = self.area(9792, 2, REL_W)
        here = load_rel(oh[0:REL_ROWS], t_["c_rel"].rearrange("a r w -> r a w"))
        load(w1[0:DH], t_["cmp_w1_k_2"].rearrange("(j d) h -> d j h", d=DH))
        load(w1[DH:P], t_["cmp_w1_v_2"].rearrange("(j d) h -> d j h", d=DH))
        load(w2[:, 0], t_["cmp_w2_k_2"])
        self.w_cmp_at = load(w2[:, 1], t_["cmp_w2_v_2"])
        pool.wait(*self.x_ready)
        pool.wait(pool.mark(pool.eng.memset(relb[N_BUCKETS:REL_ROWS], NEG)))
        set_at = pool.mark(pool.eng.memset(kct, 0.0))
        self.kv_here, self.kv_set = here, set_at
        rb = relb[0:REL_ROWS]
        rows = self.area(8768, REL_W)
        n = NSA_HEADS * REL_W
        scr = self.bias_rows = self.nc.dram_tensor("bias_rows", (P, NSA_HEADS, REL_W), F32, kind="Internal").ap()

        def by_distance():
            p = self.mm(self.acc[0][0:NSA_HEADS, :], rb, oh[0:REL_ROWS, 1], here, set_at, self.acc_free[0])
            p = self.acc_free[0] = self.a(rows[0:NSA_HEADS], self.acc[0][0:NSA_HEADS, :], ACT.Copy, p)
            act.wait(p)
            r_ap = rows[0:NSA_HEADS].unsqueeze(1).to_broadcast([NSA_HEADS, P, REL_W])
            self.bias_wrote = self.scratch.mark(act.eng.dma_start(scr.rearrange("c h w -> h c w"), r_ap))

        def by_block(t, half):
            pe.wait(here, set_at, self.acc_free[1])
            for b in range(8 * half, 8 * half + 8):
                first = T + t * P - CMP_STRIDE * b - (CMP_BLOCK - 1) if b < NC_CMP else 0
                o = self.acc[1][:].rearrange("p (t h n) -> p t n h", t=NT, h=NSA_HEADS)[:, t, b]
                self.bias_done = self.mm(o, oh[0:REL_ROWS, 0, first:first + P], rb)

        def keep():
            self.acc_free[1] = self.cb_at = self.a(
                cb, self.acc[1][:].rearrange("p (t h n) -> p t h n", t=NT, h=NSA_HEADS), ACT.Copy, self.bias_done)

        return [lambda: None] * 8 + [by_distance] + [lambda t=t, half=half: by_block(t, half) for t in range(NT) for half in range(2)] + [keep]

    def kv(self):
        a = self.kv_areas()
        kt, vv, kct, vcb, w1, kv0, blk, dup = a.kt, a.vv, a.kct, a.vcb, a.w1, a.kv0, a.blk, a.dup
        w2, hid, kc, vc = a.w2, a.hid, a.kc, a.vc
        pe, act, dve, pool = self.pe, self.act, self.dve, self.pool
        here, set_at, wrote, bias_done = self.kv_here, self.kv_set, self.bias_wrote, self.bias_done
        self.to_xt(self.x_tile, gain=G_KV, normed=True)

        def read0(t, p):
            self.kv0_at = self.bank_free[t] = self.a(
                kv0[:, 2 * t:2 * t + 2], self.bank[t][:].rearrange("p (f n) -> p f n", f=2), ACT.Copy, p, wrote)
        self.chunk(read0, feature_major=True)

        blk_at = []
        for j in range(2):
            pe_col = self.gains[:, G_PE + 16 * j:G_PE + 16 * j + 16].unsqueeze(1).to_broadcast(
                [P, GROUPS * T // 16, 16])
            blk_at.append(self.tt(blk[j].rearrange("p g (n j) -> p (g n) j", j=16),
                                  kv0.rearrange("p g (n j) -> p (g n) j", j=16), pe_col, ALU.add,
                                  self.kv0_at, bias_done))
        todo = []

        def branch(br):
            def read(t, p):
                while todo:
                    todo.pop(0)()
                self.dve.wait(self.dup_free[t], bias_done)
                self.v_pts.append(self.a(vv[:, br, t], self.bank[t][:, GROUPS * DH:CW], ACT.Copy, p))
                n = self.normed_heads(t, p, dup[:, t], dup=2, width=GROUPS * DH)

                def later():
                    self.k_pts.append(self.turn_heads(
                        t, lambda j: dup[:, t, j].rearrange("p a d -> p (a d)"),
                        kt[:, br, :, t * P:(t + 1) * P], G_KN + 1 + br, n))
                    self.dup_free[t] = self.turned_at
                todo.append(later)
            return read
        self.dup_free, self.v_pts, self.k_pts = [None, None], [], []
        for br in range(2):
            self.chunk(branch(br))
        def hidden(kv, q):
            rows_ = slice(kv * DH, (kv + 1) * DH)
            o = self.acc[2 + kv][:, 0:GROUPS * NC_CMP]
            pe.wait(*blk_at, self.w_cmp_at, self.acc_free[2 + kv])
            for j in range(8 * q, 8 * q + 8):
                b = blk[j // 16].rearrange("p g (n j) -> p g n j", j=16)
                n0 = j // 16
                p = self.mm(o.rearrange("p (g n) -> p g n", g=GROUPS), w1[rows_, j],
                            b[rows_, :, n0:n0 + NC_CMP, j % 16], start=(j == 0), stop=(j == CMP_BLOCK - 1))
            at["hidden", kv] = p

        def gelu():
            for kv in range(2):
                at["hid", kv] = self.acc_free[2 + kv] = self.a(
                    hid[:, kv, 0:GROUPS * NC_CMP], self.acc[2 + kv][:, 0:GROUPS * NC_CMP], ACT.Gelu_apprx_tanh,
                    at["hidden", kv])
            tb = self.area(4672, NSA_HEADS, T)
            scr = self.bias_rows
            act.wait(at["hid", 1], wrote)
            src = bass.AP(tensor=scr.tensor, offset=scr.offset + P - 1,
                          ap=[[NSA_HEADS * REL_W - 1, P], [REL_W, NSA_HEADS], [1, T]])
            self.tb_at = self.scratch.mark(act.eng.dma_start(tb, src))

        n = NC_CMP
        out = self.acc[0]
        rows8 = self.area(13904, 8, NB_CMP)[0:n]

        def outputs():
            pe.wait(at["hid", 0], at["hid", 1], self.acc_free[0])
            for kv in range(2):
                for g in range(GROUPS):
                    i = kv * GROUPS + g
                    p = self.mm(out[0:NC_CMP, i * DH:(i + 1) * DH], hid[:, kv, g * NC_CMP:(g + 1) * NC_CMP],
                                w2[:, kv])
            ss, ms, r = (self.small[0:n, 0, j, 0:GROUPS] for j in range(3))
            k3 = out[0:n, 0:GROUPS * DH].rearrange("p (g d) -> p g d", g=GROUPS)
            sq = self.sq_junk[0:n, 0:GROUPS * DH].rearrange("p (g d) -> p g d", g=GROUPS)
            vc_at = self.a(vc[0:n], out[0:n, GROUPS * DH:CW].rearrange("p (g d) -> p g d", g=GROUPS), ACT.Copy, p)
            q = self.a(sq, k3, ACT.Square, p, self.sq_free, self.sq_junk_at)
            q = self.red(ss, sq, ALU.add, q, self.rms_free[0])
            self.sq_free = q
            q = self.ts(ms, ss, 1.0 / DH, EPS, ALU.mult, ALU.add, q)
            dve.wait(q)
            q = dve.mark(dve.eng.reciprocal(ss, ms))
            q = self.a(r, ss, ACT.Sqrt, q)
            for j in range(2):
                q = self.tt(kc[0:n, :, j], k3, r.unsqueeze(2).to_broadcast([n, GROUPS, DH]), ALU.mult, q, p)
            self.rms_free[0] = self.acc_free[0] = at["kc"] = q
            at["vc"] = self.a(rows8, self.ident[0:n, 0:NB_CMP].unsqueeze(1).to_broadcast([n, 8, NB_CMP]), ACT.Copy, vc_at)

        def spread():
            o = self.acc[1][:, 0:GROUPS * DH]
            p = self.mm(o, rows8.rearrange("p h n -> p (h n)"), vc[0:n].rearrange("p g d -> p (g d)"), at["vc"],
                        self.acc_free[1])
            mask = self.rowmask[:, NT:NT + 8].rearrange("p (g h) -> p g h", g=2).unsqueeze(3).to_broadcast(
                [P, 2, 4, DH])
            for half in range(2):
                v4 = o.rearrange("p (g d) -> p g d", g=GROUPS)[:, 2 * half:2 * half + 2].unsqueeze(2).to_broadcast(
                    [P, 2, 4, DH])
                self.vcb_at = self.tt(vcb[:, half].rearrange("p (g h d) -> p g h d", g=2, h=4), v4, mask, ALU.mult, p)
            self.acc_free[1] = self.vcb_at

        def turn_keys():
            pe.wait(at["kc"], self.tr_free[0])
            for g in range(GROUPS):
                ins = pe.eng.transpose(self.tr[0][:, g * NB_CMP:g * NB_CMP + n],
                                       kc[0:n, g].rearrange("p a d -> p (a d)"), self.ident[0:n, 0:n])
            p = pe.mark(ins)
            self.tr_free[0] = self.kct_at = self.a(
                kct[:, :, 0:n], self.tr[0][:, 0:GROUPS * NB_CMP].rearrange("p (g n) -> p g n", g=GROUPS)[:, :, 0:n],
                ACT.Copy, p, set_at, scale=self.gains[:, G_KN:G_KN + 1])

        nothing = lambda: None
        at = {}
        self.tasks = todo + [lambda kv=kv, q=q: hidden(kv, q) for kv in range(2) for q in range(4)] + [
            nothing, gelu, nothing, nothing, outputs, nothing, spread, nothing, turn_keys]

    def nsa_chunks(self):
        w = self.t["attn_w_q_2"][0]
        return ([(self.mat_src(w, 0), CW), (self.mat_src(w, D, 3 * NSA_HEADS), 3 * NSA_HEADS), (self.mat_src(w, CW), CW)]
                + [(self.mat_src(self.t["attn_w_o_2"][0], c * CW), CW) for c in range(D // CW)])

    def nsa(self):
        H = NSA_HEADS
        assert T // 64 <= 16 and T <= 512
        kt = self.area(self.KV_T, 2, GROUPS, T)
        vv = self.area(self.KV_V, 2, NT, GROUPS * DH)
        kct = self.area(self.KV_CT, GROUPS, NB_CMP)
        vcb = self.area(self.KV_CV, 2, CW)
        cb = self.area(self.KV_CB, NT, H, NB_CMP)
        tb = self.area(4672, H, T)
        qt = self.area(8768, KT, T)
        tmp = self.area(10816, NT, D)
        s_buf = self.area(12864, 2, 2, T)
        gates = self.area(13888, NT, H, 3)
        nm, den = self.area(13984, NT, 2, H), self.area(14048, NT, 2, H)
        coef = self.area(14112, NT, 2, H)
        cpt = self.area(14176, P)
        pt = self.xg
        pe, act, dve = self.pe, self.act, self.dve
        self.to_xt(self.x_tile, gain=G_MIX + 8, normed=True)
        g_at = self.ts(self.gains[:, G_NSAQ:G_NSAQ + 1], self.gains[:, G_NSAQ:G_NSAQ + 1], DH ** -0.5, None,
                       ALU.mult, None)
        act.wait(g_at)
        later, q_pts, turned_q = [], [[], []], {}

        def q_chunk(i, b=None):
            def read(t, p):
                while later:
                    later.pop(0)()
                n = self.normed_heads(t, p, tmp[:, t, i * CW:(i + 1) * CW], b=b)

                def turn_q():
                    q_pts[i].append(self.turn_heads(
                        t, lambda j: tmp[:, t, i * CW + j * P:i * CW + (j + 1) * P],
                        qt[:, 4 * i:4 * i + 4, t * P:(t + 1) * P], G_NSAQ, n))
                    turned_q[t, i] = self.turned_at
                later.append(turn_q)
            self.chunk(read, b=b)

        def read(t, p):
            while later:
                later.pop(0)()
            self.gates_at = self.bank_free[t] = self.a(
                gates[:, t].rearrange("p h b -> p (h b)"), self.bank[t][:, 0:3 * H], ACT.Sigmoid, p)
        q_chunk(0)
        self.chunk(read, w=3 * H)

        o_at, cmp_at = {}, {}
        inner = self.h[:].rearrange("p a b -> p (a b)").rearrange("p (n c) -> p n c", n=2)
        self.cmp_pv = None

        def cmp_views(t):
            return (inner[:, t, 0:8 * NB_CMP].rearrange("p (h n) -> p h n", h=8),
                    inner[:, t, P:P + 8], inner[:, t, P + 8:P + 16])

        def cmp_scores(t, half):
            sc = cmp_views(t)[0]
            for odd in range(2):
                pe.wait(self.acc_free[odd], *q_pts[half], self.kct_at)
                rows = slice(DH * odd, DH * odd + DH)
                for i in range(4):
                    h = 8 * half + 2 * i + odd
                    p = self.mm(self.acc[odd][:, i * NB_CMP:(i + 1) * NB_CMP], qt[rows, h // 2, t * P:(t + 1) * P],
                                kct[rows, h * GROUPS // H])
                v4 = lambda a: a.rearrange("p (i o) n -> p i o n", o=2)[:, :, odd]
                self.acc_free[odd] = cmp_at[t] = self.tt(
                    v4(sc), self.acc[odd][:, 0:4 * NB_CMP].rearrange("p (i n) -> p i n", i=4),
                    v4(cb[:, t, 8 * half:8 * half + 8]), ALU.add, p, self.cmp_free)

        def cmp_softmax(t, half):
            sc, mx, sm = cmp_views(t)
            q = self.red(mx, sc, ALU.max, cmp_at[t])
            q = self.tt(sc, sc, mx.unsqueeze(2).to_broadcast([P, 8, NB_CMP]), ALU.subtract, q)
            cmp_at[t] = self.a(sc, sc, ACT.Exp, q)

        def cmp_gates(t, half):
            sc, mx, sm = cmp_views(t)
            q = self.red(sm, sc, ALU.add, cmp_at[t])
            dve.wait(q)
            q = dve.mark(dve.eng.reciprocal(sm, sm))
            q = self.stt(sm, sm, self.rowmask[:, t:t + 1], gates[:, t, 8 * half:8 * half + 8, 0],
                         ALU.mult, ALU.mult, q, self.gates_at)
            cmp_at[t] = self.tt(sc, sc, sm.unsqueeze(2).to_broadcast([P, 8, NB_CMP]), ALU.mult, q)

        def cmp_turn(t, half):
            pe.wait(cmp_at[t], self.tr_free[0])
            self.cmp_free = p = pe.mark(pe.eng.transpose(self.tr[0][:, 0:P], inner[:, t, 0:P], self.ident[:]))
            cmp_at[t] = self.tr_free[0] = self.a(cpt, self.tr[0][:, 0:P], ACT.Copy, p, self.cmp_pv)

        def cmp_values(t, half):
            pe.wait(self.vcb_at, self.acc_free[0])
            self.cmp_pv = p = self.mm(self.acc[0][:], cpt, vcb[:, half], cmp_at[t])
            self.acc_free[0] = o_at[t, half] = self.a(
                tmp[:, t, half * CW:(half + 1) * CW], self.acc[0][:], ACT.Copy, p, turned_q[t, half])

        steps = [(h, t) for h4 in range(2) for t in range(NT) for h in range(4 * h4, 4 * h4 + 4)]
        steps += [(h, t) for t in range(NT) for h in range(8, H)]
        st = {}
        ob = self.silu[:].rearrange("p a b -> p (a b)")

        def scores(i):
            h, t = steps[i]
            rows, n, g = slice(DH * (h % 2), DH * (h % 2) + DH), (t + 1) * P, h * GROUPS // H
            bank, free = ((self.bank[1], self.bank_free), (self.tr[1], self.tr_free))[i % 2]
            pe.wait(free[1], *q_pts[h // 8], *self.k_pts)
            for br in range(2):
                p = self.mm(bank[:, br * n:(br + 1) * n], qt[rows, h // 2, t * P:(t + 1) * P],
                            kt[rows, br, g, 0:n])
            s = s_buf[:, i % 2, :, 0:n]
            bias = tb[:, h, T - n:T].unsqueeze(1).to_broadcast([P, 2, n])
            p = free[1] = self.tt(
                s, bank[:, 0:2 * n].rearrange("p (b n) -> p b n", b=2), bias, ALU.add,
                p, self.tb_at, st.get(("turned", i - 2)))
            p = self.red(nm[:, t, :, h], s, ALU.max, p, negate=True)
            for br in range(2):
                q = self.a(s[:, br], s[:, br], ACT.Exp, p, bias=nm[:, t, br, h:h + 1],
                           accum_out=den[:, t, br, h:h + 1])
            st["exp", i] = q

        def turn(i):
            h, t = steps[i]
            n = (t + 1) * P
            pe.wait(st["exp", i], self.tr_free[0])
            for br in range(2):
                for b in range(t + 1):
                    ins = pe.eng.transpose(self.tr[0][:, br * n + b * P:br * n + (b + 1) * P],
                                           s_buf[:, i % 2, br, b * P:(b + 1) * P], self.ident[:])
            p = st["turned", i] = pe.mark(ins)
            st["pt", i] = self.tr_free[0] = self.a(pt[:, i % 2, 0:2 * n], self.tr[0][:, 0:2 * n], ACT.Copy, p,
                                                       st.get(("pv", i - 2)), *self.xg_free)

        def values(i):
            h, t = steps[i]
            n, g, q4 = (t + 1) * P, h * GROUPS // H, i // 4
            a = q4 % 2 + 2
            pe.wait(st["pt", i], self.acc_free[a], *self.v_pts)
            for br in range(2):
                for b in range(t + 1):
                    c = (br * 4 + h % 4) * DH
                    p = self.mm(self.acc[a][:, c:c + DH], pt[:, i % 2, br * n + b * P:br * n + (b + 1) * P],
                                vv[:, br, b, g * DH:(g + 1) * DH], start=(b == 0), stop=(b == t))
            st["pv", i] = p
            if i % 4 == 3:
                hs = slice(h - 3, h + 1)
                dve.wait(st["exp", i])
                q = dve.mark(dve.eng.reciprocal(den[:, t, :, hs], den[:, t, :, hs]))
                gg = gates[:, t, hs, 1:3].rearrange("p h b -> p b h")
                q = self.tt(coef[:, t, :, hs], den[:, t, :, hs], gg, ALU.mult, q)
                o4 = ob.rearrange("p (b h d) -> p b h d", b=2, h=4)
                q = self.tt(o4, self.acc[a][:].rearrange("p (b h d) -> p b h d", b=2, h=4),
                            coef[:, t, :, hs].unsqueeze(3).to_broadcast([P, 2, 4, DH]), ALU.mult, q, p)
                self.acc_free[a] = q
                cols = tmp[:, t, (h - 3) * DH:(h + 1) * DH]
                q = self.tt(cols, cols, ob[:, 0:FC], ALU.add, q, o_at[t, (h - 3) // 8])
                st["o", t, (h - 3) // 8] = self.tt(cols, cols, ob[:, FC:], ALU.add, q)

        def step(i):
            if i < len(steps):
                scores(i)
            if 1 <= i <= len(steps):
                turn(i - 1)
            if i >= 2:
                values(i - 2)

        def mixed(half):
            a, s_, g_, u, v_ = cmp_scores, cmp_softmax, cmp_gates, cmp_turn, cmp_values
            parts = [[(a, 0), (a, 1)], [(s_, 0), (s_, 1)], [(g_, 0), (g_, 1)], [(u, 0)], [(v_, 0), (u, 1)], [(v_, 1)]]
            first = half * len(steps) // 2
            for i in range(first, first + len(steps) // 2 + 2 * half):
                now = parts.pop(0) if parts else []
                if len(parts) > 2:
                    yield lambda i=i, now=now: [f(t, half) for f, t in now] + [step(i)]
                else:
                    yield lambda i=i, now=now: [step(i) if f is None else f(t, half)
                                                for f, t in now[:1] + [(None, 0)] + now[1:]]

        todo = list(mixed(0))

        def fill():
            if todo:
                todo.pop(0)()

        self.fill = fill
        q_chunk(1, b=0)
        self.fill = None
        for task in todo + later + list(mixed(1)):
            task()
        self.xg_free = [p_ for p_ in (st["pv", len(steps) - 2], st["pv", len(steps) - 1])]
        self.to_xt(lambda t, k: tmp[:, t, k * P:(k + 1) * P], ready=[(st["o", t, 0], st["o", t, 1]) for t in range(NT)])
        self.out_projection()

    def begin(self, stages):
        nc, t, sp, act, pe, dve = self.nc, self.t, self.sp, self.act, self.pe, self.dve
        self.xg_free = [None, None]
        self.h_at_prev = [None, None]
        self.diag_free, self.sq_at = [None, None], [None, None]
        self.warm_at = self.sq_junk_at = None
        self.src_read = self.sq_free = self.cmp_free = None
        self.rms_free = [None, None]
        x = t["x"].rearrange("o (t p) d -> p (o t) d", p=P)
        rows = self.arena[:, 0:2 * P].rearrange("p (a n) -> p a n", a=2)
        put = self.consts_in

        def load(dst, src):
            return put.mark(act.eng.dma_start(dst, src))

        load(self.ident[:], t["c_ident"])
        flat = lambda a: a.rearrange("a (k n) -> (a k) n", n=P)
        load(rows[0:48, 0, :], t["norm_g"].rearrange("a b (k n) -> (a b k) n", n=P))
        load(rows[48:64, 0, :], flat(t["ffn1_norm_2"]))
        load(rows[64:80, 0, :], flat(t["mix_norm_2"]))
        load(rows[80:96, 0, :], flat(t["ffn2_norm_2"]))
        load(rows[96:104, 0, :], t["kv_norm_2"].rearrange("(k n) -> k n", n=P))
        load(rows[104:128, 0, :], t["conv_w_2"].rearrange("a b (k n) -> (a b k) n", n=P))
        load(rows[0:8, 1, :], flat(t["hg_lb_logits"]))
        for half in range(2):
            c = slice(half * DH, (half + 1) * DH)
            load(rows[8:9, 1, c], t["fox_q_norm_g"])
            load(rows[9:10, 1, c], t["fox_k_norm_g"])
            load(rows[10:11, 1, c], t["attn_q_norm_2"])
            load(rows[11:14, 1, c], t["k_norm_2"])
        load(rows[14:46, 1, 0:DH], t["cmp_pe_k_2"])
        load(rows[14:46, 1, DH:P], t["cmp_pe_v_2"])
        load(self.masks[:], t["c_masks"])
        load(self.rowmask[:], t["c_rowmask"])
        og = t["hg_out_norm_g"]
        load(self.og, bass.AP(tensor=og.tensor, offset=og.offset, ap=[[0, P], [1, P]]))
        last = load(self.x[:], x)
        self.x_ready = [last, last]
        self.x_half = [[last, last], [last, last]]
        self.par = 1
        for piece in range(2):
            self.pop_next(piece)
            self.w_ready[0][piece] = self.split_lo[piece]
        self.par = 0
        pe.wait(last)
        pe.eng.transpose(self.tr[0][:, 0:P], rows[:, 0, :], self.ident[:])
        p = pe.mark(pe.eng.transpose(self.tr[0][:, P:G_ROWS], rows[0:G_ROWS - P, 1, :],
                                     self.ident[0:G_ROWS - P, 0:G_ROWS - P]))
        act.wait(p)
        self.gains_at = act.mark(act.eng.activation(self.gains[:], self.tr[0][:, 0:G_ROWS], ACT.Copy))
        dve.wait(self.gains_at)
        pe.wait(self.gains_at)
        logit = self.gains[:, G_LB:G_LB + KT]
        e, r, lb, om = self.small[:, 0, 0, 0:KT], self.small[:, 0, 1, 0:KT], self.lbs[:, 0], self.lbs[:, 1]
        p = self.tt(e, logit, logit, ALU.subtract, self.gains_at)
        p = self.a(e, e, ACT.Exp, p)
        dve.wait(p)
        p = dve.mark(dve.eng.reciprocal(r, e))
        p = self.tt(e, e, r, ALU.mult, p)
        p = self.tt(lb, e, e, ALU.subtract, p)
        self.lb_at = self.ts(om, lb, -1.0, 1.0, ALU.mult, ALU.add, p)

    def end(self):
        sp = self.sp
        sp.wait(*self.x_ready)
        out = self.t["out"].rearrange("o (t p) d -> p (o t) d", p=P)
        done = self.stored.mark(sp.eng.dma_start(out, self.x[:]))
        sp.wait(done)
        sp.flush()

    def chunks_of(self, stage):
        t = self.t
        kind = stage[0]
        if kind == "ffn":
            return [(self.ffn_src(stage[1], 0), CW)]
        return self.MIXER_CHUNKS[kind](self)

    MIXER_CHUNKS = {"conv": conv_chunks, "hgrn": hgrn_chunks, "fox": fox_chunks, "kv": kv_chunks,
                    "nsa": nsa_chunks}
    MIXERS = {"conv": conv, "hgrn": hgrn, "fox": fox, "kv": kv, "nsa": nsa}

    def run(self, stages):
        self.queue = [c for s in stages for c in self.chunks_of(s)]
        self.begin(stages)
        for s, following in zip(stages, stages[1:] + [None]):
            if s[0] == "ffn":
                if following == ("kv",):
                    self.tasks = self.kv_prepare()
                self.ffn(*s[1:])
            else:
                self.MIXERS[s[0]](self)
        assert not self.queue, len(self.queue)
        self.end()


def rel_tables():
    n = np.arange(T)
    nf = np.maximum(n, 1).astype(np.float32)
    large = MAX_EXACT + (np.log(nf / np.float32(MAX_EXACT)) / np.float32(np.log(MAX_DISTANCE / MAX_EXACT))
                         * np.float32(N_BUCKETS - MAX_EXACT)).astype(np.int32)
    bucket = np.where(n < MAX_EXACT, n, np.minimum(large, N_BUCKETS - 1))
    tables = np.zeros((2, REL_ROWS, REL_W), np.float32)
    for which, rel in enumerate((np.arange(REL_W) - T, T - 1 - np.arange(REL_W))):
        row = np.where(rel < 0, N_BUCKETS, bucket[np.clip(rel, 0, T - 1)])
        tables[which, row, np.arange(REL_W)] = 1.0
    return tables


def constants():
    i = np.arange(P)
    s, t = i[:, None], i[None, :]
    masks = [s == t]
    m = 1
    while m < P:
        masks.append((s // (2 * m) == t // (2 * m)) & (s % (2 * m) < m) & (t % (2 * m) >= m))
        m *= 2
    causal = np.zeros((P, 2, P), np.float32)
    causal[:, 1] = np.where(t > s, NEG, 0.0)
    select = np.zeros((P, FOX_HEADS, P), np.float32)
    select[np.arange(FOX_HEADS), np.arange(FOX_HEADS)] = 1.0
    rowmask = np.ones((P, NT + 8), np.float32)
    rowmask[:CMP_BLOCK - 1, 0] = 0.0
    rowmask[:, NT:] = i[:, None] // NB_CMP == np.arange(8)
    return {
        "c_ident": np.eye(P, dtype=np.float32),
        "c_masks": np.stack(masks, 1).astype(np.int32),
        "c_upto": (s <= t).astype(np.float32),
        "c_causal": causal,
        "c_select": select,
        "c_rel": rel_tables(),
        "c_rowmask": rowmask,
    }


def build(nc, t, stages=None):
    with ExitStack() as stack:
        k = Kernel(nc, stack, t)
        if stages is None:
            stages = all_stages(t)
        k.run(stages)


def all_stages(t):
    f_in, f_out = t["ffn_w_in"], t["ffn_w_out"]
    i1, o1, i2, o2 = t["ffn1_w_in_2"], t["ffn1_w_out_2"], t["ffn2_w_in_2"], t["ffn2_w_out_2"]
    return [
        ("ffn", f_in[0, 0], f_out[0, 0], G_NORM),
        ("hgrn",),
        ("ffn", f_in[0, 1], f_out[0, 1], G_NORM + 16),
        ("ffn", f_in[1, 0], f_out[1, 0], G_NORM + 24),
        ("fox",),
        ("ffn", f_in[1, 1], f_out[1, 1], G_NORM + 40),
        ("ffn", i1[0], o1[0], G_FFN1),
        ("conv",),
        ("ffn", i2[0], o2[0], G_FFN2),
        ("kv",),
        ("ffn", i1[1], o1[1], G_FFN1 + 8),
        ("nsa",),
        ("ffn", i2[1], o2[1], G_FFN2 + 8),
    ]


NAMES = [
    "x", "norm_g", "ffn_w_in", "ffn_w_out", "hg_w_in", "hg_lb_logits", "hg_out_norm_g", "hg_w_out",
    "fox_w_in", "fox_b_f", "fox_q_norm_g", "fox_k_norm_g", "fox_w_out", "ffn1_norm_2", "ffn1_w_in_2",
    "ffn1_w_out_2", "mix_norm_2", "ffn2_norm_2", "ffn2_w_in_2", "ffn2_w_out_2", "conv_w_in_2",
    "conv_w_2", "conv_w_out_2", "attn_w_q_2", "attn_q_norm_2", "attn_w_o_2", "kv_norm_2", "w_kv_2",
    "k_norm_2", "cmp_pe_k_2", "cmp_pe_v_2", "cmp_w1_k_2", "cmp_w2_k_2", "cmp_w1_v_2", "cmp_w2_v_2",
    "rel_bias_2",
]


def kernel(**inputs):
    import concourse.bacc as bacc
    from concourse.bass_utils import run_bass_kernel_spmd

    nc = bacc.Bacc("TRN2", target_bir_lowering=False, num_devices=1)
    arrays = {name: np.ascontiguousarray(inputs[name]) for name in NAMES}
    arrays.update(constants())
    t = {name: nc.dram_tensor(name, a.shape, mybir.dt.from_np(a.dtype), kind="ExternalInput").ap()
         for name, a in arrays.items()}
    t["out"] = nc.dram_tensor("out", (1, T, D), F32, kind="ExternalOutput").ap()
    build(nc, t)
    r = run_bass_kernel_spmd(nc, [arrays], core_ids=[0])
    return r.results[0]["out"]
```

```python
from contextlib import ExitStack

import numpy as np

import concourse.bass as bass
import concourse.mybir as mybir
from concourse.alu_op_type import AluOpType as ALU

ACT = mybir.ActivationFunctionType
AX = mybir.AxisListType
F32 = mybir.dt.float32
F32R = mybir.dt.float32r
I32 = mybir.dt.int32

P = 128
D = 1024
KT = D // P
T = 256
NT = T // P
D_FF = 2816
FC = 256
NCH = D_FF // FC
CW = 512
EPS = 1e-6
NEG = -1e30
MIN_GATE = 1e-30

HG_HEADS = 8
FOX_HEADS = NSA_HEADS = 16
DH = 64
GROUPS = 4
CMP_BLOCK, CMP_STRIDE = 32, 16
NC_CMP = (T - CMP_BLOCK) // CMP_STRIDE + 1
NB_CMP = CMP_STRIDE
N_BUCKETS, MAX_EXACT, MAX_DISTANCE = 32, 16, 4096
REL_ROWS = N_BUCKETS + 1
REL_W = 512
ARENA = 14336

G_NORM = 0
G_FFN1, G_MIX, G_FFN2 = 48, 64, 80
G_KV = 96
G_CONV = 104
G_LB = 128
G_FOXQ, G_FOXK, G_NSAQ, G_KN = 136, 137, 138, 139
G_PE = 142
G_ROWS = 174


class Loop:

    def __init__(self, n, per):
        self.n, self.per, self.var = n, per, None


class Point:

    def __init__(self, counter, k, loop):
        self.counter, self.k, self.loop = counter, k, loop


class Counter:

    def __init__(self, prog, name, step=1):
        self.prog, self.step, self.n = prog, step, 0
        self.sem = prog.stack.enter_context(prog.nc.semaphore(name))
        self.name = name
        prog.counters.append(self)

    def mark(self, ins):
        ins.then_inc(self.sem, self.step)
        self.n += 1
        return Point(self, self.n, self.prog.loop)


class Engine:

    def __init__(self, prog, eng, name):
        self.prog, self.queue, self.done = prog, eng, Counter(prog, "done_" + name)
        self.met, self.pending = {}, {}

    def mark(self, ins):
        return self.done.mark(ins)

    def wait(self, *points, fixed=False):
        cur = self.prog.loop
        for p in points:
            if p is None:
                continue
            c, k = p.counter, p.k
            if p.loop is not None and p.loop is not cur:
                k += (p.loop.n - 1) * p.loop.per.get(c.name, 0)
            moves = cur is not None and not fixed and cur.per.get(c.name, 0) > 0
            if not moves and self.met.get(c.name, 0) >= k:
                continue
            before = self.pending.get(c)
            assert before is None or before[0] == moves, c.name
            self.pending[c] = (moves, max(k, before[1] if before else 0))

    def flush(self):
        return self.eng

    @property
    def eng(self):
        cur = self.prog.loop
        for c, (moves, k) in self.pending.items():
            if moves:
                self.queue.wait_ge(c.sem, (cur.var * cur.per[c.name] + k) * c.step)
            else:
                self.queue.wait_ge(c.sem, k * c.step)
                self.met[c.name] = k
        self.pending = {}
        return self.queue


class Program:
    def __init__(self, nc, stack):
        self.nc, self.stack, self.loop, self.counters = nc, stack, None, []
        self.pe = Engine(self, nc.tensor, "pe")
        self.act = Engine(self, nc.scalar, "act")
        self.dve = Engine(self, nc.vector, "dve")
        self.sp = Engine(self, nc.sync, "sp")
        self.pool = Engine(self, nc.gpsimd, "pool")

    def repeat(self, n, per, body):
        et = mybir.EngineType
        start = {c.name: c.n for c in self.counters}
        self.loop = Loop(n, per)
        with self.nc.Fori(0, n, engines=(et.Activation, et.PE, et.DVE, et.SP)) as i:
            self.loop.var = i
            body(i)
        for c in self.counters:
            grown = c.n - start[c.name]
            assert grown == per.get(c.name, 0), (c.name, grown)
            c.n += (n - 1) * grown
        self.loop = None


class Kernel:
    def __init__(self, nc, stack, t):
        self.nc, self.stack, self.t = nc, stack, t
        g = self.g = Program(nc, stack)
        self.pe, self.act, self.dve, self.sp, self.pool = g.pe, g.act, g.dve, g.sp, g.pool
        sb = self.sb
        self.x = sb("x_tok", [P, NT, D])
        self.xt_hi = sb("xt_hi", [P, KT, T], F32R)
        self.xt_lo = sb("xt_lo", [P, KT, T], F32R)
        self.xg = sb("xt_full", [P, 2, CW])
        self.raw = sb("raw_in", [P, 2, KT // 2, CW])
        self.raw_out = sb("raw_out", [P, FC // P, D])
        self.w_hi = sb("w_hi", [P, 2, KT, CW], F32R)
        self.w_lo = sb("w_lo", [P, 2, KT, CW], F32R)
        self.wo_hi = sb("wo_hi", [P, FC // P, D], F32R)
        self.wo_lo = sb("wo_lo", [P, FC // P, D], F32R)
        self.silu = sb("silu", [P, NT, FC])
        self.h = sb("h_tok", [P, NT, FC])
        self.ht_hi = sb("ht_hi", [P, FC // P * NT, P], F32R)
        self.ht_lo = sb("ht_lo", [P, FC // P * NT, P], F32R)
        self.ident = sb("ident", [P, P])
        self.gains = sb("gains", [P, G_ROWS])
        self.rstd = sb("rstd", [P, NT])
        self.diag = sb("diag", [P, NT, P])
        self.sq_junk = sb("sq_junk", [P, CW])
        self.hn = sb("row_sums", [P, NT, 8])
        self.masks = sb("masks", [P, 7, P], I32)
        self.kct2 = sb("compressed_keys", [P, GROUPS, 2 * NB_CMP])
        self.rowmask = sb("rowmask", [P, NT + 8])
        self.og = sb("hg_gain", [P, P])[:]
        self.lbs = sb("lower_bound", [P, 2, KT])
        self.arena = sb("arena", [P, ARENA])
        self.small = sb("small", [P, 2, 5, 16])
        self.bank = [self.ps(f"bank{t}", [P, CW]) for t in range(2)]
        self.acc = [self.ps(f"acc{i}", [P, CW]) for i in range(4)]
        self.tr = [self.ps(f"tr{i}", [P, CW]) for i in range(2)]
        self.landed = [Counter(g, f"landed_{n}", 16) for n in ("a", "b", "out")]
        self.x_in = [Counter(g, f"x_in{i}", 16) for i in range(NT)]
        self.first_in = Counter(g, "first_in", 16)
        self.consts_in = Counter(g, "consts_in", 16)
        self.arena_in = Counter(g, "arena_in", 16)
        self.rel_in = Counter(g, "rel_in", 16)
        self.scratch = Counter(g, "scratch", 16)
        self.stored = Counter(g, "stored", 16)
        self.split_hi = [None, None, None]
        self.split_lo = [None, None, None]
        self.used = [None, None]
        self.w_ready = [[None, None], [None, None]]
        self.used_out = None
        self.par = 0
        self.bank_free = [None, None]
        self.acc_free = [None] * 4
        self.tr_free = [None, None]
        self.queue = []
        self.tasks = []
        self.splits = []
        self.fill = None
        self.x_ready, self.x_half = [None, None], [[None, None], [None, None]]

    def sb(self, name, shape, dt=F32):
        return self.stack.enter_context(self.nc.sbuf_tensor(name, shape, dt))

    def ps(self, name, shape):
        return self.stack.enter_context(self.nc.psum_tensor(name, shape, F32))

    def area(self, at, *shape, parts=P):
        n = int(np.prod(shape))
        assert at + n <= ARENA
        v = self.arena[0:parts, at:at + n]
        if len(shape) == 2:
            v = v.rearrange("p (a b) -> p a b", a=shape[0])
        elif len(shape) == 3:
            v = v.rearrange("p (a b c) -> p a b c", a=shape[0], b=shape[1])
        elif len(shape) == 4:
            v = v.rearrange("p (a b c d) -> p a b c d", a=shape[0], b=shape[1], c=shape[2])
        return v

    def a(self, out, src, func, *after, **kw):
        self.act.wait(*after)
        return self.act.mark(self.act.eng.activation(out, src, func, **kw))

    def tt(self, out, x, y, op, *after):
        self.dve.wait(*after)
        return self.dve.mark(self.dve.eng.tensor_tensor(out, x, y, op))

    def ts(self, out, x, s1, s2, op0, op1, *after):
        self.dve.wait(*after)
        if op1 is None:
            return self.dve.mark(self.dve.eng.tensor_scalar(out, x, s1, None, op0))
        return self.dve.mark(self.dve.eng.tensor_scalar(out, x, s1, s2, op0, op1))

    def stt(self, out, x, s, y, op0, op1, *after):
        self.dve.wait(*after)
        return self.dve.mark(self.dve.eng.scalar_tensor_tensor(out, x, s, y, op0, op1))

    def red(self, out, x, op, *after, **kw):
        self.dve.wait(*after)
        return self.dve.mark(self.dve.eng.tensor_reduce(out, x, AX.X, op, **kw))

    def mm(self, out, lhs, rhs, *after, start=True, stop=True):
        self.pe.wait(*after)
        return self.pe.mark(self.pe.eng.matmul(out, lhs, rhs, start=start, stop=stop))

    def split_piece(self, s, dst_hi, dst_lo, raw, parts, free, by_tile=False):
        act, dve, sp = self.act, self.dve, self.sp
        sp.wait(self.split_lo[s])
        for to, src in parts:
            landed = self.landed[s].mark(sp.eng.dma_start(to(raw), src))

        def split(hi, lo, r):
            act.wait(landed, free)
            self.split_hi[s] = act.mark(act.eng.activation(hi, r, ACT.Copy))
            dve.wait(self.split_hi[s])
            self.split_lo[s] = dve.mark(dve.eng.tensor_tensor(lo, r, hi.bitcast(F32), ALU.subtract))

        n = raw.shape[1]
        if by_tile:
            return [lambda k=k: split(dst_hi[:, k], dst_lo[:, k], raw[:, k]) for k in range(n)]
        split(dst_hi, dst_lo, raw)

    def prefetch(self, piece, par, parts, w=CW):
        sl = (slice(None), par, slice(piece * KT // 2, (piece + 1) * KT // 2), slice(0, w))
        self.splits = self.split_piece(piece, self.w_hi[sl], self.w_lo[sl], self.raw[:, piece, :, 0:w], parts,
                                       self.used[par], by_tile=bool(self.fill)) or []

    def prefetch_out(self, src, by_tile=False):
        return self.split_piece(2, self.wo_hi[:], self.wo_lo[:], self.raw_out[:], [(lambda r: r, src)],
                                None if by_tile else self.used_out, by_tile)

    def ffn_src(self, w_in, c):
        v = w_in.rearrange("(k p) (g n) -> p k g n", p=P, g=2)
        if not isinstance(c, int):
            c = self.sp.queue.snap(c)
        return lambda piece: [
            (lambda r, g=g: r[:, :, g * FC:(g + 1) * FC],
             v[:, piece * KT // 2:(piece + 1) * KT // 2, g, bass.ds(c * FC, FC)]) for g in range(2)]

    def mat_src(self, w, c0, wd=CW):
        v = w.rearrange("(k p) n -> p k n", p=P)
        return lambda piece: [(lambda r: r, v[:, piece * KT // 2:(piece + 1) * KT // 2, c0:c0 + wd])]

    def kv_pair_src(self, w):
        v = w.rearrange("(k p) (b g d) -> p k b g d", p=P, b=6, g=GROUPS)
        return lambda piece: [
            (lambda r, b=b, k=k: r.rearrange("p k (g b d) -> p k b g d", g=GROUPS, b=2)[:, k, b],
             v[:, piece * KT // 2 + k, b]) for b in range(2) for k in range(KT // 2)]

    def product(self, par, t, w=CW, feature_major=False, b=None):
        pe = self.pe
        b = t if b is None else b
        if self.fill:
            self.fill()
        pe.wait(self.bank_free[b])
        out = self.bank[b]
        w_hi, w_lo = self.w_hi[:, par], self.w_lo[:, par]

        def operands(half):
            pe.wait(self.w_ready[par][half])
            for tile in ((0, 1) if feature_major else (t,)):
                pe.wait(*self.xt_ready[tile][2 * half:2 * half + 2], fixed=True)

        tok = slice(t * P, (t + 1) * P)
        for f in range(2 if feature_major else 1):
            c = slice((2 * t + f) * P, (2 * t + f + 1) * P)
            for k in range(KT):
                if self.fill and k:
                    self.fill()
                    if k % 2 and self.splits:
                        self.splits.pop(0)()
                if f == 0 and k % 4 == 0:
                    operands(k // 4)
                mm = pe.eng.matmul
                first, end = k == 0, k == KT - 1
                if feature_major:
                    o = out[:, f * T:(f + 1) * T]
                    mm(o, w_hi[:, k, c], self.xt_hi[:, k, :], start=first, stop=False)
                    mm(o, w_hi[:, k, c], self.xt_lo[:, k, :], start=False, stop=False)
                    last = mm(o, w_lo[:, k, c], self.xt_hi[:, k, :], start=False, stop=end)
                else:
                    o = out[:, 0:w]
                    mm(o, self.xt_hi[:, k, tok], w_hi[:, k, 0:w], start=first, stop=False)
                    mm(o, self.xt_hi[:, k, tok], w_lo[:, k, 0:w], start=False, stop=False)
                    last = mm(o, self.xt_lo[:, k, tok], w_hi[:, k, 0:w], start=False, stop=end)
        return pe.mark(last)

    def pop_next(self, piece):
        popped = bool(self.queue)
        if popped:
            src, w = self.queue[0]
            self.prefetch(piece, 1 - self.par, src(piece), w)
            if piece == 1:
                self.queue.pop(0)
        return popped

    def chunk(self, read, w=CW, feature_major=False, between=None, b=None):
        for t in range(2):
            popped = self.pop_next(t)
            point = self.product(self.par, t, w, feature_major, b)
            while self.splits:
                self.splits.pop(0)()
            if popped:
                self.w_ready[1 - self.par][t] = self.split_lo[t]
            if t == 0 and between:
                between()
            read(t, point)
        self.used[self.par] = point
        self.par = 1 - self.par

    def narrow_views(self, w):
        v = lambda a: a[:].rearrange("p a b -> p (a b)")[:, 0:KT * w].rearrange("p (k n) -> p k n", k=KT)
        return v(self.wo_hi), v(self.wo_lo), v(self.raw_out)

    def narrow_load(self, src, w):
        hi, lo, raw = self.narrow_views(w)
        self.split_piece(2, hi, lo, raw, [(lambda r: r, src.rearrange("(k p) n -> p k n", p=P))], self.used_out)

    def narrow_product(self, w):
        pe, (hi, lo, _) = self.pe, self.narrow_views(w)
        pe.wait(self.bank_free[0], self.split_lo[2], *self.xt_ready[0], *self.xt_ready[1])
        o, mm = self.bank[0][0:w, 0:T], pe.eng.matmul
        for k in range(KT):
            mm(o, hi[:, k], self.xt_hi[:, k, :], start=(k == 0), stop=False)
            mm(o, hi[:, k], self.xt_lo[:, k, :], start=False, stop=False)
            last = mm(o, lo[:, k], self.xt_hi[:, k, :], start=False, stop=(k == KT - 1))
        self.used_out = pe.mark(last)
        return self.used_out

    def squares(self, t):
        for half in range(2):
            self.sq_at[t] = self.a(self.sq_junk[:], self.x[:, t, half * CW:(half + 1) * CW], ACT.Square,
                                   self.x_half[t][half], self.sq_junk_at, self.sq_free,
                                   accum_out=self.hn[:, t, half:half + 1])
            self.sq_junk_at = self.sq_at[t]

    def rms(self, t):
        sums = self.hn[:, t]
        q = self.ts(sums[:, 2:3], sums[:, 0:1], 1.0 / D, EPS, ALU.mult, ALU.add, self.sq_at[t])
        p = self.a(sums[:, 3:4], sums[:, 1:2], ACT.Sqrt, q, scale=1.0 / D, bias=sums[:, 2:3])
        self.dve.wait(p)
        return self.dve.mark(self.dve.eng.reciprocal(self.rstd[:, t:t + 1], sums[:, 3:4]))

    def norm(self, t):
        self.squares(t)
        return self.ts(self.diag[:, t, :], self.ident[:], self.rstd[:, t:t + 1], None, ALU.mult, None,
                       self.rms(t), self.diag_free[t])

    def to_xt(self, src, gain=None, normed=False, deferred=False, ready=None):
        pe = self.pe
        self.xt_ready = [[], []]
        free = self.used[1 - self.par]
        turned, scaled, hi_at = {}, {}, {}
        diag_at = [None, None]
        halves = range(2)
        place = lambda xt, t, half: xt[:, 4 * half:4 * half + 4, t * P:(t + 1) * P]
        if normed:
            self.a(self.hn[:, 0, 4:5], self.ident[:, 0:1], ACT.Sqrt, self.warm_at)
            ready = self.x_half

        def turn(t, half):
            pe.wait(ready[t][half], self.tr_free[half], diag_at[t])
            for k in range(4):
                lhs, o = src(t, 4 * half + k), self.tr[half][:, k * P:(k + 1) * P]
                if diag_at[t]:
                    ins = pe.eng.matmul(o, lhs, self.diag[:, t, :], start=True, stop=True)
                else:
                    ins = pe.eng.transpose(o, lhs, self.ident[:])
            self.src_read = turned[t, half] = pe.mark(ins)
            if diag_at[t]:
                self.diag_free[t] = self.src_read

        def scale(t, half):
            if gain is None:
                scaled[t, half] = self.tr[half][:].rearrange("p (k n) -> p k n", k=4), turned[t, half]
                return
            g = self.gains[:, gain + 4 * half:gain + 4 * half + 4].unsqueeze(2).to_broadcast([P, 4, P])
            o = self.xg[:, half, :].rearrange("p (k n) -> p k n", k=4)
            self.tr_free[half] = self.tt(o, self.tr[half][:].rearrange("p (k n) -> p k n", k=4), g, ALU.mult,
                                         turned[t, half], self.xg_free[half])
            scaled[t, half] = o, self.tr_free[half]

        def hi(t, half):
            v, at = scaled[t, half]
            hi_at[t, half] = self.a(place(self.xt_hi, t, half), v, ACT.Copy, at, free)

        def lo(t, half):
            v, at = scaled[t, half]
            h = place(self.xt_hi, t, half)
            p = self.tt(place(self.xt_lo, t, half), v, h.bitcast(F32), ALU.subtract, at, hi_at[t, half], free)
            if gain is not None:
                self.xg_free[half] = p
            else:
                self.tr_free[half] = p
            self.xt_ready[t] += [hi_at[t, half], p]

        for t in range(NT):
            if normed and not deferred and t == 0:
                diag_at[0] = self.norm(0)
            if normed and deferred:
                self.squares(t)
            for half in halves:
                turn(t, half)
            for half in halves:
                scale(t, half)
            if normed and not deferred and t == 0:
                diag_at[1] = self.norm(1)
            for half in halves:
                hi(t, half)
            for half in halves:
                lo(t, half)
            if self.splits:
                for part in self.splits:
                    part()
                self.splits = []
                self.w_ready[0][1] = self.split_lo[1]
        if normed and deferred:
            self.rstd_at = [self.rms(t) for t in range(NT)]
            self.warm_at = None

    def take_task(self):
        if self.tasks:
            self.tasks.pop(0)()

    def finish_tasks(self):
        self.fill = None
        while self.tasks:
            self.tasks.pop(0)()

    def x_tile(self, t, k):
        return self.x[:, t, k * P:(k + 1) * P]

    def ffn(self, w_in, w_out, gain, prepare=None):
        pe, act, dve = self.pe, self.act, self.dve
        self.to_xt(self.x_tile, gain=gain, normed=True, deferred=True)
        if prepare:
            self.tasks += prepare(self)
        rstd_at = self.rstd_at
        w_out_v = w_out.rearrange("(c k p) n -> c p k n", p=P, k=FC // P)
        h_at = [None, None]
        state = {"turned": None}

        def read(t, point):
            act.wait(point)
            act.wait(rstd_at[t], fixed=True)
            act.wait(self.h_at[t])
            s = act.mark(act.eng.activation(self.silu[:, t, :], self.bank[t][:, 0:FC], ACT.Silu,
                                            scale=self.rstd[:, t:t + 1]))
            dve.wait(s, state["turned"])
            self.h_at[t] = dve.mark(dve.eng.scalar_tensor_tensor(
                self.h[:, t, :], self.bank[t][:, FC:2 * FC], self.rstd[:, t:t + 1], self.silu[:, t, :],
                ALU.mult, ALU.mult))
            self.bank_free[t] = self.h_at[t]

        def turn():
            pe.wait(*self.h_at, self.tr_free[0])
            for f in range(FC // P):
                for t in range(NT):
                    i = f * NT + t
                    ins = pe.eng.transpose(self.tr[0][:, i * P:(i + 1) * P],
                                           self.h[:, t, f * P:(f + 1) * P], self.ident[:])
            state["turned"] = pe.mark(ins)
            full = self.tr[0][:].rearrange("p (i n) -> p i n", n=P)
            act.wait(state["turned"], self.used_out)
            self.ht_hi_at = act.mark(act.eng.activation(self.ht_hi[:], full, ACT.Copy))
            dve.wait(self.ht_hi_at)
            self.ht_at = dve.mark(dve.eng.tensor_tensor(self.ht_lo[:], full, self.ht_hi[:].bitcast(F32),
                                                        ALU.subtract))
            self.tr_free[0] = self.ht_at

        def second(c, start, stop):
            pe.wait(self.ht_at, self.split_lo[2])
            for t in range(NT):
                for half in range(2):
                    a = 2 * t + half
                    if start:
                        pe.wait(self.acc_free[a])
                    cols = slice(half * CW, (half + 1) * CW)
                    for f in range(FC // P):
                        i = f * NT + t
                        mm = pe.eng.matmul
                        mm(self.acc[a][:], self.ht_hi[:, i, :], self.wo_hi[:, f, cols],
                           start=(start and f == 0), stop=False)
                        mm(self.acc[a][:], self.ht_hi[:, i, :], self.wo_lo[:, f, cols], start=False, stop=False)
                        ins = mm(self.acc[a][:], self.ht_lo[:, i, :], self.wo_hi[:, f, cols], start=False,
                                 stop=(stop and f == FC // P - 1))
                    if stop:
                        self.acc_at[a] = pe.mark(ins)
            self.used_out = self.acc_at[3] if stop else pe.mark(ins)

        def body(c, start=False):
            if not isinstance(c, int):
                c = self.sp.queue.snap(c)
            self.prefetch_out(w_out_v[c] if isinstance(c, int) else w_out_v[bass.ds(c, 1)].rearrange(
                "c p k n -> (c p) k n"))
            self.chunk(read, between=turn)
            second(c, start, False)

        self.acc_at = [None] * 4
        self.queue.insert(0, (self.ffn_src(w_in, 1), CW))
        self.h_at = list(self.h_at_prev)
        self.fill = self.take_task if self.tasks else None
        self.chunk(read)
        self.finish_tasks()
        self.queue.insert(0, (self.ffn_src(w_in, 2), CW))
        body(0, start=True)

        per = {"done_act": 2 * 6, "done_dve": 2 * 6, "done_pe": 2 * 4,
               "landed_a": 4, "landed_b": 4, "landed_out": 2}

        def two(i):
            for j in range(2):
                c = i * 2 + (1 + j)
                self.queue.insert(0, (self.ffn_src(w_in, c + 2), CW))
                body(c)

        self.g.repeat((NCH - 3) // 2, per, two)
        self.prefetch_out(w_out_v[NCH - 2])
        self.chunk(read, between=turn)
        split_last = self.prefetch_out(w_out_v[NCH - 1], by_tile=True)
        whole, ready = [self.ht_at, self.split_lo[2]], [None, None]
        for c in (NCH - 2, NCH - 1):
            for f in range(FC // P):
                pe.wait(*(whole if c == NCH - 2 else ready[f:f + 1]))
                for a in range(4):
                    t, cols = a // 2, slice(a % 2 * CW, (a % 2 + 1) * CW)
                    i, end = f * NT + t, c == NCH - 1 and f == 1
                    mm = pe.eng.matmul
                    mm(self.acc[a][:], self.ht_hi[:, i, :], self.wo_hi[:, f, cols], start=False, stop=False)
                    mm(self.acc[a][:], self.ht_hi[:, i, :], self.wo_lo[:, f, cols], start=False, stop=False)
                    ins = mm(self.acc[a][:], self.ht_lo[:, i, :], self.wo_hi[:, f, cols], start=False, stop=end)
                    if end:
                        self.acc_at[a] = pe.mark(ins)
                if c == NCH - 1:
                    continue
                read_at = pe.mark(ins)
                pe.wait(*self.h_at, self.tr_free[f])
                for t in range(NT):
                    ins = pe.eng.transpose(self.tr[f][:, t * P:(t + 1) * P], self.h[:, t, f * P:(f + 1) * P],
                                           self.ident[:])
                turned = state["turned"] = pe.mark(ins)
                act.wait(read_at)
                split_last[f]()
                full = self.tr[f][:, 0:T].rearrange("p (i n) -> p i n", n=P)
                pair = slice(f * NT, (f + 1) * NT)
                hi_at = self.a(self.ht_hi[:, pair], full, ACT.Copy, turned)
                ready[f] = self.tr_free[f] = self.tt(self.ht_lo[:, pair], full, self.ht_hi[:, pair].bitcast(F32),
                                                     ALU.subtract, hi_at)
        self.used_out = self.acc_at[3]
        self.h_at_prev = list(self.h_at)
        for t in range(NT):
            for half in range(2):
                cols, a = slice(half * CW, (half + 1) * CW), 2 * t + half
                self.x_done(t, half, self.stt(self.x[:, t, cols], self.acc[a][:], 0.5, self.x[:, t, cols],
                                              ALU.mult, ALU.add, self.acc_at[a], self.src_read, self.sq_at[t]))
                self.acc_free[a] = self.x_ready[t]

    def x_done(self, t, half, point):
        self.x_half[t][half] = self.x_ready[t] = point

    def out_projection(self):
        for c in range(D // CW):
            def read(t, point):
                cols = slice(c * CW, (c + 1) * CW)
                self.dve.wait(point, self.src_read, self.sq_at[t])
                self.bank_free[t] = self.dve.mark(self.dve.eng.tensor_tensor(
                    self.x[:, t, cols], self.bank[t][:], self.x[:, t, cols], ALU.add))
                self.x_done(t, c, self.bank_free[t])
            self.chunk(read)

    def conv_chunks(self):
        return [(self.mat_src(self.t["conv_w_in_2"][0], c * CW), CW) for c in (2, 3, 4, 5, 0, 1)] + [
            (self.mat_src(self.t["conv_w_out_2"][0], c * CW), CW) for c in range(D // CW)]

    def conv(self):
        self.pool.wait(*self.x_ready)
        taps = 3
        y = self.area(2048, KT, T)
        u = self.area(4096, KT, T + taps - 1)
        zero = self.pool.mark(self.pool.eng.memset(u[:, :, 0:taps - 1], 0.0))
        self.to_xt(self.x_tile, gain=G_MIX, normed=True)
        c_at, y_at, z_at = {}, {}, []
        pair = lambda v, n: v[:, 2 * n:2 * n + 2]
        banked = lambda t: self.bank[t][:].rearrange("p (f n) -> p f n", f=2)
        for i in range(2):
            def read(t, p, i=i):
                dst = pair(u, 2 * i + t)[:, :, taps - 1:]
                c_at[2 * i + t] = self.bank_free[t] = self.a(dst, banked(t), ACT.Copy, p)
            self.chunk(read, feature_major=True)
        for i in range(2):
            def read(t, p, i=i):
                n = 2 * i + t
                dst = pair(u, n)[:, :, taps - 1:]
                q = self.bank_free[t] = self.tt(dst, banked(t), dst, ALU.mult, p, c_at[n], zero)
                for f in range(2):
                    k = 2 * n + f
                    g = lambda j: self.gains[:, G_CONV + j * KT + k:G_CONV + j * KT + k + 1]
                    r = self.ts(y[:, k], u[:, k, 0:T], g(0), None, ALU.mult, None, q)
                    r = self.stt(y[:, k], u[:, k, 1:T + 1], g(1), y[:, k], ALU.mult, ALU.add, r)
                    y_at[n] = self.stt(y[:, k], u[:, k, 2:T + 2], g(2), y[:, k], ALU.mult, ALU.add, r)
            self.chunk(read, feature_major=True)
        for i in range(2):
            def read(t, p, i=i):
                n = 2 * i + t
                self.bank_free[t] = self.tt(pair(y, n), pair(y, n), banked(t), ALU.mult, p, y_at[n])
                z_at.append(self.bank_free[t])
            self.chunk(read, feature_major=True)
        his, los = [], []
        for n in range(4):
            his.append(self.a(pair(self.xt_hi, n), pair(y, n), ACT.Copy, z_at[n], self.used[1 - self.par]))
            los.append(self.tt(pair(self.xt_lo, n), pair(y, n), pair(self.xt_hi, n).bitcast(F32), ALU.subtract,
                               his[n]))
        half_at = [his[1], los[1], his[3], los[3]]
        self.xt_ready = [half_at, half_at]
        self.out_projection()

    def head_rms(self, t, src, heads, width, point, slot=0):
        sq = self.sq_junk[:, 0:heads * width]
        ss, ms, r = (self.small[:, slot, j, 0:heads] for j in range(3))
        s3 = src.rearrange("p (h d) -> p h d", h=heads)
        p = self.a(sq.rearrange("p (h d) -> p h d", h=heads), s3, ACT.Square, point, self.sq_free, self.sq_junk_at)
        p = self.red(ss, sq.rearrange("p (h d) -> p h d", h=heads), ALU.add, p, self.rms_free[slot])
        self.sq_free = p
        p = self.ts(ms, ss, 1.0 / width, EPS, ALU.mult, ALU.add, p)
        self.dve.wait(p)
        p = self.dve.mark(self.dve.eng.reciprocal(ss, ms))
        return r, self.a(r, ss, ACT.Sqrt, p)

    def turn_heads(self, t, src, dst, gain, *after):
        self.pe.wait(self.tr_free[t], *after)
        for i in range(4):
            ins = self.pe.eng.transpose(self.tr[t][:, i * P:(i + 1) * P], src(i), self.ident[:])
        p = self.pe.mark(ins)
        self.turned_at = p
        v = self.tr[t][:].rearrange("p (i n) -> p i n", i=4)
        self.tr_free[t] = self.a(dst, v, ACT.Copy, p, scale=self.gains[:, gain:gain + 1])
        return self.tr_free[t]

    def normed_heads(self, t, point, dst, dup=1, width=CW, b=None):
        n = width // DH
        b = t if b is None else b
        r, p = self.head_rms(t, self.bank[b][:, 0:width], n, DH, point, slot=t)
        src = self.bank[b][:, 0:width].rearrange("p (h d) -> p h d", h=n)
        if dup == 1:
            o, s, rr = dst.rearrange("p (h d) -> p h d", h=n), src, r.unsqueeze(2).to_broadcast([P, n, DH])
            p = self.tt(o, s, rr, ALU.mult, p)
        else:
            for j in range(dup):
                p = self.tt(dst[:, :, j, :], src, r.unsqueeze(2).to_broadcast([P, n, DH]), ALU.mult, p)
        self.rms_free[t] = self.bank_free[b] = p
        return p

    def fox_chunks(self):
        w = self.t["fox_w_in"][0]
        return ([(self.mat_src(w, c), CW) for c in (0, CW, D, D + CW)]
                + [(self.mat_src(w, c), CW) for c in (2 * D, 2 * D + CW, 3 * D, 3 * D + CW)]
                + [(self.mat_src(self.t["fox_w_out"][0], c * CW), CW) for c in range(D // CW)])

    def fox_prepare(self):
        select, causal = self.area(10240, FOX_HEADS, P), self.area(13568, T)
        nct, ones, bf = self.area(13312, T), self.area(13824, T), self.area(14176, 1)[0:FOX_HEADS]
        pool = self.pool
        self.act.wait(*self.x_ready)
        load = lambda d, s_: self.arena_in.mark(self.act.eng.dma_start(d, s_))
        load(select, self.t["c_select"])
        load(causal, self.t["c_causal"].rearrange("p a b -> p (a b)"))
        b_f = self.t["fox_b_f"]
        here = load(bf, bass.AP(tensor=b_f.tensor, offset=b_f.offset, ap=[[1, FOX_HEADS], [1, 1]]))
        pool.wait(*self.x_ready)
        pool.wait(pool.mark(pool.eng.memset(ones, 1.0)))
        set_at = pool.mark(pool.eng.memset(nct, 0.0))
        self.fox_here, self.fox_set = here, set_at
        return []

    def fox(self):
        tmp = self.area(0, NT, D)
        qt, kt = self.area(2048, KT, T), self.area(4096, KT, T)
        v, g = self.area(6144, NT, D), self.area(8192, NT, D)
        select = self.area(10240, FOX_HEADS, P)
        s_buf = self.area(12288, 2, T)
        pt = self.area(12800, 2, T)
        nct = self.area(13312, T)
        causal = self.area(13568, T)
        H = FOX_HEADS
        ones = self.area(13824, T)
        cc = self.area(14112, NT, FOX_HEADS)
        bf = self.area(14176, 1)[0:H]
        z, e = pt[0:H, 0], pt[0:H, 1]
        nm, den = self.area(14192, NT, FOX_HEADS), self.area(14224, NT, FOX_HEADS)
        pe, here, set_at = self.pe, self.fox_here, self.fox_set
        self.to_xt(self.x_tile, gain=G_NORM + 32, normed=True)
        self.narrow_load(self.t["fox_w_in"][0][:, 4 * D:4 * D + H], H)

        gq_at = self.ts(self.gains[:, G_FOXQ:G_FOXQ + 1], self.gains[:, G_FOXQ:G_FOXQ + 1], DH ** -0.5, None,
                        ALU.mult, None)
        self.act.wait(gq_at)
        last = {}
        turned = {}
        todo = []

        def turn_todo():
            while todo:
                todo.pop(0)()

        for i in range(4):
            dst_t, gain = (qt, G_FOXQ) if i < 2 else (kt, G_FOXK)

            def read(t, p, i=i, dst_t=dst_t, gain=gain):
                c = i % 2
                turn_todo()
                cols = tmp[:, t, c * CW:(c + 1) * CW]
                self.dve.wait(turned.get((i - 2, t)))
                n = self.normed_heads(t, p, cols)

                def later():
                    last[i, t] = self.turn_heads(
                        t, lambda j: tmp[:, t, c * CW + j * P:c * CW + (j + 1) * P],
                        dst_t[:, 4 * c:4 * c + 4, t * P:(t + 1) * P], gain, n)
                    turned[i, t] = self.turned_at
                todo.append(later)
            self.chunk(read)
        p = self.narrow_product(H)
        p = self.bank_free[0] = self.ts(z, self.bank[0][0:H, 0:T], bf, None, ALU.add, None, p, here)
        q = self.a(e, z, ACT.Abs, p)
        q = self.a(e, e, ACT.Exp, q, scale=-1.0)
        q = self.a(e, e, ACT.Ln, q, bias=1.0)
        self.lf_at = self.stt(z, z, 0.0, e, ALU.min, ALU.subtract, q)
        turn_todo()
        qk_at = [last[k] for k in last]

        def cumulate():
            p = self.ts(z, z, -1.0, None, ALU.mult, None, self.lf_at)
            self.dve.wait(p, set_at)
            self.nct_at = self.dve.mark(self.dve.eng.tensor_tensor_scan(nct[0:H], ones[0:H], z, 0.0, ALU.mult,
                                                                        ALU.add))
            pe.wait(self.nct_at, self.tr_free[0])
            for t in range(NT):
                ins = pe.eng.transpose(self.tr[0][:, t * H:(t + 1) * H], nct[0:H, t * P:(t + 1) * P],
                                       self.ident[0:H, 0:H])
            p = pe.mark(ins)
            self.tr_free[0] = self.cc_at = self.a(cc, self.tr[0][:, 0:NT * H].rearrange("p (t h) -> p t h", t=NT),
                                                  ACT.Copy, p, scale=-1.0)

        steps = [(h, t) for h in range(FOX_HEADS) for t in range(NT)]
        st = {}
        v_at = {}

        def scores(i):
            h, t = steps[i]
            rows, n = slice(DH * (h % 2), DH * (h % 2) + DH), (t + 1) * P
            bank, free = ((self.bank[1], self.bank_free), (self.tr[1], self.tr_free))[i % 2]
            pe.wait(free[1], self.nct_at, *qk_at)
            o = bank[:, 0:n]
            self.mm(o, qt[rows, h // 2, t * P:(t + 1) * P], kt[rows, h // 2, 0:n], start=True, stop=False)
            p = self.mm(o, select[:, h], nct[:, 0:n], start=False, stop=True)
            s = s_buf[:, i % 2, 0:n]
            p = free[1] = self.stt(s, o, cc[:, t, h:h + 1], causal[:, T - n:T], ALU.add, ALU.add,
                                                 p, self.cc_at, st.get(("turned", i - 2)))
            p = self.red(nm[:, t, h:h + 1], s, ALU.max, p, negate=True)
            st["exp", i] = self.a(s, s, ACT.Exp, p, bias=nm[:, t, h:h + 1], accum_out=den[:, t, h:h + 1])

        def turn(i):
            t = steps[i][1]
            pe.wait(st["exp", i], self.tr_free[0])
            for b in range(t + 1):
                ins = pe.eng.transpose(self.tr[0][:, b * P:(b + 1) * P],
                                       s_buf[:, i % 2, b * P:(b + 1) * P], self.ident[:])
            p = st["turned", i] = pe.mark(ins)
            n = (t + 1) * P
            st["pt", i] = self.tr_free[0] = self.a(pt[:, i % 2, 0:n], self.tr[0][:, 0:n], ACT.Copy, p,
                                                   st.get(("pv", i - 2)))

        def values(i):
            h, t = steps[i]
            a = 2 * t + h // 8
            pe.wait(st["pt", i], v_at[h // 8], self.acc_free[a])
            for b in range(t + 1):
                p = self.mm(self.acc[a][:, (h % 8) * DH:(h % 8 + 1) * DH], pt[:, i % 2, b * P:(b + 1) * P],
                            v[:, b, h * DH:(h + 1) * DH], start=(b == 0), stop=(b == t))
            st["pv", i] = p

        scaled = {}

        def step(i):
            if i < len(steps):
                scores(i)
            if 1 <= i <= len(steps):
                turn(i - 1)
            if i >= 2:
                values(i - 2)

        def normalise():
            self.dve.wait(st["exp", len(steps) - 1])
            inv_at = self.dve.mark(self.dve.eng.reciprocal(den, den))
            for t in range(NT):
                for half in range(2):
                    r = den[:, t, 8 * half:8 * half + 8].unsqueeze(2).to_broadcast([P, 8, DH])
                    o3 = tmp[:, t, half * CW:(half + 1) * CW].rearrange("p (h d) -> p h d", h=8)
                    scaled[t, half] = self.acc_free[2 * t + half] = self.tt(
                        o3, self.acc[2 * t + half][:].rearrange("p (h d) -> p h d", h=8), r, ALU.mult,
                        st["pv", len(steps) - 1], inv_at)

        o_at = {}

        def gate(t, half):
            cols = slice(half * CW, (half + 1) * CW)
            o_at[t, half] = self.tt(tmp[:, t, cols], tmp[:, t, cols], g[:, t, cols], ALU.mult,
                                    scaled[t, half], g_at[t, half])

        todo_steps = [lambda i=i: step(i) for i in range(len(steps) + 2)] + [normalise]

        def fill():
            if todo_steps:
                todo_steps.pop(0)()

        for i in range(2):
            def read(t, p, i=i):
                v_at[i] = self.bank_free[0] = self.a(v[:, t, i * CW:(i + 1) * CW], self.bank[0][:], ACT.Copy, p)
            if i == 1:
                cumulate()
                self.fill = fill
            self.chunk(read, b=0)
        g_at = {}
        for i in range(2):
            def read(t, p, i=i):
                c = g[:, t, i * CW:(i + 1) * CW]
                if i == 0:
                    g_at[t, 0] = self.bank_free[0] = self.a(c, self.bank[0][:], ACT.Copy, p)
                    return
                while todo_steps:
                    todo_steps.pop(0)()
                if t == 0:
                    for tile in range(NT):
                        c0 = g[:, tile, 0:CW]
                        g_at[tile, 0] = self.a(c0, c0, ACT.Sigmoid, g_at[tile, 0])
                g_at[t, 1] = self.bank_free[0] = self.a(c, self.bank[0][:], ACT.Sigmoid, p)
                gate(t, 0)
                gate(t, 1)
            self.chunk(read, b=0)
        self.fill = None
        self.to_xt(lambda t, k: tmp[:, t, k * P:(k + 1) * P],
                   ready=[(o_at[t, 0], o_at[t, 1]) for t in range(NT)])
        self.out_projection()

    def hgrn_chunks(self):
        w = self.t["hg_w_in"][0]
        cols = [D, D + CW, 0, CW, 2 * D, 2 * D + CW, 3 * D, 3 * D + CW]
        return [(self.mat_src(w, c), CW) for c in cols] + [
            (self.mat_src(self.t["hg_w_out"][0], c * CW), CW) for c in range(D // CW)]

    def hgrn(self):
        H = HG_HEADS
        kk, qq = self.area(2048, H, T), self.area(4096, H, T)
        v, g = self.area(6144, NT, D), self.area(8192, NT, D)
        pt = self.area(10240, 2, 3, 4 * P)
        prods = {1: self.area(0, H, T), 2: self.xg[:].rearrange("p a (h n) -> p (a h) n", h=H // 2)}
        at = 13312
        for m in (4, 8, 16, 32, 64):
            prods[m] = self.area(at, H, T // m)
            at += H * T // m
        prods_at = {}
        pool, pe, dve = self.pool, self.pe, self.dve
        pool.wait(*self.x_ready)
        pt_zero = pool.mark(pool.eng.memset(pt[:], 0.0))
        self.to_xt(self.x_tile, gain=G_NORM + 8, normed=True)
        k_at, q_at = [], []

        for i in range(2):
            def read(t, p, i=i):
                n = 2 * i + t
                src = self.bank[t][:].rearrange("p (f n) -> p f n", f=2)
                f_ = prods[1][:, 2 * n:2 * n + 2]
                p1 = self.a(f_, src, ACT.Sigmoid, p)
                p2 = self.bank_free[t] = self.a(kk[:, 2 * n:2 * n + 2], src, ACT.Sigmoid, p, scale=-1.0)
                for f in range(2):
                    h = 2 * n + f
                    lb, om = self.lbs[:, 0, h:h + 1], self.lbs[:, 1, h:h + 1]
                    p1 = self.ts(prods[1][:, h], prods[1][:, h], om, lb, ALU.mult, ALU.add, p1, self.lb_at)
                    k_at.append(self.ts(kk[:, h], kk[:, h], om, None, ALU.mult, None, p2))
                prods_at[1] = self.ts(f_, f_, MIN_GATE, None, ALU.max, None, p1)
            self.chunk(read, feature_major=True)
        for i in range(2):
            def read(t, p, i=i):
                n = 2 * i + t
                self.bank_free[t] = self.a(
                    qq[:, 2 * n:2 * n + 2], self.bank[t][:].rearrange("p (f n) -> p f n", f=2), ACT.Silu, p)
                q_at.append(self.bank_free[t])
            self.chunk(read, feature_major=True)
        dve.wait(*self.xg_free)
        ready = {(0, grp): [k_at[4 * grp + 3], q_at[2 * grp + 1]] for grp in range(2)}
        state = {"n": 0, "pt": [None, None], "cross": [None, None]}

        def scores_step(level, grp):
            hs = slice(4 * grp, 4 * grp + 4)
            m = 2 ** (level - 1) if level else 0
            n = state["n"] = state["n"] + 1
            made = []
            for tile in range(NT if level <= 7 else 1):
                a = 2 * (n % 2) + tile
                acc = self.acc[a]
                pe.wait(*ready[level, grp], self.acc_free[a])
                s0, t0, w = tile * P, tile * P, P
                if level == 7:
                    t0, w = tile * P + m, m
                elif level == 8:
                    t0 = P
                for h in range(4):
                    p = self.mm(acc[0:w, h * w:(h + 1) * w], kk[:, 4 * grp + h, s0:s0 + w],
                                qq[:, 4 * grp + h, t0:t0 + w])
                made.append((a, tile, p))
            if level < 8:
                if level == 0:
                    q = self.tt(qq[:, hs], qq[:, hs], prods[1][:, hs], ALU.mult, p, prods_at[1])
                    ready[1, grp] = [q]
                else:
                    if m > 1 and m not in prods_at:
                        pair = prods[m // 2].rearrange("p h (n u) -> p (h n) u", u=2)
                        prods_at[m] = self.tt(prods[m].rearrange("p h n -> p (h n)"), pair[:, :, 0],
                                              pair[:, :, 1], ALU.mult, prods_at[m // 2])
                    half = lambda v_, j_: v_.rearrange("p h (n u m) -> p (h n) u m", u=2, m=m)[:, :, j_]
                    nb = T // (2 * m)
                    other = lambda j_: prods[m][:, hs].rearrange("p h (n u) -> p (h n) u", u=2)[
                        :, :, j_:j_ + 1].to_broadcast([P, 4 * nb, m])
                    q0 = self.tt(half(kk[:, hs], 0), half(kk[:, hs], 0), other(1), ALU.mult, p, prods_at[m],
                                 *ready[level, grp])
                    q1 = self.tt(half(qq[:, hs], 1), half(qq[:, hs], 1), other(0), ALU.mult)
                    ready[level + 1, grp] = [q0, q1]
            for a, tile, p in made:
                if level <= 6:
                    mask = self.masks[:, level, :].unsqueeze(1).to_broadcast([P, 4, P])
                    dve.wait(p, pt_zero, state["pt"][grp])
                    q = dve.mark(dve.eng.copy_predicated(
                        pt[:, grp, tile].rearrange("p (h n) -> p h n", h=4), mask,
                        self.acc[a][:].rearrange("p (h n) -> p h n", h=4)))
                    if tile == 1:
                        state["pt"][grp] = q
                elif level == 7:
                    q = self.a(pt[0:m, grp, tile].rearrange("p (h n) -> p h n", h=4)[:, :, m:],
                               self.acc[a][0:m, 0:4 * m].rearrange("p (h n) -> p h n", h=4), ACT.Copy,
                               p, pt_zero, state["pt"][grp])
                    state["half"] = q
                else:
                    q = state["cross"][grp] = self.a(pt[:, grp, 2], self.acc[a][:], ACT.Copy, p, pt_zero)
                self.acc_free[a] = q

        sums = self.small[:, 0, 0:2].rearrange("p a n -> p (a n)")[:, 0:16]
        ms, r = self.small[:, 0, 2], self.small[:, 0, 3]
        square_at, o_at = [], {}

        def values(grp, t):
            a = 2 * grp + t
            pe.wait(state["pt"][grp], state["half"], state["cross"][grp], self.v_at, self.acc_free[a])
            for h in range(4):
                hc = slice((4 * grp + h) * P, (4 * grp + h + 1) * P)
                o = self.acc[a][:, h * P:(h + 1) * P]
                score = lambda j: pt[:, grp, j, h * P:(h + 1) * P]
                p = self.mm(o, score(t), v[:, t, hc], start=True, stop=(t == 0))
                if t == 1:
                    p = self.mm(o, score(2), v[:, 0, hc], start=False, stop=True)
            o_at[grp, t] = p
            p = self.a(self.sq_junk[:], self.acc[a][:], ACT.Square, p, self.sq_free, self.sq_junk_at)
            self.sq_free = self.red(sums[:, 4 * a:4 * a + 4], self.sq_junk[:].rearrange("p (h d) -> p h d", h=4),
                                    ALU.add, p, self.rms_free[0])
            square_at.append(self.sq_free)

        def roots():
            p = self.ts(ms, sums, 1.0 / P, EPS, ALU.mult, ALU.add, *square_at)
            dve.wait(p)
            p = dve.mark(dve.eng.reciprocal(sums, ms))
            self.root_at = self.a(r, sums, ACT.Sqrt, p)

        gated = {}

        def gate(grp, t):
            a = 2 * grp + t
            for h in range(4):
                hc, gc = slice(h * P, (h + 1) * P), slice((4 * grp + h) * P, (4 * grp + h + 1) * P)
                gated[t, grp] = self.stt(self.out_hg(grp, t)[:, hc], self.acc[a][:, hc], r[:, 4 * a + h:4 * a + h + 1],
                                         g[:, t, gc], ALU.mult, ALU.mult, o_at[grp, t], self.root_at, g_at[grp, t])
            self.acc_free[a] = self.rms_free[0] = gated[t, grp]

        todo = [lambda lv=lv, grp=grp: scores_step(lv, grp) for lv in range(9) for grp in range(2)]
        todo += [lambda grp=grp, t=t: values(grp, t) for grp in range(2) for t in range(NT)]
        todo.append(roots)
        slot = {"n": 0}

        def fill():
            slot["n"] += 1
            if slot["n"] % 2 and todo:
                todo.pop(0)()

        self.fill = fill
        for i in range(2):
            def read(t, p, i=i):
                self.v_at = self.bank_free[t] = self.a(v[:, t, i * CW:(i + 1) * CW], self.bank[t][:], ACT.Copy, p)
            self.chunk(read)
        g_at = {}
        for i in range(2):
            def read(t, p, i=i):
                c = g[:, t, i * CW:(i + 1) * CW].rearrange("p (h d) -> p h d", h=4)
                self.bank_free[t] = self.a(c, self.bank[t][:].rearrange("p (h d) -> p h d", h=4), ACT.Silu, p)
                g_at[i, t] = self.tt(c, c, self.og.unsqueeze(1).to_broadcast([P, 4, P]), ALU.mult,
                                     self.bank_free[t])
                if i == 1:
                    while todo:
                        todo.pop(0)()
                    if t == 0:
                        gate(0, 0)
                        gate(0, 1)
                    gate(1, t)
            self.chunk(read)
        self.fill = None
        self.xg_free = [g_at[1, 1], g_at[1, 1]]
        self.to_xt(lambda t, k: self.out_hg(k // 4, t)[:, (k % 4) * P:(k % 4 + 1) * P],
                   ready=[(gated[t, 0], gated[t, 1]) for t in range(NT)])
        self.out_projection()

    def out_hg(self, grp, t):
        return self.area(4096, 2, NT, CW)[:, grp, t]

    KV_T, KV_V, KV_CV, KV_CB = 0, 2048, 3136, 4160

    def kv_chunks(self):
        w = self.t["w_kv_2"]
        return [(self.kv_pair_src(w), CW)] + [(self.mat_src(w, c * CW), CW) for c in (1, 2)]

    def kv_areas(self):
        class Areas:
            pass
        a = Areas()
        a.kt = self.area(self.KV_T, 2, GROUPS, T)
        a.vv = self.area(self.KV_V, 2, NT, GROUPS * DH)
        a.vcb = self.area(self.KV_CV, 2, CW)
        a.cb = self.area(self.KV_CB, NT, NSA_HEADS, NB_CMP)
        a.w1 = self.area(4672, CMP_BLOCK, P)
        a.kv0 = self.area(8768, GROUPS, T)
        a.blk = [self.area(9792, GROUPS, T), self.area(10816, GROUPS, T)]
        a.dup = self.area(11840, 2, GROUPS, 2, DH)
        a.w2 = self.area(12864, 2, DH)
        a.hid = self.area(12992, 2, GROUPS * NC_CMP + 4)
        a.kc = self.area(13120, GROUPS, 2, DH)
        a.vc = self.area(13632, GROUPS, DH)
        a.relb = self.area(13888, NSA_HEADS)
        return a

    def kv_prepare(self):
        t_, a = self.t, self.kv_areas()
        pe, act, pool = self.pe, self.act, self.pool
        cb, w1, w2, relb = a.cb, a.w1, a.w2, a.relb
        act.wait(*self.x_ready)
        load = lambda d, s_: self.arena_in.mark(act.eng.dma_start(d, s_))
        load_rel = lambda d, s_: self.rel_in.mark(act.eng.dma_start(d, s_))
        load_rel(relb[0:N_BUCKETS], t_["rel_bias_2"])
        oh = self.area(9792, 2, REL_W)
        here = load_rel(oh[0:REL_ROWS], t_["c_rel"].rearrange("a r w -> r a w"))
        load(w1[0:DH], t_["cmp_w1_k_2"].rearrange("(j d) h -> d j h", d=DH))
        load(w1[DH:P], t_["cmp_w1_v_2"].rearrange("(j d) h -> d j h", d=DH))
        load(w2[:, 0], t_["cmp_w2_k_2"])
        self.w_cmp_at = load(w2[:, 1], t_["cmp_w2_v_2"])
        pool.wait(*self.x_ready)
        pool.wait(pool.mark(pool.eng.memset(relb[N_BUCKETS:REL_ROWS], NEG)))
        set_at = pool.mark(pool.eng.memset(self.kct2[:], 0.0))
        self.kv_set = set_at
        rb = relb[0:REL_ROWS]
        rows = self.area(8768, REL_W)
        scr = self.bias_rows = self.nc.dram_tensor("bias_rows", (P, NSA_HEADS, REL_W), F32, kind="Internal").ap()

        def by_distance():
            p = self.mm(self.acc[0][0:NSA_HEADS, :], rb, oh[0:REL_ROWS, 1], here, set_at, self.acc_free[0])
            p = self.acc_free[0] = self.a(rows[0:NSA_HEADS], self.acc[0][0:NSA_HEADS, :], ACT.Copy, p)
            act.wait(p)
            r_ap = rows[0:NSA_HEADS].unsqueeze(1).to_broadcast([NSA_HEADS, P, REL_W])
            self.bias_wrote = self.scratch.mark(act.eng.dma_start(scr.rearrange("c h w -> h c w"), r_ap))

        def by_block(t, half):
            pe.wait(here, set_at, self.acc_free[1])
            for b in range(8 * half, 8 * half + 8):
                first = T + t * P - CMP_STRIDE * b - (CMP_BLOCK - 1) if b < NC_CMP else 0
                o = self.acc[1][:].rearrange("p (t h n) -> p t n h", t=NT, h=NSA_HEADS)[:, t, b]
                self.bias_done = self.mm(o, oh[0:REL_ROWS, 0, first:first + P], rb)

        def keep():
            self.acc_free[1] = self.a(
                cb, self.acc[1][:].rearrange("p (t h n) -> p t h n", t=NT, h=NSA_HEADS), ACT.Copy, self.bias_done)

        return [lambda: None] * 8 + [by_distance] + [lambda t=t, half=half: by_block(t, half) for t in range(NT) for half in range(2)] + [keep]

    def kv(self):
        a = self.kv_areas()
        kt, vv, vcb, w1, kv0, blk, dup = a.kt, a.vv, a.vcb, a.w1, a.kv0, a.blk, a.dup
        w2, hid, kc, vc = a.w2, a.hid, a.kc, a.vc
        pe, act, dve = self.pe, self.act, self.dve
        set_at, wrote, bias_done = self.kv_set, self.bias_wrote, self.bias_done
        self.to_xt(self.x_tile, gain=G_KV, normed=True)

        def read0(t, p):
            self.kv0_at = self.bank_free[t] = self.a(
                kv0[:, 2 * t:2 * t + 2], self.bank[t][:].rearrange("p (f n) -> p f n", f=2), ACT.Copy, p, wrote)
        self.chunk(read0, feature_major=True)

        blk_at = []
        for j in range(2):
            pe_col = self.gains[:, G_PE + 16 * j:G_PE + 16 * j + 16].unsqueeze(1).to_broadcast(
                [P, GROUPS * T // 16, 16])
            blk_at.append(self.tt(blk[j].rearrange("p g (n j) -> p (g n) j", j=16),
                                  kv0.rearrange("p g (n j) -> p (g n) j", j=16), pe_col, ALU.add,
                                  self.kv0_at, bias_done))
        todo = []

        def branch(br):
            def read(t, p):
                while todo:
                    todo.pop(0)()
                self.dve.wait(self.dup_free[t], bias_done)
                self.v_pts.append(self.a(vv[:, br, t], self.bank[t][:, GROUPS * DH:CW], ACT.Copy, p))
                n = self.normed_heads(t, p, dup[:, t], dup=2, width=GROUPS * DH)

                def later():
                    self.k_pts.append(self.turn_heads(
                        t, lambda j: dup[:, t, j].rearrange("p a d -> p (a d)"),
                        kt[:, br, :, t * P:(t + 1) * P], G_KN + 1 + br, n))
                    self.dup_free[t] = self.turned_at
                todo.append(later)
            return read
        self.dup_free, self.v_pts, self.k_pts = [None, None], [], []
        for br in range(2):
            self.chunk(branch(br))
        def hidden(kv, q):
            rows_ = slice(kv * DH, (kv + 1) * DH)
            o = self.acc[2 + kv][:, 0:GROUPS * NC_CMP]
            pe.wait(*blk_at, self.w_cmp_at, self.acc_free[2 + kv])
            for j in range(8 * q, 8 * q + 8):
                b = blk[j // 16].rearrange("p g (n j) -> p g n j", j=16)
                n0 = j // 16
                p = self.mm(o.rearrange("p (g n) -> p g n", g=GROUPS), w1[rows_, j],
                            b[rows_, :, n0:n0 + NC_CMP, j % 16], start=(j == 0), stop=(j == CMP_BLOCK - 1))
            at["hidden", kv] = p

        def gelu():
            for kv in range(2):
                at["hid", kv] = self.acc_free[2 + kv] = self.a(
                    hid[:, kv, 0:GROUPS * NC_CMP], self.acc[2 + kv][:, 0:GROUPS * NC_CMP], ACT.Gelu_apprx_tanh,
                    at["hidden", kv])
            tb = self.area(4672, NSA_HEADS, T)
            scr = self.bias_rows
            act.wait(at["hid", 1], wrote)
            src = bass.AP(tensor=scr.tensor, offset=scr.offset + P - 1,
                          ap=[[NSA_HEADS * REL_W - 1, P], [REL_W, NSA_HEADS], [1, T]])
            self.tb_at = self.scratch.mark(act.eng.dma_start(tb, src))

        n = NC_CMP
        out = self.acc[0]
        rows8 = self.area(13904, 8, NB_CMP)[0:n]

        def outputs():
            pe.wait(at["hid", 0], at["hid", 1], self.acc_free[0])
            for kv in range(2):
                for g in range(GROUPS):
                    i = kv * GROUPS + g
                    p = self.mm(out[0:NC_CMP, i * DH:(i + 1) * DH], hid[:, kv, g * NC_CMP:(g + 1) * NC_CMP],
                                w2[:, kv])
            ss, ms, r = (self.small[0:n, 0, j, 0:GROUPS] for j in range(3))
            k3 = out[0:n, 0:GROUPS * DH].rearrange("p (g d) -> p g d", g=GROUPS)
            sq = self.sq_junk[0:n, 0:GROUPS * DH].rearrange("p (g d) -> p g d", g=GROUPS)
            vc_at = self.a(vc[0:n], out[0:n, GROUPS * DH:CW].rearrange("p (g d) -> p g d", g=GROUPS), ACT.Copy, p)
            q = self.a(sq, k3, ACT.Square, p, self.sq_free, self.sq_junk_at)
            q = self.red(ss, sq, ALU.add, q, self.rms_free[0])
            self.sq_free = q
            q = self.ts(ms, ss, 1.0 / DH, EPS, ALU.mult, ALU.add, q)
            dve.wait(q)
            q = dve.mark(dve.eng.reciprocal(ss, ms))
            q = self.a(r, ss, ACT.Sqrt, q)
            for j in range(2):
                q = self.tt(kc[0:n, :, j], k3, r.unsqueeze(2).to_broadcast([n, GROUPS, DH]), ALU.mult, q, p)
            self.rms_free[0] = self.acc_free[0] = at["kc"] = q
            at["vc"] = self.a(rows8, self.ident[0:n, 0:NB_CMP].unsqueeze(1).to_broadcast([n, 8, NB_CMP]), ACT.Copy, vc_at)

        def spread():
            o = self.acc[1][:, 0:GROUPS * DH]
            p = self.mm(o, rows8.rearrange("p h n -> p (h n)"), vc[0:n].rearrange("p g d -> p (g d)"), at["vc"],
                        self.acc_free[1])
            mask = self.rowmask[:, NT:NT + 8].rearrange("p (g h) -> p g h", g=2).unsqueeze(3).to_broadcast(
                [P, 2, 4, DH])
            for half in range(2):
                v4 = o.rearrange("p (g d) -> p g d", g=GROUPS)[:, 2 * half:2 * half + 2].unsqueeze(2).to_broadcast(
                    [P, 2, 4, DH])
                self.vcb_at = self.tt(vcb[:, half].rearrange("p (g h d) -> p g h d", g=2, h=4), v4, mask, ALU.mult, p)
            self.acc_free[1] = self.vcb_at

        def turn_keys():
            pe.wait(at["kc"], self.tr_free[0])
            for g in range(GROUPS):
                ins = pe.eng.transpose(self.tr[0][:, g * NB_CMP:g * NB_CMP + n],
                                       kc[0:n, g].rearrange("p a d -> p (a d)"), self.ident[0:n, 0:n])
            p = pe.mark(ins)
            for odd in range(2):
                r_, c_ = slice(odd * DH, (odd + 1) * DH), odd * NB_CMP
                self.tr_free[0] = self.kct_at = self.a(
                    self.kct2[r_, :, c_:c_ + n],
                    self.tr[0][r_, 0:GROUPS * NB_CMP].rearrange("p (g n) -> p g n", g=GROUPS)[:, :, 0:n],
                    ACT.Copy, p, set_at, scale=self.gains[r_, G_KN:G_KN + 1])

        nothing = lambda: None
        at = {}
        self.tasks += todo + [lambda kv=kv, q=q: hidden(kv, q) for kv in range(2) for q in range(4)] + [
            nothing, gelu, nothing, nothing, outputs, nothing, spread, nothing, turn_keys]

    def nsa_chunks(self):
        w = self.t["attn_w_q_2"][0]
        return ([(self.mat_src(w, 0), CW), (self.mat_src(w, CW), CW)]
                + [(self.mat_src(self.t["attn_w_o_2"][0], c * CW), CW) for c in range(D // CW)])

    def nsa(self):
        H = NSA_HEADS
        assert T // 64 <= 16 and T <= 512
        kt = self.area(self.KV_T, 2, GROUPS, T)
        vv = self.area(self.KV_V, 2, NT, GROUPS * DH)
        vcb = self.area(self.KV_CV, 2, CW)
        cb = self.area(self.KV_CB, NT, H, NB_CMP)
        tb = self.area(4672, H, T)
        qt = self.area(8768, KT, T)
        tmp = self.area(10816, NT, D)
        s_buf = self.area(12864, 2, 2, T)
        gates = self.area(13888, NT, H, 3)
        nm, den = self.area(13984, NT, 2, H), self.area(14048, NT, 2, H)
        coef = self.area(14112, NT, 2, H)
        cpt = self.area(14176, P)
        pt = self.xg
        pe, act, dve = self.pe, self.act, self.dve
        self.to_xt(self.x_tile, gain=G_MIX + 8, normed=True)
        g_at = self.ts(self.gains[:, G_NSAQ:G_NSAQ + 1], self.gains[:, G_NSAQ:G_NSAQ + 1], DH ** -0.5, None,
                       ALU.mult, None)
        act.wait(g_at)
        later, q_pts, turned_q = [], [[], []], {}

        def q_chunk(i, b=None):
            def read(t, p):
                while later:
                    later.pop(0)()
                n = self.normed_heads(t, p, tmp[:, t, i * CW:(i + 1) * CW], b=b)

                def turn_q():
                    q_pts[i].append(self.turn_heads(
                        t, lambda j: tmp[:, t, i * CW + j * P:i * CW + (j + 1) * P],
                        qt[:, 4 * i:4 * i + 4, t * P:(t + 1) * P], G_NSAQ, n))
                    turned_q[t, i] = self.turned_at
                later.append(turn_q)
            self.chunk(read, b=b)

        gt = self.silu[:].rearrange("p a b -> p (a b)")[0:3 * H, 0:T]

        self.narrow_load(self.t["attn_w_q_2"][0][:, D:D + 3 * H], 3 * H)
        q_chunk(0)
        p = self.narrow_product(3 * H)
        while later:
            later.pop(0)()
        p = self.bank_free[0] = self.a(gt, self.bank[0][0:3 * H, 0:T], ACT.Sigmoid, p)
        pe.wait(p, self.tr_free[1])
        for tile in range(NT):
            ins = pe.eng.transpose(self.tr[1][:, tile * 3 * H:(tile + 1) * 3 * H],
                                   gt[:, tile * P:(tile + 1) * P], self.ident[0:3 * H, 0:3 * H])
        p = pe.mark(ins)
        self.tr_free[1] = self.gates_at = self.a(
            gates.rearrange("p t h b -> p (t h b)"), self.tr[1][:, 0:NT * 3 * H], ACT.Copy, p)

        o_at, cmp_at = {}, {}
        inner = self.h[:].rearrange("p a b -> p (a b)").rearrange("p (n c) -> p n c", n=2)
        self.cmp_pv = None

        def cmp_views(t):
            return (inner[:, t, 0:8 * NB_CMP].rearrange("p (h n) -> p h n", h=8),
                    inner[:, t, P:P + 8], inner[:, t, P + 8:P + 16])

        def cmp_scores(t, half):
            sc = cmp_views(t)[0]
            pe.wait(self.acc_free[0], *q_pts[half], self.kct_at)
            for i in range(4):
                h = 8 * half + 2 * i
                p = self.mm(self.acc[0][:, 2 * i * NB_CMP:(2 * i + 2) * NB_CMP], qt[:, h // 2, t * P:(t + 1) * P],
                            self.kct2[:, h * GROUPS // H])
            self.acc_free[0] = cmp_at[t] = self.tt(
                sc, self.acc[0][:, 0:8 * NB_CMP].rearrange("p (i n) -> p i n", i=8), cb[:, t, 8 * half:8 * half + 8],
                ALU.add, p, self.cmp_free)

        def cmp_softmax(t, half):
            sc, mx, _ = cmp_views(t)
            q = self.red(mx, sc, ALU.max, cmp_at[t])
            q = self.tt(sc, sc, mx.unsqueeze(2).to_broadcast([P, 8, NB_CMP]), ALU.subtract, q)
            cmp_at[t] = self.a(sc, sc, ACT.Exp, q)

        def cmp_gates(t, half):
            sc, _, sm = cmp_views(t)
            q = self.red(sm, sc, ALU.add, cmp_at[t])
            dve.wait(q)
            q = dve.mark(dve.eng.reciprocal(sm, sm))
            q = self.stt(sm, sm, self.rowmask[:, t:t + 1], gates[:, t, 8 * half:8 * half + 8, 0],
                         ALU.mult, ALU.mult, q, self.gates_at)
            cmp_at[t] = self.tt(sc, sc, sm.unsqueeze(2).to_broadcast([P, 8, NB_CMP]), ALU.mult, q)

        def cmp_turn(t, half):
            pe.wait(cmp_at[t], self.tr_free[0])
            self.cmp_free = p = pe.mark(pe.eng.transpose(self.tr[0][:, 0:P], inner[:, t, 0:P], self.ident[:]))
            cmp_at[t] = self.tr_free[0] = self.a(cpt, self.tr[0][:, 0:P], ACT.Copy, p, self.cmp_pv)

        def cmp_values(t, half):
            pe.wait(self.vcb_at, self.acc_free[0])
            self.cmp_pv = p = self.mm(self.acc[0][:], cpt, vcb[:, half], cmp_at[t])
            self.acc_free[0] = o_at[t, half] = self.a(
                tmp[:, t, half * CW:(half + 1) * CW], self.acc[0][:], ACT.Copy, p, turned_q[t, half])

        steps = [(h, t) for h4 in range(2) for t in range(NT) for h in range(4 * h4, 4 * h4 + 4)]
        steps += [(h, t) for t in range(NT) for h in range(8, H)]
        st = {}
        ob = self.silu[:].rearrange("p a b -> p (a b)")

        early = len(steps) // 2
        third = self.sq_junk[:].rearrange("p (b n) -> p b n", b=2)

        def buffers(i):
            j, before = (i % 2, i - 2) if i < early else ((i - early) % 3, i - 3 + (i < early + 2))
            s = third if j == 2 else s_buf[:, j]
            bank, free, at = ((self.bank[1], self.bank_free, 1), (self.tr[1], self.tr_free, 1),
                              (self.bank[0], self.bank_free, 0))[j]
            return s, bank, free, at, (None if i == early + 2 else before)

        def scores(i):
            h, t = steps[i]
            rows, n, g = slice(DH * (h % 2), DH * (h % 2) + DH), (t + 1) * P, h * GROUPS // H
            s, bank, free, at, before = buffers(i)
            s = s[:, :, 0:n]
            pe.wait(free[at], *q_pts[h // 8], *self.k_pts)
            for br in range(2):
                p = self.mm(bank[:, br * n:(br + 1) * n], qt[rows, h // 2, t * P:(t + 1) * P],
                            kt[rows, br, g, 0:n])
            bias = tb[:, h, T - n:T].unsqueeze(1).to_broadcast([P, 2, n])
            p = free[at] = self.tt(
                s, bank[:, 0:2 * n].rearrange("p (b n) -> p b n", b=2), bias, ALU.add,
                p, self.tb_at, st.get(("turned", before)), self.sq_free)
            p = self.red(nm[:, t, :, h], s, ALU.max, p, negate=True)
            for br in range(2):
                q = self.a(s[:, br], s[:, br], ACT.Exp, p, bias=nm[:, t, br, h:h + 1],
                           accum_out=den[:, t, br, h:h + 1])
            st["exp", i] = q

        def turn(i):
            t = steps[i][1]
            n = (t + 1) * P
            s = buffers(i)[0]
            tr, free, at = (self.acc[1], self.acc_free, 1) if i >= early and i % 2 else (self.tr[0], self.tr_free, 0)
            pe.wait(st["exp", i], free[at])
            for br in range(2):
                for b in range(t + 1):
                    ins = pe.eng.transpose(tr[:, br * n + b * P:br * n + (b + 1) * P],
                                           s[:, br, b * P:(b + 1) * P], self.ident[:])
            p = st["turned", i] = pe.mark(ins)
            st["pt", i] = free[at] = self.a(pt[:, i % 2, 0:2 * n], tr[:, 0:2 * n], ACT.Copy, p,
                                            st.get(("pv", i - 2)), *self.xg_free)

        def values(i):
            h, t = steps[i]
            n, g, q4 = (t + 1) * P, h * GROUPS // H, i // 4
            a = q4 % 2 + 2
            pe.wait(st["pt", i], self.acc_free[a], *self.v_pts)
            for br in range(2):
                for b in range(t + 1):
                    c = (br * 4 + h % 4) * DH
                    p = self.mm(self.acc[a][:, c:c + DH], pt[:, i % 2, br * n + b * P:br * n + (b + 1) * P],
                                vv[:, br, b, g * DH:(g + 1) * DH], start=(b == 0), stop=(b == t))
            st["pv", i] = p
            if i % 4 == 3:
                hs = slice(h - 3, h + 1)
                dve.wait(st["exp", i])
                q = dve.mark(dve.eng.reciprocal(den[:, t, :, hs], den[:, t, :, hs]))
                gg = gates[:, t, hs, 1:3].rearrange("p h b -> p b h")
                q = self.tt(coef[:, t, :, hs], den[:, t, :, hs], gg, ALU.mult, q)
                o4 = ob.rearrange("p (b h d) -> p b h d", b=2, h=4)
                q = self.tt(o4, self.acc[a][:].rearrange("p (b h d) -> p b h d", b=2, h=4),
                            coef[:, t, :, hs].unsqueeze(3).to_broadcast([P, 2, 4, DH]), ALU.mult, q, p)
                self.acc_free[a] = q
                cols = tmp[:, t, (h - 3) * DH:(h + 1) * DH]
                q = self.tt(cols, cols, ob[:, 0:FC], ALU.add, q, o_at[t, (h - 3) // 8])
                st["o", t, (h - 3) // 8] = self.tt(cols, cols, ob[:, FC:], ALU.add, q)

        done = {"turned": 0, "values": 0}

        def step(i):
            if i < len(steps):
                scores(i)
            lag = 1 if i <= early else 2
            while done["turned"] <= min(i - lag, len(steps) - 1):
                turn(done["turned"])
                done["turned"] += 1
                if done["turned"] > 1 and done["values"] < done["turned"] - 1:
                    values(done["values"])
                    done["values"] += 1

        def mixed(half):
            a, s_, g_, u, v_ = cmp_scores, cmp_softmax, cmp_gates, cmp_turn, cmp_values
            parts = [[(a, 0), (a, 1)], [(s_, 0), (s_, 1)], [(g_, 0), (g_, 1)], [(u, 0)], [(v_, 0), (u, 1)], [(v_, 1)]]
            first = half * len(steps) // 2
            for i in range(first, first + len(steps) // 2 + 2 * half):
                now = parts.pop(0) if parts else []
                if len(parts) > 2:
                    yield lambda i=i, now=now: [f(t, half) for f, t in now] + [step(i)]
                else:
                    yield lambda i=i, now=now: [step(i) if f is None else f(t, half)
                                                for f, t in now[:1] + [(None, 0)] + now[1:]]

        todo = list(mixed(0))

        def fill():
            if todo:
                todo.pop(0)()

        self.fill = fill
        q_chunk(1, b=0)
        self.fill = None
        for task in todo + later + list(mixed(1)):
            task()
        values(len(steps) - 1)
        self.sq_free = st["turned", len(steps) - 1]
        self.xg_free = [p_ for p_ in (st["pv", len(steps) - 2], st["pv", len(steps) - 1])]
        self.to_xt(lambda t, k: tmp[:, t, k * P:(k + 1) * P], ready=[(st["o", t, 0], st["o", t, 1]) for t in range(NT)])
        self.out_projection()

    def begin(self, stages):
        t, act, pe, dve = self.t, self.act, self.pe, self.dve
        self.xg_free = [None, None]
        self.h_at_prev = [None, None]
        self.diag_free, self.sq_at = [None, None], [None, None]
        self.warm_at = self.sq_junk_at = None
        self.src_read = self.sq_free = self.cmp_free = None
        self.rms_free = [None, None]
        rows = self.arena[:, 0:2 * P].rearrange("p (a n) -> p a n", a=2)
        self.first_in.mark(act.eng.dma_start(self.ident[:], t["c_ident"]))
        first = self.first_in.mark(act.eng.dma_start(
            rows[0:48, 0, :], t["norm_g"].rearrange("a b (k n) -> (a b k) n", n=P)))
        for tile in range(NT):
            self.x_ready[tile] = self.x_in[tile].mark(act.eng.dma_start(
                self.x[:, tile], t["x"][0, tile * P:(tile + 1) * P, :]))
        self.x_half = [[p, p] for p in self.x_ready]
        pe.wait(first)
        p = pe.mark(pe.eng.transpose(self.tr[0][:, 0:48], rows[0:48, 0, :], self.ident[0:48, 0:48]))
        self.tr_free[0] = self.a(self.gains[:, 0:48], self.tr[0][:, 0:48], ACT.Copy, p)
        dve.wait(self.tr_free[0])
        act.wait(first)
        dve.wait(first)

        self.par = 1
        self.pop_next(0)
        self.w_ready[0][0] = self.split_lo[0]
        self.fill = lambda: None
        self.pop_next(1)
        self.par, self.fill = 0, None

        def load(dst, src):
            return self.consts_in.mark(self.pool.eng.dma_start(dst, src))

        flat = lambda a: a.rearrange("a (k n) -> (a k) n", n=P)
        rest = self.arena[:, 2 * P:4 * P].rearrange("p (a n) -> p a n", a=2)
        load(rest[48:64, 0, :], flat(t["ffn1_norm_2"]))
        load(rest[64:80, 0, :], flat(t["mix_norm_2"]))
        load(rest[80:96, 0, :], flat(t["ffn2_norm_2"]))
        load(rest[96:104, 0, :], t["kv_norm_2"].rearrange("(k n) -> k n", n=P))
        load(rest[104:128, 0, :], t["conv_w_2"].rearrange("a b (k n) -> (a b k) n", n=P))
        load(rest[0:48, 0, :], t["norm_g"].rearrange("a b (k n) -> (a b k) n", n=P))
        load(rest[0:8, 1, :], flat(t["hg_lb_logits"]))
        for half in range(2):
            c = slice(half * DH, (half + 1) * DH)
            load(rest[8:9, 1, c], t["fox_q_norm_g"])
            load(rest[9:10, 1, c], t["fox_k_norm_g"])
            load(rest[10:11, 1, c], t["attn_q_norm_2"])
            load(rest[11:14, 1, c], t["k_norm_2"])
        load(rest[14:46, 1, 0:DH], t["cmp_pe_k_2"])
        load(rest[14:46, 1, DH:P], t["cmp_pe_v_2"])
        load(self.masks[:], t["c_masks"])
        load(self.rowmask[:], t["c_rowmask"])
        og = t["hg_out_norm_g"]
        last = load(self.og, bass.AP(tensor=og.tensor, offset=og.offset, ap=[[0, P], [1, P]]))
        def other_gains():
            pe.wait(last, self.tr_free[0])
            pe.eng.transpose(self.tr[0][:, 0:P], rest[:, 0, :], self.ident[:])
            p = pe.mark(pe.eng.transpose(self.tr[0][:, P:G_ROWS], rest[0:G_ROWS - P, 1, :],
                                         self.ident[0:G_ROWS - P, 0:G_ROWS - P]))
            gains_at = self.tr_free[0] = self.a(self.gains[:, 48:], self.tr[0][:, 48:G_ROWS], ACT.Copy, p)
            dve.wait(gains_at, last)
            logit = self.gains[:, G_LB:G_LB + KT]
            e, r, lb, om = self.small[:, 0, 0, 0:KT], self.small[:, 0, 1, 0:KT], self.lbs[:, 0], self.lbs[:, 1]
            p = self.tt(e, logit, logit, ALU.subtract)
            p = self.a(e, e, ACT.Exp, p)
            dve.wait(p)
            p = dve.mark(dve.eng.reciprocal(r, e))
            p = self.tt(e, e, r, ALU.mult, p)
            p = self.tt(lb, e, e, ALU.subtract, p)
            self.lb_at = self.ts(om, lb, -1.0, 1.0, ALU.mult, ALU.add, p)

        self.tasks = [lambda: None] * 15 + [other_gains]

    def end(self):
        sp = self.sp
        out = self.t["out"].rearrange("o (t p) d -> p (o t) d", p=P)
        for t in range(NT):
            for half in range(2):
                cols = slice(half * CW, (half + 1) * CW)
                sp.wait(self.x_half[t][half])
                done = self.stored.mark(sp.eng.dma_start(out[:, t, cols], self.x[:, t, cols]))
        sp.wait(done)
        sp.flush()

    def chunks_of(self, stage):
        t = self.t
        kind = stage[0]
        if kind == "ffn":
            return [(self.ffn_src(stage[1], 0), CW)]
        return self.MIXER_CHUNKS[kind](self)

    MIXER_CHUNKS = {"conv": conv_chunks, "hgrn": hgrn_chunks, "fox": fox_chunks, "kv": kv_chunks,
                    "nsa": nsa_chunks}
    PREPARE = {"fox": fox_prepare, "kv": kv_prepare}
    MIXERS = {"conv": conv, "hgrn": hgrn, "fox": fox, "kv": kv, "nsa": nsa}

    def run(self, stages):
        self.queue = [c for s in stages for c in self.chunks_of(s)]
        self.begin(stages)
        if stages[0][0] != "ffn" or stages[0][3] >= 48:
            self.finish_tasks()
        for s, following in zip(stages, stages[1:] + [None]):
            if s[0] == "ffn":
                self.ffn(*s[1:], prepare=self.PREPARE.get(following[0]) if following else None)
            else:
                self.MIXERS[s[0]](self)
        assert not self.queue, len(self.queue)
        self.end()


def rel_tables():
    n = np.arange(T)
    nf = np.maximum(n, 1).astype(np.float32)
    large = MAX_EXACT + (np.log(nf / np.float32(MAX_EXACT)) / np.float32(np.log(MAX_DISTANCE / MAX_EXACT))
                         * np.float32(N_BUCKETS - MAX_EXACT)).astype(np.int32)
    bucket = np.where(n < MAX_EXACT, n, np.minimum(large, N_BUCKETS - 1))
    tables = np.zeros((2, REL_ROWS, REL_W), np.float32)
    for which, rel in enumerate((np.arange(REL_W) - T, T - 1 - np.arange(REL_W))):
        row = np.where(rel < 0, N_BUCKETS, bucket[np.clip(rel, 0, T - 1)])
        tables[which, row, np.arange(REL_W)] = 1.0
    return tables


def constants():
    i = np.arange(P)
    s, t = i[:, None], i[None, :]
    masks = [s == t]
    m = 1
    while m < P // 2:
        masks.append((s // (2 * m) == t // (2 * m)) & (s % (2 * m) < m) & (t % (2 * m) >= m))
        m *= 2
    causal = np.zeros((P, 2, P), np.float32)
    causal[:, 1] = np.where(t > s, NEG, 0.0)
    select = np.zeros((P, FOX_HEADS, P), np.float32)
    select[np.arange(FOX_HEADS), np.arange(FOX_HEADS)] = 1.0
    rowmask = np.ones((P, NT + 8), np.float32)
    rowmask[:CMP_BLOCK - 1, 0] = 0.0
    rowmask[:, NT:] = i[:, None] // NB_CMP == np.arange(8)
    return {
        "c_ident": np.eye(P, dtype=np.float32),
        "c_masks": np.stack(masks, 1).astype(np.int32),
        "c_causal": causal,
        "c_select": select,
        "c_rel": rel_tables(),
        "c_rowmask": rowmask,
    }


def build(nc, t, stages=None):
    with ExitStack() as stack:
        k = Kernel(nc, stack, t)
        if stages is None:
            stages = all_stages(t)
        k.run(stages)


def all_stages(t):
    f_in, f_out = t["ffn_w_in"], t["ffn_w_out"]
    i1, o1, i2, o2 = t["ffn1_w_in_2"], t["ffn1_w_out_2"], t["ffn2_w_in_2"], t["ffn2_w_out_2"]
    return [
        ("ffn", f_in[0, 0], f_out[0, 0], G_NORM),
        ("hgrn",),
        ("ffn", f_in[0, 1], f_out[0, 1], G_NORM + 16),
        ("ffn", f_in[1, 0], f_out[1, 0], G_NORM + 24),
        ("fox",),
        ("ffn", f_in[1, 1], f_out[1, 1], G_NORM + 40),
        ("ffn", i1[0], o1[0], G_FFN1),
        ("conv",),
        ("ffn", i2[0], o2[0], G_FFN2),
        ("kv",),
        ("ffn", i1[1], o1[1], G_FFN1 + 8),
        ("nsa",),
        ("ffn", i2[1], o2[1], G_FFN2 + 8),
    ]


NAMES = [
    "x", "norm_g", "ffn_w_in", "ffn_w_out", "hg_w_in", "hg_lb_logits", "hg_out_norm_g", "hg_w_out",
    "fox_w_in", "fox_b_f", "fox_q_norm_g", "fox_k_norm_g", "fox_w_out", "ffn1_norm_2", "ffn1_w_in_2",
    "ffn1_w_out_2", "mix_norm_2", "ffn2_norm_2", "ffn2_w_in_2", "ffn2_w_out_2", "conv_w_in_2",
    "conv_w_2", "conv_w_out_2", "attn_w_q_2", "attn_q_norm_2", "attn_w_o_2", "kv_norm_2", "w_kv_2",
    "k_norm_2", "cmp_pe_k_2", "cmp_pe_v_2", "cmp_w1_k_2", "cmp_w2_k_2", "cmp_w1_v_2", "cmp_w2_v_2",
    "rel_bias_2",
]


def kernel(**inputs):
    import concourse.bacc as bacc
    from concourse.bass_utils import run_bass_kernel_spmd

    nc = bacc.Bacc("TRN2", target_bir_lowering=False, num_devices=1)
    arrays = {name: np.ascontiguousarray(inputs[name]) for name in NAMES}
    arrays.update(constants())
    t = {name: nc.dram_tensor(name, a.shape, mybir.dt.from_np(a.dtype), kind="ExternalInput").ap()
         for name, a in arrays.items()}
    t["out"] = nc.dram_tensor("out", (1, T, D), F32, kind="ExternalOutput").ap()
    build(nc, t)
    r = run_bass_kernel_spmd(nc, [arrays], core_ids=[0])
    return r.results[0]["out"]
```
